# Optimizing a Trainium2 kernel written in Bass

```python
import jax
import jax.numpy as jnp
from jax import lax
import numpy as np
import math

D_MODEL = 1024
BATCH = 1
SEQ = 512
DEPTH = 2

GRID_W = 64
CTX_LEN = 256
N_EVEN = (DEPTH + 1) // 2
N_ODD = DEPTH // 2

HEAD_DIM = 64
ATTN_HEADS = (D_MODEL // 2) // HEAD_DIM
ATTN_KV_HEADS = ATTN_HEADS // 4
ATTN_GROUP = ATTN_HEADS // ATTN_KV_HEADS
WINDOW = 128
ATTN_BLOCK = 128
ROPE_BASE = 10000.0

HGRN_EXPAND = 128
HGRN_WIDTH = D_MODEL // 2
HGRN_HEADS = HGRN_WIDTH // HGRN_EXPAND
HGRN_DK = HGRN_EXPAND
HGRN_DV = HGRN_EXPAND
CHUNK = 64

RET_HEADS = 4
RET_DK = D_MODEL // RET_HEADS
RET_DV = 2 * RET_DK
RET_BASE = 10000.0

FFN_HIDDEN = -(-8 * D_MODEL // (3 * 256)) * 256

A_Q = ATTN_HEADS * HEAD_DIM
A_KV = ATTN_KV_HEADS * HEAD_DIM
EVEN_PARTS = (('a_q', A_Q), ('a_k', A_KV), ('a_v', A_KV), ('b_q', HGRN_WIDTH), ('b_ff', HGRN_WIDTH),
              ('b_fb', HGRN_WIDTH), ('b_i', HGRN_WIDTH), ('b_g', HGRN_WIDTH))
EVEN_IN = A_Q + 2 * A_KV + 5 * HGRN_WIDTH
EVEN_OUT = A_Q + HGRN_HEADS * HGRN_DV
ODD_PARTS = (('q', RET_HEADS * RET_DK), ('k', RET_HEADS * RET_DK), ('v', RET_HEADS * RET_DV),
             ('g', RET_HEADS * RET_DV))
ODD_IN = 2 * RET_HEADS * RET_DK + 2 * RET_HEADS * RET_DV
ODD_OUT = RET_HEADS * RET_DV
EPS = 1e-6
F32 = jnp.float32


def _offsets(parts):
    out, start = {}, 0
    for name, width in parts:
        out[name] = (start, start + width)
        start += width
    return out

def split_parts(u, parts):
    return {n: u[..., s:e] for n, (s, e) in _offsets(parts).items()}

def project_parts(h, w, parts, names):
    off = _offsets(parts)
    return {n: h @ w[:, off[n][0]:off[n][1]] for n in names}

def rms_norm(x, g=None):
    xf = x.astype(F32)
    y = xf * lax.rsqrt(jnp.mean(xf * xf, axis=-1, keepdims=True) + EPS)
    if g is not None:
        y = y * g.astype(F32)
    return y.astype(x.dtype)

def modulate(h, shift, scale):
    return h * (1.0 + scale) + shift

def to_heads(u, n_heads):
    b, l, _ = u.shape
    return u.reshape(b, l, n_heads, -1).transpose(0, 2, 1, 3)

def from_heads(o):
    return o.transpose(0, 2, 1, 3)

def flip(a):
    return jnp.flip(a, axis=2)

def axial_rope_tables(n_tok):
    t = jnp.arange(n_tok)
    row = (t // GRID_W).astype(F32)
    col = (t % GRID_W).astype(F32)
    n_freq = HEAD_DIM // 4
    inv = ROPE_BASE ** (-jnp.arange(n_freq, dtype=F32) / n_freq)
    ang = jnp.concatenate([row[:, None] * inv, col[:, None] * inv], axis=-1)
    return jnp.cos(ang), jnp.sin(ang)

def retention_rope_tables(n_tok):
    theta = 1.0 / (RET_BASE ** jnp.linspace(0.0, 1.0, RET_DK // 2, dtype=F32))
    ang = jnp.arange(n_tok, dtype=F32)[:, None] * theta
    return jnp.cos(ang), jnp.sin(ang)

def apply_rope(x, cos, sin):
    half = x.shape[-1] // 2
    xf = x.astype(F32)
    x1, x2 = xf[..., :half], xf[..., half:]
    return jnp.concatenate([x1 * cos - x2 * sin, x2 * cos + x1 * sin], axis=-1).astype(x.dtype)

def attn_q_heads(u, g):
    b, l, _ = u.shape
    q = rms_norm(u.reshape(b, l, ATTN_KV_HEADS, ATTN_GROUP, HEAD_DIM), g)
    return q.transpose(0, 2, 3, 1, 4)

def kv_heads(u, g=None):
    b, l, _ = u.shape
    h = u.reshape(b, l, ATTN_KV_HEADS, HEAD_DIM)
    if g is not None:
        h = rms_norm(h, g)
    return h.transpose(0, 2, 1, 3)

def window_attention(q, k, v, k_ctx, v_ctx, sink):
    b, kv, g, l, d = q.shape
    n_blocks = l // ATTN_BLOCK
    span = ATTN_BLOCK + 2 * WINDOW
    pad = ((0, 0), (0, 0), (WINDOW, WINDOW), (0, 0))
    kp, vp = jnp.pad(k, pad), jnp.pad(v, pad)
    scale = d ** -0.5
    sink_col = jnp.broadcast_to(sink[None, :, :, None, None], (b, kv, g, ATTN_BLOCK, 1))

    def block(i):
        start = i * ATTN_BLOCK
        qb = lax.dynamic_slice_in_dim(q, start, ATTN_BLOCK, axis=3)
        kb = lax.dynamic_slice_in_dim(kp, start, span, axis=2)
        vb = lax.dynamic_slice_in_dim(vp, start, span, axis=2)
        q_pos = start + jnp.arange(ATTN_BLOCK)
        k_pos = start - WINDOW + jnp.arange(span)
        valid = ((jnp.abs(k_pos[None, :] - q_pos[:, None]) <= WINDOW)
                 & (k_pos >= 0)[None, :] & (k_pos < l)[None, :])
        s_lat = jnp.einsum('bkgqd,bksd->bkgqs', qb, kb, preferred_element_type=F32) * scale
        s_lat = jnp.where(valid, s_lat, -jnp.inf)
        s_ctx = jnp.einsum('bkgqd,bkcd->bkgqc', qb, k_ctx, preferred_element_type=F32) * scale
        p = jax.nn.softmax(jnp.concatenate([sink_col, s_lat, s_ctx], axis=-1), axis=-1)
        p_lat = p[..., 1:1 + span].astype(v.dtype)
        p_ctx = p[..., 1 + span:].astype(v.dtype)
        return (jnp.einsum('bkgqs,bksd->bkgqd', p_lat, vb)
                + jnp.einsum('bkgqc,bkcd->bkgqd', p_ctx, v_ctx))

    o = lax.map(block, jnp.arange(n_blocks))
    return o.transpose(1, 0, 4, 2, 3, 5).reshape(b, l, kv * g * d)

def context_attention(q, k, v, sink):
    b, kv, g, lc, d = q.shape
    s = jnp.einsum('bkgqd,bkcd->bkgqc', q, k, preferred_element_type=F32) * d ** -0.5
    sink_col = jnp.broadcast_to(sink[None, :, :, None, None], (b, kv, g, lc, 1))
    p = jax.nn.softmax(jnp.concatenate([sink_col, s], axis=-1), axis=-1)[..., 1:].astype(v.dtype)
    o = jnp.einsum('bkgqc,bkcd->bkgqd', p, v)
    return o.transpose(0, 3, 1, 2, 4).reshape(b, lc, kv * g * d)

def chunk_scan(q_in, k_in, v, decay, s0):
    xs = (jnp.moveaxis(q_in, 2, 0), jnp.moveaxis(k_in, 2, 0), jnp.moveaxis(v, 2, 0), decay)

    def step(s, inp):
        q_n, k_n, v_n, a_n = inp
        o_n = jnp.einsum('bhcd,bhde->bhce', q_n, s)
        s = a_n * s + jnp.einsum('bhcd,bhce->bhde', k_n, v_n)
        return s, o_n

    s, o = lax.scan(step, s0, xs)
    return jnp.moveaxis(o, 0, 2), s

def gla_chunked(q, k, v, log_f, s0):
    b, h, l, dk = q.shape
    dv = v.shape[-1]
    n = l // CHUNK
    qc, kc, lc = (a.reshape(b, h, n, CHUNK, dk) for a in (q, k, log_f))
    vc = v.reshape(b, h, n, CHUNK, dv)
    cum = jnp.cumsum(lc, axis=3)
    ref = cum[:, :, :, CHUNK // 2:CHUNK // 2 + 1]
    scores = jnp.einsum('bhntd,bhnsd->bhnts', qc * jnp.exp(cum - ref), kc * jnp.exp(ref - cum))
    lower = jnp.tril(jnp.ones((CHUNK, CHUNK), dtype=bool))
    o_intra = jnp.einsum('bhnts,bhnse->bhnte', jnp.where(lower, scores, 0.0), vc)
    cum_last = cum[:, :, :, -1:]
    decay = jnp.moveaxis(jnp.exp(cum_last[:, :, :, 0]), 2, 0)[..., None]
    o_inter, s = chunk_scan(qc * jnp.exp(cum), kc * jnp.exp(cum_last - cum), vc, decay, s0)
    return (o_intra + o_inter).reshape(b, h, l, dv), s

def gla_final_state(k, v, log_f):
    cum = jnp.cumsum(log_f, axis=2)
    return jnp.einsum('bhld,bhle->bhde', k * jnp.exp(cum[:, :, -1:] - cum), v)

def retention_chunked(q, k, v, log_gamma, s0):
    b, h, l, dk = q.shape
    dv = v.shape[-1]
    n = l // CHUNK
    qc = q.reshape(b, h, n, CHUNK, dk)
    kc = k.reshape(b, h, n, CHUNK, dk)
    vc = v.reshape(b, h, n, CHUNK, dv)
    pos = jnp.arange(CHUNK, dtype=F32)
    rel = pos[:, None] - pos[None, :]
    dmat = jnp.where(rel >= 0, jnp.exp(log_gamma[:, None, None] * jnp.maximum(rel, 0.0)), 0.0)
    scores = jnp.einsum('bhntd,bhnsd->bhnts', qc, kc) * dmat[None, :, None]
    o_intra = jnp.einsum('bhnts,bhnse->bhnte', scores, vc)
    lg = log_gamma[:, None]
    q_in = qc * jnp.exp(lg * (pos + 1.0))[None, :, None, :, None]
    k_in = kc * jnp.exp(lg * (CHUNK - 1.0 - pos))[None, :, None, :, None]
    decay = jnp.broadcast_to(jnp.exp(log_gamma * CHUNK)[None, None, :, None, None], (n, 1, h, 1, 1))
    o_inter, s = chunk_scan(q_in, k_in, vc, decay, s0)
    return (o_intra + o_inter).reshape(b, h, l, dv), s

def retention_final_state(k, v, log_gamma):
    lc = k.shape[2]
    w = jnp.exp(log_gamma[:, None] * (lc - 1.0 - jnp.arange(lc, dtype=F32)))
    return jnp.einsum('bhld,bhle->bhde', k * w[None, :, :, None], v)

def gated_head_norm(o, g_raw, gain=None):
    b, h, l, dv = o.shape
    y = rms_norm(from_heads(o), gain) * jax.nn.silu(g_raw.reshape(b, l, h, dv).astype(F32))
    return y.reshape(b, l, h * dv)

def even_mixer(h_ctx, h_lat, w_in, w_out, qk_g, sink, out_g, lb, cos, sin, need_ctx):
    dt = h_lat.dtype
    n_b = h_ctx.shape[0]
    sink = sink.astype(F32).reshape(ATTN_KV_HEADS, ATTN_GROUP)
    lb = lb.reshape(HGRN_HEADS, 1, HGRN_DK)
    p = split_parts(h_lat @ w_in, EVEN_PARTS)
    names = [n for n, _ in EVEN_PARTS] if need_ctx else ['a_k', 'a_v', 'b_ff', 'b_fb', 'b_i']
    pc = project_parts(h_ctx, w_in, EVEN_PARTS, names)

    def gates(f_raw):
        f = lb + (1.0 - lb) * jax.nn.sigmoid(to_heads(f_raw, HGRN_HEADS).astype(F32))
        return 1.0 - f, jnp.log(f)

    k_ctx = kv_heads(pc['a_k'], qk_g[1])
    v_ctx = kv_heads(pc['a_v'])
    q_lat = apply_rope(attn_q_heads(p['a_q'], qk_g[0]), cos, sin)
    k_lat = apply_rope(kv_heads(p['a_k'], qk_g[1]), cos, sin)
    a_lat = window_attention(q_lat, k_lat, kv_heads(p['a_v']), k_ctx, v_ctx, sink)

    k_fw_c, lf_fw_c = gates(pc['b_ff'])
    k_bw_c, lf_bw_c = gates(pc['b_fb'])
    i_c = to_heads(pc['b_i'], HGRN_HEADS).astype(F32)
    if need_ctx:
        zeros = jnp.zeros((n_b, HGRN_HEADS, HGRN_DK, HGRN_DV), F32)
        q_c = jax.nn.silu(to_heads(pc['b_q'], HGRN_HEADS).astype(F32))
        o_fw_c, s_fw = gla_chunked(q_c, k_fw_c, i_c, lf_fw_c, zeros)
        o_bw_c, s_bw = gla_chunked(flip(q_c), flip(k_bw_c), flip(i_c), flip(lf_bw_c), zeros)
    else:
        s_fw = gla_final_state(k_fw_c, i_c, lf_fw_c)
        s_bw = gla_final_state(flip(k_bw_c), flip(i_c), flip(lf_bw_c))
    k_fw, lf_fw = gates(p['b_ff'])
    k_bw, lf_bw = gates(p['b_fb'])
    q_l = jax.nn.silu(to_heads(p['b_q'], HGRN_HEADS).astype(F32))
    i_l = to_heads(p['b_i'], HGRN_HEADS).astype(F32)
    o_fw, _ = gla_chunked(q_l, k_fw, i_l, lf_fw, s_fw)
    o_bw, _ = gla_chunked(flip(q_l), flip(k_bw), flip(i_l), flip(lf_bw), s_bw)
    b_lat = gated_head_norm(o_fw + flip(o_bw), p['b_g'], out_g)

    y_lat = jnp.concatenate([a_lat.astype(dt), b_lat.astype(dt)], axis=-1) @ w_out
    if not need_ctx:
        return None, y_lat
    a_ctx = context_attention(attn_q_heads(pc['a_q'], qk_g[0]), k_ctx, v_ctx, sink)
    b_ctx = gated_head_norm(o_fw_c + flip(o_bw_c), pc['b_g'], out_g)
    y_ctx = jnp.concatenate([a_ctx.astype(dt), b_ctx.astype(dt)], axis=-1) @ w_out
    return y_ctx, y_lat

def odd_mixer(h_ctx, h_lat, w_in, w_out, cos, sin, need_ctx):
    dt = h_lat.dtype
    n_b = h_ctx.shape[0]
    log_g_fw = jnp.log(1.0 - 2.0 ** (-5.0 - jnp.arange(RET_HEADS, dtype=F32)))
    log_g_bw = log_g_fw[::-1]
    k_scale = RET_DK ** -0.5
    p = split_parts(h_lat @ w_in, ODD_PARTS)
    names = [n for n, _ in ODD_PARTS] if need_ctx else ['k', 'v']
    pc = project_parts(h_ctx, w_in, ODD_PARTS, names)

    k_c = to_heads(pc['k'], RET_HEADS).astype(F32) * k_scale
    v_c = to_heads(pc['v'], RET_HEADS).astype(F32)
    if need_ctx:
        zeros = jnp.zeros((n_b, RET_HEADS, RET_DK, RET_DV), F32)
        q_c = to_heads(pc['q'], RET_HEADS).astype(F32)
        o_fw_c, s_fw = retention_chunked(q_c, k_c, v_c, log_g_fw, zeros)
        o_bw_c, s_bw = retention_chunked(flip(q_c), flip(k_c), flip(v_c), log_g_bw, zeros)
    else:
        s_fw = retention_final_state(k_c, v_c, log_g_fw)
        s_bw = retention_final_state(flip(k_c), flip(v_c), log_g_bw)

    q_l = apply_rope(to_heads(p['q'], RET_HEADS).astype(F32), cos, sin)
    k_l = apply_rope(to_heads(p['k'], RET_HEADS).astype(F32), cos, sin) * k_scale
    v_l = to_heads(p['v'], RET_HEADS).astype(F32)
    o_fw, _ = retention_chunked(q_l, k_l, v_l, log_g_fw, s_fw)
    o_bw, _ = retention_chunked(flip(q_l), flip(k_l), flip(v_l), log_g_bw, s_bw)
    y_lat = gated_head_norm(o_fw + flip(o_bw), p['g']).astype(dt) @ w_out
    if not need_ctx:
        return None, y_lat
    y_ctx = gated_head_norm(o_fw_c + flip(o_bw_c), pc['g']).astype(dt) @ w_out
    return y_ctx, y_lat

def swiglu(h, w_in, w_out):
    gate, up = jnp.split(h @ w_in, 2, axis=-1)
    return (jax.nn.silu(gate) * up) @ w_out

def first_inputs(seed: int = 0) -> dict:
    key = jax.random.key(seed)
    ks = jax.random.split(key, 17)
    d = D_MODEL

    def nrm(k, shape, scale):
        return jax.random.normal(k, shape, F32) * scale

    return {
        'x': nrm(ks[0], (BATCH, SEQ, d), 1.0),
        'c': nrm(ks[1], (BATCH, d), 1.0),
        'ctx': nrm(ks[2], (BATCH, CTX_LEN, d), 1.0),
        'c_ctx': nrm(ks[3], (d,), 1.0),
        'mod_w': nrm(ks[4], (DEPTH, d, 6 * d), 0.5 * d ** -0.5),
        'mod_b': nrm(ks[5], (DEPTH, 6 * d), 0.02),
        'norm_g': 1.0 + nrm(ks[6], (DEPTH, 2, d), 0.02),
        'ffn_w_in': nrm(ks[7], (DEPTH, d, 2 * FFN_HIDDEN), d ** -0.5),
        'ffn_w_out': nrm(ks[8], (DEPTH, FFN_HIDDEN, d), FFN_HIDDEN ** -0.5),
        'even_w_in': nrm(ks[9], (N_EVEN, d, EVEN_IN), d ** -0.5),
        'even_w_out': nrm(ks[10], (N_EVEN, EVEN_OUT, d), EVEN_OUT ** -0.5),
        'attn_qk_norm_g': 1.0 + nrm(ks[11], (N_EVEN, 2, HEAD_DIM), 0.02),
        'attn_sink': nrm(ks[12], (N_EVEN, ATTN_HEADS), 0.5),
        'hgrn_out_norm_g': 1.0 + nrm(ks[13], (N_EVEN, HGRN_DV), 0.02),
        'hgrn_lb': nrm(ks[14], (N_EVEN + 1, HGRN_WIDTH), 0.1),
        'odd_w_in': nrm(ks[15], (N_ODD, d, ODD_IN), d ** -0.5),
        'odd_w_out': nrm(ks[16], (N_ODD, ODD_OUT, d), ODD_OUT ** -0.5),
    }

def first_block(x, c, ctx, c_ctx, mod_w, mod_b, norm_g, ffn_w_in, ffn_w_out, even_w_in, even_w_out,
              attn_qk_norm_g, attn_sink, hgrn_out_norm_g, hgrn_lb, odd_w_in, odd_w_out):
    n_tok = x.shape[1]
    rope_cos, rope_sin = axial_rope_tables(n_tok)
    ret_cos, ret_sin = retention_rope_tables(n_tok)
    lower_bounds = jnp.cumsum(jax.nn.softmax(hgrn_lb.astype(F32), axis=0), axis=0)
    cond_lat = jax.nn.silu(c)
    cond_ctx = jax.nn.silu(c_ctx)
    for layer in range(DEPTH):
        last = layer == DEPTH - 1
        j = layer // 2
        m_lat = jnp.split((cond_lat @ mod_w[layer] + mod_b[layer])[:, None, :], 6, axis=-1)
        m_ctx = jnp.split((cond_ctx @ mod_w[layer] + mod_b[layer])[None, None, :], 6, axis=-1)
        h_lat = modulate(rms_norm(x, norm_g[layer, 0]), m_lat[0], m_lat[1])
        h_ctx = modulate(rms_norm(ctx, norm_g[layer, 0]), m_ctx[0], m_ctx[1])
        if layer % 2 == 0:
            y_ctx, y_lat = even_mixer(h_ctx, h_lat, even_w_in[j], even_w_out[j], attn_qk_norm_g[j],
                                      attn_sink[j], hgrn_out_norm_g[j], lower_bounds[j],
                                      rope_cos, rope_sin, not last)
        else:
            y_ctx, y_lat = odd_mixer(h_ctx, h_lat, odd_w_in[j], odd_w_out[j], ret_cos, ret_sin, not last)
        x = x + m_lat[2] * y_lat
        x = x + m_lat[5] * swiglu(modulate(rms_norm(x, norm_g[layer, 1]), m_lat[3], m_lat[4]),
                                  ffn_w_in[layer], ffn_w_out[layer])
        if not last:
            ctx = ctx + m_ctx[2] * y_ctx
            ctx = ctx + m_ctx[5] * swiglu(modulate(rms_norm(ctx, norm_g[layer, 1]), m_ctx[3], m_ctx[4]),
                                          ffn_w_in[layer], ffn_w_out[layer])
    return x


DIFF_W = (D_MODEL * 3 // 8)
DELTA_W = (D_MODEL * 3 // 8)
CONV_CH = D_MODEL - DIFF_W - DELTA_W
DIFF_HEADS = DIFF_W // HEAD_DIM
DIFF_DIM = HEAD_DIM // 2
DELTA_HEADS = DELTA_W // HEAD_DIM
CONV_WIDTH = 31
SHORT_CONV = 3
Q_BLOCK = 128
D_FF = 4 * D_MODEL
IN_W = 2 * CONV_CH + 3 * DIFF_W + 4 * DELTA_W + 4 * DELTA_HEADS
NORM_EPS = 1e-6


def rms_norm_2(x, w, eps=NORM_EPS):
    xf = x.astype(jnp.float32)
    y = xf * lax.rsqrt(jnp.mean(xf * xf, axis=-1, keepdims=True) + eps)
    return (y * w.astype(jnp.float32)).astype(x.dtype)

def layer_norm(x, w, b, eps=1e-5):
    xf = x.astype(jnp.float32)
    mu = jnp.mean(xf, axis=-1, keepdims=True)
    xc = xf - mu
    var = jnp.mean(xc * xc, axis=-1, keepdims=True)
    y = xc * lax.rsqrt(var + eps) * w.astype(jnp.float32) + b.astype(jnp.float32)
    return y.astype(x.dtype)

def l2norm(x, eps=1e-6):
    xf = x.astype(jnp.float32)
    return xf * lax.rsqrt(jnp.sum(xf * xf, axis=-1, keepdims=True) + eps)

def depthwise_conv(x, w):
    k, c = w.shape
    pad = (k - 1) // 2
    return lax.conv_general_dilated(
        x, w[:, None, :].astype(x.dtype), window_strides=(1,), padding=[(pad, pad)],
        dimension_numbers=("NWC", "WIO", "NWC"), feature_group_count=c)

def alibi_slopes(n):
    def pow2(m):
        start = 2.0 ** (-8.0 / m)
        return [start ** (i + 1) for i in range(m)]
    if math.log2(n).is_integer():
        s = pow2(n)
    else:
        c = 2 ** int(math.floor(math.log2(n)))
        s = pow2(c) + pow2(2 * c)[0::2][: n - c]
    return jnp.asarray(s, dtype=jnp.float32)

def conv_module(u, dw_w, dw_b, ln_w, ln_b):
    a, g = jnp.split(u, 2, axis=-1)
    h = a * jax.nn.sigmoid(g)
    h = depthwise_conv(h, dw_w) + dw_b.astype(h.dtype)
    h = layer_norm(h, ln_w, ln_b)
    return jax.nn.silu(h)

def diff_attention(q, k, v, lam_q1, lam_k1, lam_q2, lam_k2, subln_w, layer_idx):
    B, S = q.shape[0], q.shape[1]
    H = DIFF_HEADS
    f32 = jnp.float32
    lambda_init = 0.8 - 0.6 * math.exp(-0.3 * layer_idx)
    lam = (jnp.exp(jnp.sum(lam_q1.astype(f32) * lam_k1.astype(f32)))
           - jnp.exp(jnp.sum(lam_q2.astype(f32) * lam_k2.astype(f32))) + lambda_init)
    slopes = jnp.repeat(alibi_slopes(H), 2)
    n_blk = S // Q_BLOCK
    qf = q.astype(f32).reshape(B, n_blk, Q_BLOCK, 2 * H, DIFF_DIM) * (DIFF_DIM ** -0.5)
    qf = jnp.moveaxis(qf, 1, 0)
    kf = k.astype(f32).reshape(B, S, 2 * H, DIFF_DIM)
    vf = v.astype(f32).reshape(B, S, H, HEAD_DIM)
    kpos = jnp.arange(S)

    def block(args):
        q_blk, blk = args
        s = jnp.einsum("bqmd,bkmd->bmqk", q_blk, kf)
        qpos = blk * Q_BLOCK + jnp.arange(Q_BLOCK)
        dist = jnp.abs(qpos[:, None] - kpos[None, :]).astype(f32)
        p = jax.nn.softmax(s - slopes[:, None, None] * dist, axis=-1)
        p = p.reshape(B, H, 2, Q_BLOCK, S)
        a = p[:, :, 0] - lam * p[:, :, 1]
        return jnp.einsum("bhqk,bkhe->bqhe", a, vf)

    o = lax.map(block, (qf, jnp.arange(n_blk)))
    o = jnp.moveaxis(o, 0, 1).reshape(B, S, H, HEAD_DIM)
    o = rms_norm_2(o, subln_w, eps=1e-5) * (1.0 - lambda_init)
    return o.reshape(B, S, H * HEAD_DIM).astype(q.dtype)

def chunk_gated_delta(q, k, v, g, beta):
    B, S, H, Dk = q.shape
    Dv = v.shape[-1]
    N = S // CHUNK
    q = q * (Dk ** -0.5)

    def chunks(t):
        return t.reshape(B, N, CHUNK, H, -1).transpose(0, 3, 1, 2, 4)

    qc, kc, vc = chunks(q), chunks(k), chunks(v)
    gc = jnp.cumsum(g.reshape(B, N, CHUNK, H).transpose(0, 3, 1, 2), axis=-1)
    bc = beta.reshape(B, N, CHUNK, H).transpose(0, 3, 1, 2)
    idx = jnp.arange(CHUNK)
    lower = idx[:, None] >= idx[None, :]
    strict = idx[:, None] > idx[None, :]
    decay = jnp.exp(jnp.where(lower, gc[..., :, None] - gc[..., None, :], -jnp.inf))
    kb = kc * bc[..., None]
    A = jnp.where(strict, jnp.einsum("bhncd,bhnsd->bhncs", kb, kc) * decay, 0.0)
    rhs = jnp.concatenate([vc * bc[..., None], kb * jnp.exp(gc)[..., None]], axis=-1)
    sol = lax.linalg.triangular_solve(A, rhs, left_side=True, lower=True, unit_diagonal=True)
    u, w = sol[..., :Dv], sol[..., Dv:]
    Aqk = jnp.einsum("bhncd,bhnsd->bhncs", qc, kc) * decay
    qg = qc * jnp.exp(gc)[..., None]
    kdec = kc * jnp.exp(gc[..., -1:] - gc)[..., None]
    glast = jnp.exp(gc[..., -1])

    def step(state, inp):
        u_i, w_i, qg_i, aqk_i, kdec_i, gl_i = inp
        v_new = u_i - jnp.einsum("bhcd,bhde->bhce", w_i, state)
        o = jnp.einsum("bhcd,bhde->bhce", qg_i, state) + jnp.einsum("bhcs,bhse->bhce", aqk_i, v_new)
        state = state * gl_i[..., None, None] + jnp.einsum("bhcd,bhce->bhde", kdec_i, v_new)
        return state, o

    xs = tuple(jnp.moveaxis(t, 2, 0) for t in (u, w, qg, Aqk, kdec, glast))
    s0 = jnp.zeros((B, H, Dk, Dv), jnp.float32)
    _, o = lax.scan(step, s0, xs)
    return o.transpose(1, 0, 3, 2, 4).reshape(B, S, H, Dv)

def gated_deltanet(qkv, z, b_f, b_b, a_f, a_b, conv_w, A_log, dt_bias, norm_w):
    B, S, _ = qkv.shape
    H, D = DELTA_HEADS, HEAD_DIM
    f32 = jnp.float32
    out_dtype = qkv.dtype
    qkv = jax.nn.silu(depthwise_conv(qkv, conv_w))
    q, k, v = jnp.split(qkv, 3, axis=-1)
    q = l2norm(q.reshape(B, S, H, D))
    k = l2norm(k.reshape(B, S, H, D))
    v = v.reshape(B, S, H, D).astype(f32)

    def log_decay(a, a_log, dtb):
        return -jnp.exp(a_log.astype(f32)) * jax.nn.softplus(a.astype(f32) + dtb.astype(f32))

    g_f = log_decay(a_f, A_log[0], dt_bias[0])
    g_b = log_decay(a_b, A_log[1], dt_bias[1])
    beta_f = jax.nn.sigmoid(b_f.astype(f32))
    beta_b = jax.nn.sigmoid(b_b.astype(f32))
    o_f = chunk_gated_delta(q, k, v, g_f, beta_f)
    rev = lambda t: jnp.flip(t, axis=1)
    o_b = rev(chunk_gated_delta(rev(q), rev(k), rev(v), rev(g_b), rev(beta_b)))
    o = rms_norm_2(o_f + o_b, norm_w) * jax.nn.silu(z.astype(f32).reshape(B, S, H, D))
    return o.reshape(B, S, H * D).astype(out_dtype)

def second_inputs(seed: int = 0) -> dict:
    key = jax.random.key(seed)
    ks = jax.random.split(key, 24)
    f32 = jnp.float32
    nrm = lambda k, shape, scale: jax.random.normal(k, shape, f32) * scale
    gain = lambda k, shape: 1.0 + 0.05 * jax.random.normal(k, shape, f32)
    dt = jnp.exp(jax.random.uniform(ks[20], (DEPTH, 2, DELTA_HEADS), f32, math.log(1e-3), math.log(1e-1)))
    return {
        "x": nrm(ks[0], (BATCH, SEQ, D_MODEL), 1.0),
        "w_in": nrm(ks[1], (DEPTH, D_MODEL, IN_W), D_MODEL ** -0.5),
        "w_out": nrm(ks[2], (DEPTH, D_MODEL, D_MODEL), D_MODEL ** -0.5),
        "pre_mix_w": gain(ks[3], (DEPTH, D_MODEL)),
        "post_mix_w": gain(ks[4], (DEPTH, D_MODEL)),
        "pre_mlp_w": gain(ks[5], (DEPTH, D_MODEL)),
        "post_mlp_w": gain(ks[6], (DEPTH, D_MODEL)),
        "w_ff1": nrm(ks[7], (DEPTH, D_MODEL, D_FF), D_MODEL ** -0.5),
        "w_ff2": nrm(ks[8], (DEPTH, D_FF, D_MODEL), D_FF ** -0.5),
        "conv_dw_w": nrm(ks[9], (DEPTH, CONV_WIDTH, CONV_CH), CONV_WIDTH ** -0.5),
        "conv_dw_b": nrm(ks[10], (DEPTH, CONV_CH), 0.02),
        "conv_ln_w": gain(ks[11], (DEPTH, CONV_CH)),
        "conv_ln_b": nrm(ks[12], (DEPTH, CONV_CH), 0.02),
        "diff_lambda_q1": nrm(ks[13], (DEPTH, DIFF_DIM), 0.1),
        "diff_lambda_k1": nrm(ks[14], (DEPTH, DIFF_DIM), 0.1),
        "diff_lambda_q2": nrm(ks[15], (DEPTH, DIFF_DIM), 0.1),
        "diff_lambda_k2": nrm(ks[16], (DEPTH, DIFF_DIM), 0.1),
        "diff_subln_w": gain(ks[17], (DEPTH, HEAD_DIM)),
        "delta_conv_w": nrm(ks[18], (DEPTH, SHORT_CONV, 3 * DELTA_W), SHORT_CONV ** -0.5),
        "delta_A_log": jnp.log(jax.random.uniform(ks[19], (DEPTH, 2, DELTA_HEADS), f32, 1.0, 16.0)),
        "delta_dt_bias": dt + jnp.log(-jnp.expm1(-dt)),
        "delta_norm_w": gain(ks[21], (DEPTH, HEAD_DIM)),
    }

def second_block(x, w_in, w_out, pre_mix_w, post_mix_w, pre_mlp_w, post_mlp_w, w_ff1, w_ff2,
              conv_dw_w, conv_dw_b, conv_ln_w, conv_ln_b,
              diff_lambda_q1, diff_lambda_k1, diff_lambda_q2, diff_lambda_k2, diff_subln_w,
              delta_conv_w, delta_A_log, delta_dt_bias, delta_norm_w):
    sizes = [2 * CONV_CH, DIFF_W, DIFF_W, DIFF_W, 3 * DELTA_W, DELTA_W,
             DELTA_HEADS, DELTA_HEADS, DELTA_HEADS, DELTA_HEADS]
    offs = [sum(sizes[: i + 1]) for i in range(len(sizes) - 1)]
    for l in range(DEPTH):
        h = rms_norm_2(x, pre_mix_w[l])
        u = h @ w_in[l]
        (u_conv, dq, dk, dv, gqkv, gz, b_f, b_b, a_f, a_b) = jnp.split(u, offs, axis=-1)
        y_conv = conv_module(u_conv, conv_dw_w[l], conv_dw_b[l], conv_ln_w[l], conv_ln_b[l])
        y_diff = diff_attention(dq, dk, dv, diff_lambda_q1[l], diff_lambda_k1[l],
                                diff_lambda_q2[l], diff_lambda_k2[l], diff_subln_w[l], l)
        y_delta = gated_deltanet(gqkv, gz, b_f, b_b, a_f, a_b, delta_conv_w[l],
                                 delta_A_log[l], delta_dt_bias[l], delta_norm_w[l])
        y = jnp.concatenate([y_conv, y_diff, y_delta], axis=-1) @ w_out[l]
        x = x + rms_norm_2(y, post_mix_w[l])
        h = rms_norm_2(x, pre_mlp_w[l])
        y = jnp.square(jax.nn.relu(h @ w_ff1[l])) @ w_ff2[l]
        x = x + rms_norm_2(y, post_mlp_w[l])
    return x


def setup_inputs(seed=0):
    out = dict(first_inputs(seed))
    for name, value in second_inputs(seed + 1).items():
        if name != "x":
            out[name + "_2"] = value
    return out


def reference(
    x, c, ctx, c_ctx, mod_w, mod_b, norm_g, ffn_w_in, ffn_w_out, even_w_in, even_w_out,
    attn_qk_norm_g, attn_sink, hgrn_out_norm_g, hgrn_lb, odd_w_in, odd_w_out, w_in_2, w_out_2,
    pre_mix_w_2, post_mix_w_2, pre_mlp_w_2, post_mlp_w_2, w_ff1_2, w_ff2_2, conv_dw_w_2,
    conv_dw_b_2, conv_ln_w_2, conv_ln_b_2, diff_lambda_q1_2, diff_lambda_k1_2, diff_lambda_q2_2,
    diff_lambda_k2_2, diff_subln_w_2, delta_conv_w_2, delta_A_log_2, delta_dt_bias_2,
    delta_norm_w_2,
):
    x = first_block(
        x, c, ctx, c_ctx, mod_w, mod_b, norm_g, ffn_w_in, ffn_w_out, even_w_in, even_w_out,
        attn_qk_norm_g, attn_sink, hgrn_out_norm_g, hgrn_lb, odd_w_in, odd_w_out,
    )
    return second_block(
        x, w_in_2, w_out_2, pre_mix_w_2, post_mix_w_2, pre_mlp_w_2, post_mlp_w_2, w_ff1_2,
        w_ff2_2, conv_dw_w_2, conv_dw_b_2, conv_ln_w_2, conv_ln_b_2, diff_lambda_q1_2,
        diff_lambda_k1_2, diff_lambda_q2_2, diff_lambda_k2_2, diff_subln_w_2, delta_conv_w_2,
        delta_A_log_2, delta_dt_bias_2, delta_norm_w_2,
    )


_drawn_inputs = setup_inputs


def setup_inputs(seed=0):
    import zlib

    import numpy as np

    out = dict(_drawn_inputs(seed))
    spreads = {}
    factors = {'norm_g': 3.002,
     'attn_qk_norm_g': 8.0,
     'attn_sink': 8.0,
     'hgrn_out_norm_g': 8.0,
     'hgrn_lb': 8.0,
     'conv_dw_b_2': 11.458,
     'conv_ln_b_2': 20.404,
     'diff_lambda_k2_2': 11.322,
     'post_mix_w_2': 4.056,
     'pre_mlp_w_2': 3.759,
     'post_mlp_w_2': 4.194,
     'conv_ln_w_2': 7.074,
     'diff_lambda_k1_2': 3.797,
     'diff_subln_w_2': 5.852,
     'delta_norm_w_2': 8.0}
    for name, (base, spread) in spreads.items():
        noise = np.random.default_rng([zlib.crc32(name.encode()), seed]).standard_normal(out[name].shape)
        drawn = base * np.exp(spread * noise) if base else spread * noise
        out[name] = jnp.asarray(drawn.astype(out[name].dtype))
    for name, factor in factors.items():
        out[name] = (out[name] * factor).astype(out[name].dtype)
    return out
```

```python
from contextlib import ExitStack
import math

import numpy as np

import concourse.bass as bass
from concourse import mybir

ALU = mybir.AluOpType
ACT = mybir.ActivationFunctionType
AXX = mybir.AxisListType.X
F32 = mybir.dt.float32
F32R = mybir.dt.float32r
F16, BF16 = mybir.dt.float16, mybir.dt.bfloat16
U32 = mybir.dt.uint32

P = 128
D = 1024
KD = D // P
CTX, SEQ = 256, 512
T = CTX + SEQ
LAT = slice(CTX, T)
GRID_W = 64
HID = 2816
EVEN_IN = 3328
ODD_DK, ODD_DV, ODD_H = 256, 512, 4
HD = 64
CH = 64
WIN = 128
D_FF = 4096
CONV_CH, DIFF_W, DELTA_W = 256, 384, 384
CONV_K = 31
IN2 = 2 * CONV_CH + 3 * DIFF_W + 4 * DELTA_W + 24
NEG = -1.0e30
SET = 26

GW = 256
SLOTS = 2
SLOT_W = KD * GW
X0 = 0
H0 = X0 + KD * T
RING0 = H0 + 2 * KD * T
SPLIT0 = RING0 + SLOTS * SLOT_W
C0 = SPLIT0 + 2 * SLOTS * SLOT_W
IDENT0, ONES0, BD0 = C0, C0 + P, C0 + 2 * P
PV0 = C0 + 3 * P
PV_W = 5 * P
M0 = PV0 + PV_W
M_W = 2 * 48 * 2
SM0 = M0 + M_W
SM_W = 256
U0 = SM0 + SM_W
U_W = 26 * T
ARENA = 53200
assert U0 + U_W <= ARENA and U0 + (D_FF // P + KD) * SEQ <= ARENA
T0 = H0
TW0 = RING0
Y0 = U0 + D_FF // P * SEQ

ROW_C, ROW_CC, ROW_NG, ROW_LB, ROW_OG, ROW_QKG = 0, 8, 16, 48, 56, 57
ROW2 = 2 * P
ROW_PREMIX, ROW_POSTMIX, ROW_PREMLP, ROW_POSTMLP = ROW2, ROW2 + 16, ROW2 + 32, ROW2 + 48
ROW_DWB, ROW_LNW, ROW_LNB, ROW_SUB, ROW_DN = ROW2 + 64, ROW2 + 68, ROW2 + 72, ROW2 + 76, ROW2 + 78
ROW_DW, ROW_SC = 3 * P, 4 * P

EPS6, EPS5, ZERO, ONE = SM0, SM0 + 1, SM0 + 2, SM0 + 3
COND0 = SM0 + 4
A0 = SM0 + 20
LBV0 = SM0 + 36
SINK0 = SM0 + 44
EIGHTH, SUBG, NLAM = SM0 + 76, SM0 + 77, SM0 + 78
GX0 = SM0 + 80


def constants():
    p = np.arange(P)
    c = {}
    c["ident"] = np.eye(P)
    c["ones"] = np.ones((P, P))
    c["bd"] = (p[:, None] // HD == p[None, :] // HD) * 1.0
    rot = np.zeros((P, P))
    for m in range(P):
        b, r = m // HD * HD, m % HD
        if r < HD // 2:
            rot[b + r + HD // 2, m] = -1.0
        else:
            rot[b + r - HD // 2, m] = 1.0
    c["rot"] = rot
    for v in range(2):
        c[f"dup{v}"] = (p[:, None] == v * HD + p[None, :] % HD) * 1.0
    s, q = p[None, :], p[:, None]
    c["wmask"] = np.concatenate([np.where(s >= q, 0, NEG), np.zeros((P, P)), np.where(s <= q, 0, NEG)], 1)
    t = np.arange(SEQ)
    n_freq = HD // 4
    inv = 10000.0 ** (-np.arange(n_freq, dtype=np.float32) / np.float32(n_freq))
    inv = inv.astype(np.float32)
    ang = np.concatenate([(t // GRID_W).astype(np.float32)[:, None] * inv,
                          (t % GRID_W).astype(np.float32)[:, None] * inv], 1).astype(np.float32)
    c["cosA"] = np.cos(ang.astype(np.float64)).T[p % (HD // 2)]
    c["sinA"] = np.sin(ang.astype(np.float64)).T[p % (HD // 2)]
    cols = np.arange(T)
    c["scan"] = np.tile(np.where(cols % CH == 0, 0.0, 1.0), (P, 1))
    same = p[:, None] // CH == p[None, :] // CH
    c["tri_fw"], c["tri_bw"] = (same & (p[:, None] <= p[None, :])) * 1, (same & (p[:, None] >= p[None, :])) * 1
    theta = (1.0 / (10000.0 ** np.linspace(0.0, 1.0, ODD_DK // 2))).astype(np.float32)
    ang = (t.astype(np.float32)[:, None] * theta).astype(np.float32).astype(np.float64)
    c["cosR"], c["sinR"] = np.cos(ang).T, np.sin(ang).T
    lg = np.log(1.0 - 2.0 ** (-5.0 - np.arange(ODD_H)))
    for h in range(ODD_H):
        gf, gb = lg[h], lg[ODD_H - 1 - h]
        d = np.arange(7 * P)[None, :] - p[:, None] - 3 * P
        w = np.where(d >= 0, np.exp(gf * np.maximum(d, 0)), 0) + np.where(d <= 0, np.exp(gb * np.maximum(-d, 0)), 0)
        d = np.arange(5 * P)[None, :] - p[:, None] - P
        wc = np.exp(gf * (d + CTX)) + np.exp(gb * (SEQ - d))
        c[f"ret{h}"] = np.concatenate([w, wc], 1) * ODD_DK ** -0.5
    c["dist"] = np.abs(p[:, None] - (np.arange(7 * P)[None, :] - 3 * P))
    c["cum_fw"] = (p[:, None] <= p[None, :]) * 1.0
    c["cum_bw"] = (p[:, None] >= p[None, :]) * 1.0
    for lv in range(7):
        b = 1 << lv
        r, q2 = p[:, None] // b, p[None, :] // b
        low = (r % 2 == 1) & (q2 == r - 1)
        c[f"lev_fw{lv}"] = low * 1.0
        c[f"lev_bw{lv}"] = low.T * 1.0
    names = list(c)
    at, off = {}, 0
    for n in names:
        c[n] = np.asarray(c[n])
        at[n] = (off, c[n].shape[1])
        off += c[n].shape[1]
    table = np.concatenate([c[n].astype(np.int32).view(np.float32) if n.startswith("tri_") else
                            c[n].astype(np.float32) for n in names], 1)
    return np.ascontiguousarray(table), at


S0 = H0
DT = IN2 // P


class Chain:

    def __init__(self, eng, sem):
        self.eng, self.sem, self.n = eng, sem, 0

    def __call__(self, ins):
        ins.then_inc(self.sem, 1)
        self.n += 1
        return self.n

    def wait(self, n=None):
        n = self.n if n is None else n
        if n > 0:
            self.eng.wait_ge(self.sem, n)


def rounds(eng, n, body):
    if n == 1:
        body(0)
    elif n > 1:
        with eng.Fori(0, n) as i:
            body(i)


class Core:

    def __init__(self, nc, table, at):
        self.nc = nc
        base = -(-nc.sbuf_base // 32) * 32

        def at_word(name, first, end, dtype=F32):
            return nc.alloc_sbuf_tensor_at(name, [P, end - first], dtype, offset=base + 4 * first)
        self.parts = [(0, H0, at_word("stream", 0, H0)), (H0, C0, at_word("work", H0, C0)),
                      (C0, ARENA, at_word("kept", C0, ARENA))]
        self.h_halves = at_word("h_halves", H0, RING0, F32R)
        self.w_halves = at_word("w_halves", SPLIT0, C0, F32R)
        self.ps = nc.alloc_psum_tensor("banks", [P, 8, 512], F32)
        self.ring_ready = [nc.alloc_semaphore(f"ring_ready{s}") for s in range(SLOTS)]
        self.ring_count = [0] * SLOTS
        self.table = nc.inline_tensor(table, "tables").ap()
        self.at = at
        self.sets = [[nc.alloc_semaphore(f"stage{r}_{n}") for n in range(SET)] for r in range(3)]
        self.stages = 0

    def sb(self, first, width, rows=P):
        if isinstance(first, int):
            lo, _, part = [p for p in self.parts if p[0] <= first < p[1]][0]
            return part[0:rows, first - lo:first - lo + width]
        return self.parts[2][2][:, bass.ds(first - C0, width)]

    def stream(self, first, width):
        part = self.parts[0][2]
        return part[:, first:first + width] if isinstance(first, int) else part[:, bass.ds(first, width)]

    def x(self, k):
        return self.sb(X0 + k * T, T)

    def h(self, k, low=0):
        return self.h_halves[:, (low * KD + k) * T:(low * KD + k + 1) * T]

    def u(self, k):
        return self.sb(U0 + k * T, T)

    def ident(self):
        return self.sb(IDENT0, P)

    def col(self, c):
        return self.sb(c, 1)

    def const(self, name):
        o, w = self.at[name]
        return self.table[:, o:o + w]

    def slot(self, s):
        return self.sb(RING0 + s * SLOT_W, SLOT_W).rearrange("p (k n) -> p k n", k=KD)

    def half(self, s, low):
        return self.w_halves[:, (2 * s + low) * SLOT_W:(2 * s + low + 1) * SLOT_W]

    def sems(self, n):
        r = self.stages % 3
        if self.stages > 0:
            last = self.sets[(r + 2) % 3]
            self.nc.sync.sem_clear(range(last[0].num, last[0].num + self.used))
        self.used = n
        self.stages += 1
        return self.sets[r][:n]


def halves_high(core, act, dst, src):
    return core.nc.scalar.activation(dst, src, ACT.Copy)


def halves_low(core, dve, dst, src, high):
    return core.nc.vector.tensor_tensor(dst, src, high.bitcast(F32), ALU.subtract)


class Dense:

    def __init__(self, core, w, rhs, k_tiles, groups, col, segs, finish, split=False, widths=None):
        self.core, self.rhs, self.groups, self.col, self.segs, self.finish = core, rhs, groups, col, segs, finish
        self.w = w.rearrange("(k p) n -> p k n", p=P)
        self.K = k_tiles
        n = -(-k_tiles // KD)
        self.chunks = [(c * KD, min(k_tiles, (c + 1) * KD)) for c in range(n)]
        self.body = 4 if n % 2 else 2
        self.split, self.once = split, k_tiles <= KD
        self.widths = widths or {}
        self.base, self.retired = None, False

    def width(self, g):
        return self.widths.get(g, GW)

    def load(self, sp, i, u):
        core, C = self.core, len(self.chunks)
        j, c = divmod(u, C)
        a, b = self.chunks[c]
        wd = self.width(i * self.body + j) if isinstance(i, int) else GW
        cols = self.col(i * self.body, j)
        src = self.w[:, a:b, cols:cols + wd] if isinstance(cols, int) else self.w[:, a:b, bass.ds(cols, wd)]
        s = u % SLOTS
        sp.dma_start(core.slot(s)[:, 0:b - a, 0:wd], src).then_inc(core.ring_ready[s], 16)

    def preload(self, sp):
        self.base = list(self.core.ring_count)
        for u in range(min(SLOTS, self.groups * len(self.chunks))):
            self.load(sp, 0, u)

    def run(self, name, after=None):
        core, nc, C, B, G, K = self.core, self.core.nc, len(self.chunks), self.body, self.groups, self.K
        units, finish = G * C, self.finish
        releases = sum(finish.releases)
        (group_summed, chunk_used, relu_done, even_free, odd_free, high_done, low_done, rhs_high, rhs_low,
         rhs_used) = core.sems(10)
        free = [even_free, odd_free]
        fly = self.split and not self.once
        preloaded = self.base is not None
        lo, width = min(s[0] for s in self.segs), sum(s[1] for s in self.segs)

        def banks(j, f):
            return [core.ps[:, 4 * n + (j % 2) * 2 + f, 0:w] for n, (_, w) in enumerate(self.segs)]

        def wait_unit(eng, i, u):
            j, c = divmod(u, C)
            if c < C - 1:
                eng.wait_ge(chunk_used, (i * B + j) * (C - 1) + c + 1)
            else:
                eng.wait_ge(group_summed, (i * B + j) * 2 + 2)

        def units_of(eng, n, body):
            rounds(eng, n // (B * C), lambda i: [body(i, u) for u in range(B * C)])
            for u in range(n % (B * C)):
                body(n // (B * C), u)

        def at(i, v):
            return (i + v // (B * C), v % (B * C)) if isinstance(i, int) else (i, v)

        def unit_words(v):
            a, b = self.chunks[v % C]
            return (b - a) * GW

        def first_tile(v):
            return v // C * K + self.chunks[v % C][0]

        def splitter(eng, weights, tiles):
            def run(evacuate):
                if self.split:
                    for k in range(self.chunks[0][1]):
                        tiles(0, k, k)
                weights(0, 0)
                if units > 1:
                    weights(0, 1)

                def step(i, u):
                    if fly:
                        a, b = self.chunks[(u + 1) % C]
                        for k in range(a, b):
                            tiles(i, first_tile(u + 1) + k - a, k)
                    wait_unit(eng, i, u)
                    if u % C == C - 1:
                        evacuate(i, u // C)
                    weights(i, u + 2)
                n = max(0, units - 2)
                units_of(eng, n, step)
                for u in range(n, units):
                    i, v = divmod(u, B * C)
                    if fly and u < units - 1:
                        a, b = self.chunks[(v + 1) % C]
                        for k in range(a, b):
                            tiles(i, first_tile(v + 1) + k - a, k)
                    wait_unit(eng, i, v)
                    if v % C == C - 1:
                        evacuate(i, v // C)
            return run

        with nc.Block() as block:
            @block.sync
            def _(sp):
                if not preloaded:
                    self.preload(sp)

                def refill(i, u):
                    sp.wait_ge(low_done, i * B * C + u + 1)
                    self.load(sp, *at(i, u + SLOTS))
                units_of(sp, max(0, units - SLOTS), refill)
                if after is not None:
                    sp.wait_ge(low_done, units)
                    self.retire()
                    after.preload(sp)

            @block.tensor
            def _(pe):
                def group(i, j):
                    r = i * (B // 2) + j // 2
                    pe.wait_ge(free[j % 2], (r + 1) * 2 * releases)
                    for c, (a, b) in enumerate(self.chunks):
                        u = j * C + c
                        pe.wait_ge(low_done, i * B * C + u + 1)
                        high, low = (core.half(u % SLOTS, n).rearrange("p (k n) -> p k n", k=KD) for n in range(2))
                        for k in range(a, b):
                            n = j * K + k
                            if fly:
                                pe.wait_ge(rhs_low, i * B * K + n + 1)
                            elif self.split:
                                pe.wait_ge(rhs_low, k + 1)
                            q = n % KD if fly else k
                            rh, rl = (core.h(q), core.h(q, 1)) if self.split else (self.rhs(k, 0), self.rhs(k, 1))
                            for f in range(2):
                                fc = slice(f * P, (f + 1) * P)
                                for s, (t0, tw) in enumerate(self.segs):
                                    tc = slice(t0, t0 + tw)
                                    o = banks(j, f)[s]
                                    nc.tensor.matmul(o, low[:, k - a, fc], rh[:, tc], start=(k == 0), stop=False)
                                    nc.tensor.matmul(o, high[:, k - a, fc], rl[:, tc], start=False, stop=False)
                                    mm = nc.tensor.matmul(o, high[:, k - a, fc], rh[:, tc], start=False, stop=(k == K - 1))
                                if k == K - 1:
                                    mm.then_inc(group_summed, 1)
                            if k == b - 1 and c < C - 1:
                                mm.then_inc(chunk_used, 1)
                            elif fly and k < K - 1:
                                mm.then_inc(rhs_used, 1)
                rounds(pe, G // B, lambda i: [group(i, j) for j in range(B)])
                for j in range(G % B):
                    group(G // B, j)

            def wait_tile(eng, i, n):
                m = n - KD
                if n < KD and isinstance(i, int) and i == 0:
                    return
                j, k = divmod(m, K) if m >= 0 else (-1, m + K)
                c = k // KD
                if k == self.chunks[c][1] - 1:
                    if c < C - 1:
                        eng.wait_ge(chunk_used, (i * B + j) * (C - 1) + c + 1)
                    else:
                        eng.wait_ge(group_summed, (i * B + j) * 2 + 2)
                else:
                    eng.wait_ge(rhs_used, (i * B + j) * (K - C) + k - c + 1)

            @block.scalar
            def _(act):
                act.sem_inc(even_free, 2 * releases)
                act.sem_inc(odd_free, 2 * releases)

                def weights(i, v):
                    s = v % SLOTS
                    act.wait_ge(core.ring_ready[s], self.base[s] + (i * (B * C // SLOTS) + v // SLOTS + 1) * 16)
                    n = unit_words(v)
                    halves_high(core, act, core.half(s, 0)[:, 0:n],
                                core.sb(RING0 + s * SLOT_W, n)).then_inc(high_done, 1)

                def tiles(i, n, k):
                    if fly:
                        wait_tile(act, i, n)
                    halves_high(core, act, core.h(n % KD)[:, lo:lo + width],
                                self.rhs(k)[:, lo:lo + width]).then_inc(rhs_high, 1)

                def evacuate(i, j):
                    if finish.scalar is not None and finish.takes(j)[0]:
                        for f in range(2):
                            finish.scalar(act, i * B + j, j, f, banks(j, f), relu_done, free[j % 2])
                splitter(act, weights, tiles)(evacuate)

            @block.vector
            def _(dve):
                def weights(i, v):
                    s = v % SLOTS
                    dve.wait_ge(high_done, i * B * C + v + 1)
                    n = unit_words(v)
                    halves_low(core, dve, core.half(s, 1)[:, 0:n], core.sb(RING0 + s * SLOT_W, n),
                               core.half(s, 0)[:, 0:n]).then_inc(low_done, 1)

                def tiles(i, n, k):
                    dve.wait_ge(rhs_high, i * B * K + n + 1)
                    halves_low(core, dve, core.h(n % KD, 1)[:, lo:lo + width], self.rhs(k)[:, lo:lo + width],
                               core.h(n % KD)[:, lo:lo + width]).then_inc(rhs_low, 1)

                def evacuate(i, j):
                    if finish.vector is not None and finish.takes(j)[1]:
                        for f in range(2):
                            if finish.after_scalar:
                                dve.wait_ge(relu_done, (i * B + j) * 2 + f + 1)
                            finish.vector(dve, i * B + j, j, f, banks(j, f), free[j % 2], even_free)
                splitter(dve, weights, tiles)(evacuate)

        if after is None:
            self.retire()

    def retire(self):
        if self.base is not None and not self.retired:
            n = self.groups * len(self.chunks)
            self.core.ring_count = [self.base[s] + 16 * ((n - s + SLOTS - 1) // SLOTS) for s in range(SLOTS)]
            self.retired = True


class Finish:
    scalar = vector = None
    after_scalar = False
    releases = (0, 0)

    def takes(self, j):
        return True, True


class Copy(Finish):

    def __init__(self, core, nc, dst, segs, where=None):
        self.releases = (1, 1) if len(segs) == 2 else (1, 0)
        self.where = where or (lambda g, f: dst + (g * 2 + f) * T)

        def scalar(act, g, j, f, banks, half, free):
            lo, w = segs[0]
            nc.scalar.activation(core.sb(self.where(g, f) + lo, w), banks[0], ACT.Copy).then_inc(free, 1)

        def vector(dve, g, j, f, banks, free, gates):
            lo, w = segs[1]
            nc.vector.tensor_copy(core.sb(self.where(g, f) + lo, w), banks[1]).then_inc(free, 1)
        self.scalar = scalar
        self.vector = vector if len(segs) == 2 else None


class Residual(Finish):

    def __init__(self, core, nc, gate, segs):
        self.releases = (0, 1)

        def vector(dve, g, j, f, banks, free, gates):
            for n, (lo, w) in enumerate(segs):
                x = core.stream((g * 2 + f) * T + lo, w)
                ins = nc.vector.scalar_tensor_tensor(out=x, in0=banks[n], scalar=core.col(gate + (g * 2 + f) * 2 + n),
                                                     in1=x, op0=ALU.mult, op1=ALU.add)
            ins.then_inc(free, 1)
        self.vector = vector


class Swiglu(Finish):

    def __init__(self, core, nc, dst, segs):
        self.releases = (1, 0)

        def tile(g, j, f):
            return dst + ((g - j % 2) + f) * T

        def scalar(act, g, j, f, banks, half, free):
            for n, (lo, w) in enumerate(segs):
                ins = nc.scalar.activation(core.sb(tile(g, j, f) + lo, w), banks[n], ACT.Silu)
            ins.then_inc(free, 1)

        def vector(dve, g, j, f, banks, free, gates):
            dve.wait_ge(gates, g + f + 2)
            for n, (lo, w) in enumerate(segs):
                o = core.sb(tile(g, j, f) + lo, w)
                ins = nc.vector.tensor_tensor(o, o, banks[n], ALU.mult)
            ins.then_inc(free, 1)
        self.scalar, self.vector = scalar, vector

    def takes(self, j):
        return j % 2 == 0, j % 2 == 1


class SquaredRelu(Finish):
    after_scalar = True

    def __init__(self, core, nc, dst, segs):
        self.releases = (0, 1)
        lo, w = segs[0]

        def scalar(act, g, j, f, banks, half, free):
            nc.scalar.activation(core.sb(dst + (g * 2 + f) * SEQ, w), banks[0], ACT.Relu).then_inc(half, 1)

        def vector(dve, g, j, f, banks, free, gates):
            o = core.sb(dst + (g * 2 + f) * SEQ, w)
            nc.vector.tensor_tensor(o, o, banks[0], ALU.mult).then_inc(free, 1)
        self.scalar, self.vector = scalar, vector


def params_stage(core, nc, a, x_in, ctx_in):
    rows = [[], [], [], [], []]
    r1 = lambda ap, n: ap.rearrange("(r p) -> r p", p=P) if n else ap
    at = lambda t, r, n, c0=0, cw=P: core.sb(T0 + t * P + c0, cw)[r:r + n]
    loads = [
        (at(0, ROW_C, 8), a["c"].rearrange("o (r p) -> (o r) p", p=P)),
        (at(0, ROW_CC, 8), a["c_ctx"].rearrange("(r p) -> r p", p=P)),
        (at(0, ROW_NG, 32), a["norm_g"].rearrange("l n (r p) -> (l n r) p", p=P)),
        (at(0, ROW_LB, 8), a["hgrn_lb"].rearrange("l (r p) -> (l r) p", p=P)),
        (at(0, ROW_OG, 1), a["hgrn_out_norm_g"]),
        (at(1, 0, 96), a["mod_b"].rearrange("l (r p) -> (l r) p", p=P)),
    ]
    for half in range(2):
        loads.append((at(0, ROW_QKG, 2, half * HD, HD), a["attn_qk_norm_g"].rearrange("o r p -> (o r) p")))
        loads.append((at(2, ROW_SUB - ROW2, 2, half * HD, HD), a["diff_subln_w_2"]))
        loads.append((at(2, ROW_DN - ROW2, 2, half * HD, HD), a["delta_norm_w_2"]))
    for row, name in ((ROW_PREMIX, "pre_mix_w_2"), (ROW_POSTMIX, "post_mix_w_2"), (ROW_PREMLP, "pre_mlp_w_2"),
                      (ROW_POSTMLP, "post_mlp_w_2"), (ROW_DWB, "conv_dw_b_2"), (ROW_LNW, "conv_ln_w_2"),
                      (ROW_LNB, "conv_ln_b_2")):
        v = a[name].rearrange("l (r p) -> (l r) p", p=P)
        loads.append((at(2, row - ROW2, v.shape[0]), v))
    loads.append((at(3, 0, 124), a["conv_dw_w_2"].rearrange("l k (r p) -> (l k r) p", p=P)))
    loads.append((at(4, 0, 54), a["delta_conv_w_2"].rearrange("l k (r p) -> (l k r) p", p=P)))
    heights = [59, 96, 80, 124, 54]
    tok = core.sb(U0, 6 * D).rearrange("p (t d) -> p t d", t=6)

    tables_in, rows_in, tokens_in, rows_turned, tokens_turned, turned_used, smalls = core.sems(7)

    with nc.Block() as block:
        @block.sync
        def _(sp):
            for name, o in (("ident", IDENT0), ("ones", ONES0), ("bd", BD0)):
                sp.dma_start(core.sb(o, P), core.const(name)).then_inc(tables_in, 16)
            for dst, src in loads:
                sp.dma_start(dst, src).then_inc(rows_in, 16)
            sp.dma_start(core.sb(SINK0, 8), a["attn_sink"][0].partition_broadcast(P)).then_inc(rows_in, 16)
            sp.dma_start(tok[:, 0:2], ctx_in.rearrange("(t p) d -> p t d", p=P)).then_inc(tokens_in, 16)
            sp.dma_start(tok[:, 2:6], x_in.rearrange("(t p) d -> p t d", p=P)).then_inc(tokens_in, 16)

        @block.tensor
        def _(pe):
            pe.wait_ge(tables_in, 48)
            pe.wait_ge(rows_in, 16 * (len(loads) + 1))
            for t, n in enumerate(heights):
                mm = nc.tensor.transpose(core.ps[:, t, 0:n], core.sb(T0 + t * P, P, n),
                                         core.sb(IDENT0, n, n))
            mm.then_inc(rows_turned, 1)
            pe.wait_ge(tokens_in, 32)
            pe.wait_ge(turned_used, 1)
            for b in range(12):
                if b >= 8:
                    pe.wait_ge(turned_used, b - 8 + 2)
                for q in range(4):
                    k, t = divmod(b * 4 + q, 6)
                    mm = nc.tensor.transpose(core.ps[:, b % 8, q * P:(q + 1) * P], tok[:, t, k * P:(k + 1) * P],
                                             core.ident())
                mm.then_inc(tokens_turned, 1)

        @block.vector
        def _(dve):
            nc.vector.memset(core.col(EPS6), 1e-6)
            nc.vector.memset(core.col(EPS5), 1e-5)
            nc.vector.memset(core.col(ZERO), 0.0)
            nc.vector.memset(core.col(ONE), 1.0)
            nc.vector.memset(core.col(EIGHTH), HD ** -0.5)
            dve.wait_ge(rows_turned, 1)
            for t, n in enumerate(heights):
                last = nc.vector.tensor_copy(core.sb(PV0 + t * P, n), core.ps[:, t, 0:n])
            last.then_inc(turned_used, 1)
            dve.wait_ge(turned_used, 1)
            nc.vector.tensor_scalar(core.sb(SINK0 + 8, 8), core.sb(SINK0, 8), -1.0, None, ALU.mult)
            nc.vector.tensor_tensor(core.sb(LBV0, 4), core.sb(PV0 + ROW_LB + 4, 4), core.sb(PV0 + ROW_LB, 4),
                                    ALU.subtract).then_inc(smalls, 1)
            for b in range(12):
                dve.wait_ge(tokens_turned, b + 1)
                nc.vector.tensor_copy(core.sb(X0 + b * 512, 512), core.ps[:, b % 8, :]).then_inc(turned_used, 1)
            dve.wait_ge(smalls, 2)
            nc.vector.tensor_scalar(core.sb(LBV0 + 4, 4), core.sb(LBV0, 4), -1.0, 1.0, ALU.mult, ALU.add)

        @block.scalar
        def _(act):
            act.wait_ge(smalls, 1)
            nc.scalar.activation(core.sb(LBV0, 4), core.sb(LBV0, 4), ACT.Sigmoid, scale=-1.0).then_inc(smalls, 1)
            cond = core.sb(COND0, 16).rearrange("p (k n) -> p k n", n=2)
            for n, row in enumerate((ROW_C, ROW_CC)):
                nc.scalar.activation(cond[:, :, n], core.sb(PV0 + row, 8), ACT.Silu).then_inc(smalls, 1)


def modulation_stage(core, nc, mod_w):
    slots, body, cols = 3, 6, 512
    per_layer = mod_w.shape[2] // cols
    slot = lambda s: core.sb(RING0 + s * KD * cols, KD * cols).rearrange("p (k n) -> p k n", k=KD)
    row = lambda b: core.sb(U0 + b * cols, cols, 2)
    (in0, in1, in2, rows_summed, rows_copied, rows_turned, bias_added) = core.sems(7)
    weights_in = [in0, in1, in2]
    layers = mod_w.shape[0]
    R = per_layer // body
    turned = lambda j: core.ps[:, 2 + j % 2, 0:8]

    def loop(eng, body_of):
        for layer in range(layers):
            if layer == 0:
                body_of(0, 0, 0)
                rounds(eng, R - 1, lambda i: body_of(0, i + 1, 1))
            else:
                rounds(eng, R, lambda i: body_of(layer, i, 1))

    with nc.Block() as block:
        @block.sync
        def _(sp):
            def body_of(layer, i, later):
                for j in range(body):
                    g = (layer * R + i) * body + j
                    if later or j >= slots:
                        sp.wait_ge(rows_summed, g - slots + 1)
                    w = mod_w[layer].rearrange("(k p) n -> p k n", p=P)
                    sp.dma_start(slot(j % slots), w[:, :, bass.ds((i * body + j) * cols, cols)]
                                 ).then_inc(weights_in[j % slots], 16)
            loop(sp, body_of)

        @block.tensor
        def _(pe):
            def turn(g, j):
                for q in range(4):
                    mm = nc.tensor.transpose(turned(j)[:, 2 * q:2 * q + 2], row(j % 2)[:, q * P:(q + 1) * P],
                                             core.sb(IDENT0, 2, 2))
                mm.then_inc(rows_turned, 1)

            def body_of(layer, i, later):
                for j in range(body):
                    r = layer * R + i
                    g = r * body + j
                    pe.wait_ge(weights_in[j % slots], (r * (body // slots) + j // slots + 1) * 16)
                    if later or j >= 2:
                        pe.wait_ge(rows_copied, g - 1)
                    if later or j >= 4:
                        pe.wait_ge(bias_added, g - 3)
                    for k in range(KD):
                        mm = nc.tensor.matmul(core.ps[0:2, j % 2, 0:cols], core.sb(COND0 + 2 * k, 2),
                                              slot(j % slots)[:, k], start=(k == 0), stop=(k == KD - 1))
                    mm.then_inc(rows_summed, 1)
                    if later or j >= 2:
                        turn(g - 2, (j - 2) % body)
            loop(pe, body_of)
            for g in range(layers * per_layer - 2, layers * per_layer):
                pe.wait_ge(rows_copied, g + 1)
                pe.wait_ge(bias_added, g - 1)
                turn(g, g % body)

        @block.scalar
        def _(act):
            def body_of(layer, i, later):
                for j in range(body):
                    g = (layer * R + i) * body + j
                    act.wait_ge(rows_summed, g + 1)
                    if later or j >= 2:
                        act.wait_ge(rows_turned, g - 1)
                    nc.scalar.activation(row(j % 2), core.ps[0:2, j % 2, 0:cols], ACT.Copy).then_inc(rows_copied, 1)
            loop(act, body_of)

        @block.vector
        def _(dve):
            def body_of(layer, i, later):
                for j in range(body):
                    g = (layer * R + i) * body + j
                    dve.wait_ge(rows_turned, g + 1)
                    bias = core.sb(PV0 + P + g * 4, 4).rearrange("p (q n) -> p q n", n=1).broadcast_to([P, 4, 2])
                    nc.vector.tensor_tensor(core.sb(M0 + g * 8, 8).rearrange("p (q n) -> p q n", n=2),
                                            turned(j).rearrange("p (q n) -> p q n", n=2), bias,
                                            ALU.add).then_inc(bias_added, 1)
            loop(dve, body_of)


def norm_stage(core, nc, segs, gain, shift=None, scale=None, src=None, residual=False, extra_sync=None):
    src = src or core.x
    lo, w = min(s[0] for s in segs), sum(s[1] for s in segs)
    sq = [core.sb(U0 + b * T, T) for b in range(4)]
    std = core.sb(U0 + 4 * T, T)
    squared, square_used, summed, std_done, rstd_done, scaled, gains, high, low = core.sems(9)
    gaincol = (lambda n, k: core.col(A0 + n * 8 + k)) if scale is not None else (lambda n, k: core.col(gain + k))
    shiftcol = (lambda n, k: core.col(shift + k * 2 + n)) if shift is not None else (lambda n, k: core.col(ZERO))
    with nc.Block() as block:
        @block.scalar
        def _(act):
            for k in range(KD):
                if k >= 4:
                    act.wait_ge(square_used, k - 3)
                nc.scalar.activation(sq[k % 4][:, lo:lo + w], src(k)[:, lo:lo + w], ACT.Square).then_inc(squared, 1)
            act.wait_ge(summed, 1)
            for n, (s, sw) in enumerate(segs):
                nc.scalar.activation(std[:, s:s + sw], core.ps[:, n, 0:sw], ACT.Sqrt, bias=core.col(EPS6),
                                     scale=1.0 / D).then_inc(std_done, 1)
            if not residual:
                for k in range(KD):
                    act.wait_ge(scaled, k + 1)
                    for n, (s, sw) in enumerate(segs):
                        ins = nc.scalar.activation(core.h(k)[:, s:s + sw], sq[k % 4][:, s:s + sw], ACT.Identity,
                                                   bias=shiftcol(n, k), scale=1.0)
                    ins.then_inc(high, 1)

        @block.tensor
        def _(pe):
            for k in range(KD):
                pe.wait_ge(squared, k + 1)
                for n, (s, sw) in enumerate(segs):
                    mm = nc.tensor.matmul(core.ps[:, n, 0:sw], core.sb(ONES0, P), sq[k % 4][:, s:s + sw],
                                          start=(k == 0), stop=(k == KD - 1))
                mm.then_inc(square_used if k < KD - 1 else summed, 1)

        @block.vector
        def _(dve):
            if scale is not None:
                for n in range(len(segs)):
                    m = core.sb(scale, 16).rearrange("p (k n) -> p k n", n=2)[:, :, n]
                    nc.vector.scalar_tensor_tensor(out=core.sb(A0 + n * 8, 8), in0=m, scalar=1.0,
                                                   in1=core.sb(gain, 8), op0=ALU.add, op1=ALU.mult).then_inc(gains, 1)
                dve.wait_ge(gains, len(segs))
            for n, (s, sw) in enumerate(segs):
                dve.wait_ge(std_done, n + 1)
                nc.vector.reciprocal(std[:, s:s + sw], std[:, s:s + sw]).then_inc(rstd_done, 1)
            dve.wait_ge(rstd_done, len(segs))

            def lower(k):
                dve.wait_ge(high, k + 1)
                for n, (s, sw) in enumerate(segs):
                    ins = nc.vector.scalar_tensor_tensor(out=core.h(k, 1)[:, s:s + sw], in0=sq[k % 4][:, s:s + sw],
                                                         scalar=shiftcol(n, k), in1=core.h(k)[:, s:s + sw].bitcast(F32),
                                                         op0=ALU.add, op1=ALU.subtract)
                ins.then_inc(low, 1)

            for k in range(KD):
                if not residual and k >= 4:
                    dve.wait_ge(low, k - 3)
                for n, (s, sw) in enumerate(segs):
                    o = src(k)[:, s:s + sw] if residual else sq[k % 4][:, s:s + sw]
                    ins = nc.vector.scalar_tensor_tensor(out=o, in0=src(k)[:, s:s + sw], scalar=gaincol(n, k),
                                                         in1=std[:, s:s + sw], op0=ALU.mult, op1=ALU.mult)
                ins.then_inc(scaled, 1)
                if not residual and k:
                    lower(k - 1)
            if not residual:
                lower(KD - 1)

        @block.gpsimd
        def _(pool):
            if residual:
                for k in range(KD):
                    pool.wait_ge(scaled, k + 1)
                    s, sw = segs[0]
                    nc.gpsimd.tensor_tensor(core.x(k)[:, s:s + sw], core.x(k)[:, s:s + sw], src(k)[:, s:s + sw],
                                            ALU.add)

        if extra_sync is not None:
            block.sync(extra_sync)


def store_stage(core, nc, y):
    turned, copied, stored = core.sems(3)
    tok = core.sb(U0, 4 * D).rearrange("p (t d) -> p t d", t=4)
    with nc.Block() as block:
        @block.tensor
        def _(pe):
            for b in range(8):
                t, half = divmod(b, 2)
                for q in range(4):
                    mm = nc.tensor.transpose(core.ps[:, b, q * P:(q + 1) * P],
                                             core.x(half * 4 + q)[:, CTX + t * P:CTX + (t + 1) * P], core.ident())
                mm.then_inc(turned, 1)

        @block.vector
        def _(dve):
            for b in range(8):
                t, half = divmod(b, 2)
                dve.wait_ge(turned, b + 1)
                nc.vector.tensor_copy(tok[:, t, half * 512:half * 512 + 512], core.ps[:, b, :]).then_inc(copied, 1)

        @block.sync
        def _(sp):
            for t in range(4):
                sp.wait_ge(copied, 2 * t + 2)
                sp.dma_start(y[t * P:(t + 1) * P, :], tok[:, t]).then_inc(stored, 16)
            sp.wait_ge(stored, 64)


def group_norm(core, nc, name, groups, ones, count, segs, eps, sync=None, scratch=T0):
    lo, w = min(s[0] for s in segs), sum(s[1] for s in segs)
    sq = [core.sb(scratch + b * T, T) for b in range(4)]
    std = [core.sb(scratch + (4 + b) * T, T) for b in range(2)]
    squared, square_used, summed, std_done, rstd_done, scaled, multiplied = core.sems(7)
    items = [(g, q, it) for g, grp in enumerate(groups) for q, it in enumerate(grp)]
    first = [sum(len(x) for x in groups[:g]) for g in range(len(groups) + 1)]
    ns = len(segs)
    with nc.Block() as block:
        @block.scalar
        def _(act):
            def root(g):
                for n, (s, sw) in enumerate(segs):
                    act.wait_ge(summed, g + 1)
                    if g >= 2:
                        act.wait_ge(scaled, first[g - 1])
                    nc.scalar.activation(std[g % 2][:, s:s + sw], core.ps[:, (g % 2) * 2 + n, 0:sw], ACT.Sqrt,
                                         bias=core.col(eps), scale=1.0 / count).then_inc(std_done, 1)
            for g, grp in enumerate(groups):
                for q, it in enumerate(grp):
                    m = first[g] + q
                    if m >= 4:
                        act.wait_ge(square_used, m - 3)
                    nc.scalar.activation(sq[m % 4][:, lo:lo + w], it[0][:, lo:lo + w], ACT.Square).then_inc(squared, 1)
                if g >= 1:
                    root(g - 1)
            root(len(groups) - 1)

        @block.tensor
        def _(pe):
            for g, grp in enumerate(groups):
                if g >= 2:
                    pe.wait_ge(std_done, (g - 1) * ns)
                for q in range(len(grp)):
                    m = first[g] + q
                    pe.wait_ge(squared, m + 1)
                    for n, (s, sw) in enumerate(segs):
                        mm = nc.tensor.matmul(core.ps[:, (g % 2) * 2 + n, 0:sw], ones, sq[m % 4][:, s:s + sw],
                                              start=(q == 0), stop=(q == len(grp) - 1))
                    mm.then_inc(square_used, 1)
                pe.wait_ge(square_used, first[g + 1])
                pe.sem_inc(summed, 1)

        @block.vector
        def _(dve):
            for g, grp in enumerate(groups):
                for n, (s, sw) in enumerate(segs):
                    dve.wait_ge(std_done, g * ns + n + 1)
                    r = std[g % 2][:, s:s + sw]
                    nc.vector.reciprocal(r, r).then_inc(rstd_done, 1)
                dve.wait_ge(rstd_done, (g + 1) * ns)
                for src, out, gain, mul in grp:
                    nc.vector.scalar_tensor_tensor(out=out[:, lo:lo + w], in0=src[:, lo:lo + w],
                                                   scalar=core.col(gain), in1=std[g % 2][:, lo:lo + w],
                                                   op0=ALU.mult, op1=ALU.mult).then_inc(scaled, 1)

        @block.gpsimd
        def _(pool):
            for m, (g, q, (src, out, gain, mul)) in enumerate(items):
                if mul is not None:
                    pool.wait_ge(scaled, m + 1)
                    nc.gpsimd.tensor_tensor(out[:, lo:lo + w], out[:, lo:lo + w], mul[:, lo:lo + w], ALU.mult)

        if sync is not None:
            block.sync(sync)


def rope_stage(core, nc, tiles, wanted, v_tile, kdup, vtok, cos, sin, rot, dups):
    n = len(tiles)
    tmp = [core.sb(T0 + b * SEQ, SEQ) for b in range(4)]
    tables_in, rotated, sined, cosined, roped, duplicated, moved = core.sems(7)
    with nc.Block() as block:
        @block.sync
        def _(sp):
            for dst, name in wanted:
                sp.dma_start(dst, core.const(name)).then_inc(tables_in, 16)

        @block.tensor
        def _(pe):
            pe.wait_ge(tables_in, 16 * len(wanted))
            for t in range(n):
                if t >= 2:
                    pe.wait_ge(sined, t - 1)
                nc.tensor.matmul(core.ps[:, t % 2, :], rot, tiles[t][:, LAT], start=True, stop=True).then_inc(rotated, 1)
            for t in range(6):
                mm = nc.tensor.transpose(core.ps[:, 6 + t // 4, (t % 4) * P:(t % 4 + 1) * P],
                                         v_tile[:, t * P:(t + 1) * P], core.ident())
            mm.then_inc(duplicated, 1)
            pe.wait_ge(roped, n)
            for v in range(2):
                nc.tensor.matmul(core.ps[:, 2 + v, :], dups[v], tiles[n - 1][:, LAT], start=True, stop=True)
                mm = nc.tensor.matmul(core.ps[:, 4 + v, 0:CTX], dups[v], tiles[n - 1][:, 0:CTX], start=True, stop=True)
            mm.then_inc(duplicated, 1)

        @block.gpsimd
        def _(pool):
            pool.wait_ge(tables_in, 16 * len(wanted))
            for t in range(n):
                if t >= 2:
                    pool.wait_ge(roped, t - 1)
                nc.gpsimd.tensor_tensor(tmp[2 + t % 2], tiles[t][:, LAT], cos, ALU.mult).then_inc(cosined, 1)

        @block.vector
        def _(dve):
            dve.wait_ge(tables_in, 16 * len(wanted))
            for t in range(n):
                dve.wait_ge(rotated, t + 1)
                nc.vector.tensor_tensor(tmp[t % 2], core.ps[:, t % 2, :], sin, ALU.mult).then_inc(sined, 1)
                dve.wait_ge(sined, t + 1)
                dve.wait_ge(cosined, t + 1)
                nc.vector.tensor_tensor(tiles[t][:, LAT], tmp[t % 2], tmp[2 + t % 2], ALU.add).then_inc(roped, 1)

        @block.scalar
        def _(act):
            act.wait_ge(duplicated, 1)
            for b, w in ((0, 512), (1, 256)):
                nc.scalar.activation(vtok[:, b * 512:b * 512 + w], core.ps[:, 6 + b, 0:w], ACT.Copy)
            act.wait_ge(duplicated, 2)
            for v in range(2):
                nc.scalar.activation(kdup[v][:, LAT], core.ps[:, 2 + v, :], ACT.Copy)
                nc.scalar.activation(kdup[v][:, 0:CTX], core.ps[:, 4 + v, 0:CTX], ACT.Copy)


def window_stage(core, nc, tiles, kdup, vtok, wmask):
    steps = [(h, i) for h in range(8) for i in range(6)]
    N = len(steps)
    pr = [core.sb(T0 + b * 640, 640) for b in range(2)]
    pt = [core.sb(T0 + 1280 + b * 640, 640) for b in range(2)]
    ident16 = core.sb(T0 + 2560, P // 2).bitcast(BF16)
    mask16 = core.sb(T0 + 2560 + P // 2, 3 * P // 2).bitcast(BF16)
    small = lambda s, c: core.col(GX0 + (s % 2) * 8 + c)
    masks_ready, scored, maxed, exped, normalised, turned, turned_copied, weighted, out_done, chain_s = core.sems(10)
    flat = core.ps[:, :, :].rearrange("p b n -> p (b n)")

    def keys(i):
        if i < 2:
            return [], 0
        b = i - 2
        ks = [t for t in (b - 1, b, b + 1) if 0 <= t < 4]
        return ks, (ks[0] - b + 1) * P

    def span(s):
        n = len(keys(steps[s][1])[0])
        o = (s % 2) * 1024
        return flat[:, o + 512 - n * P:o + 768], n

    with nc.Block() as block:
        @block.tensor
        def _(pe):
            def scores(s):
                h, i = steps[s]
                ks, m0 = keys(i)
                hh = slice((h % 2) * HD, (h % 2 + 1) * HD)
                q = tiles[h // 2][hh, i * P:(i + 1) * P]
                k = kdup[h // 4]
                if s >= 2:
                    pe.wait_ge(exped, s - 1)
                n = len(ks)
                if n:
                    lat = core.ps[:, (s % 2) * 2, 512 - n * P:512]
                    nc.tensor.matmul(lat, ident16, mask16[:, m0:m0 + n * P], start=True, stop=False)
                    nc.tensor.matmul(lat, q, k[hh, CTX + ks[0] * P:CTX + (ks[0] + n) * P], start=False, stop=True)
                nc.tensor.matmul(core.ps[:, (s % 2) * 2 + 1, 0:CTX], q, k[hh, 0:CTX], start=True,
                                 stop=True).then_inc(scored, 1)

            def turn(s):
                pe.wait_ge(normalised, s + 1)
                if s:
                    pe.wait_ge(turned_copied, s)
                _, n = span(s)
                for j in range(n + 2):
                    mm = nc.tensor.transpose(flat[:, 2048 + j * P:2048 + (j + 1) * P],
                                             pr[s % 2][:, j * P:(j + 1) * P], core.ident())
                mm.then_inc(turned, 1)

            def weigh(s):
                h, i = steps[s]
                ks, _ = keys(i)
                vt = [2 + k for k in ks] + [0, 1]
                kv = h // 4
                pe.wait_ge(turned_copied, s + 1)
                if s >= 2:
                    pe.wait_ge(out_done, s - 1)
                o = core.ps[(h % 2) * HD:(h % 2 + 1) * HD, 6 + s % 2, 0:P]
                for j, t in enumerate(vt):
                    mm = nc.tensor.matmul(o, vtok[:, t * P + kv * HD:t * P + (kv + 1) * HD],
                                          pt[s % 2][:, j * P:(j + 1) * P], start=(j == 0), stop=(j == len(vt) - 1))
                mm.then_inc(weighted, 1)

            pe.wait_ge(masks_ready, 2)
            scores(0)
            for s in range(N):
                if s + 1 < N:
                    scores(s + 1)
                if s:
                    weigh(s - 1)
                turn(s)
            weigh(N - 1)

        @block.gpsimd
        def _(pool):
            nc.gpsimd.tensor_copy(ident16, core.ident()).then_inc(masks_ready, 1)
            nc.gpsimd.tensor_copy(mask16, wmask).then_inc(masks_ready, 1)

        @block.scalar
        def _(act):
            def exps(s):
                h, i = steps[s]
                src, n = span(s)
                act.wait_ge(maxed, s + 1)
                if s >= 2:
                    act.wait_ge(turned, s - 1)
                nc.scalar.activation(small(s, 3), core.col(SINK0 + h), ACT.Exp, bias=small(s, 1), scale=1.0)
                nc.scalar.activation(pr[s % 2][:, 0:(n + 2) * P], src, ACT.Exp, bias=small(s, 1), scale=HD ** -0.5,
                                     accum_out=small(s, 2)).then_inc(exped, 1)

            def copy(s):
                _, n = span(s)
                act.wait_ge(turned, s + 1)
                if s >= 2:
                    act.wait_ge(weighted, s - 1)
                nc.scalar.activation(pt[s % 2][:, 0:(n + 2) * P], flat[:, 2048:2048 + (n + 2) * P],
                                     ACT.Copy).then_inc(turned_copied, 1)
            exps(0)
            for s in range(N):
                if s + 1 < N:
                    exps(s + 1)
                copy(s)

        @block.vector
        def _(dve):
            chain = Chain(dve, chain_s)

            def top(s):
                h, i = steps[s]
                src, n = span(s)
                dve.wait_ge(scored, s + 1)
                if s >= 2:
                    dve.wait_ge(normalised, s - 1)
                chain(nc.vector.reduce_max(small(s, 0), src, AXX))
                chain.wait()
                nc.vector.tensor_scalar(small(s, 1), small(s, 0), -HD ** -0.5, core.col(SINK0 + 8 + h), ALU.mult,
                                        ALU.min).then_inc(maxed, 1)

            def normalise(s):
                _, n = span(s)
                dve.wait_ge(exped, s + 1)
                chain(nc.vector.tensor_tensor(small(s, 4), small(s, 2), small(s, 3), ALU.add))
                chain.wait()
                chain(nc.vector.reciprocal(small(s, 5), small(s, 4)))
                chain.wait()
                p = pr[s % 2][:, 0:(n + 2) * P]
                nc.vector.tensor_scalar(p, p, small(s, 5), None, ALU.mult).then_inc(normalised, 1)

            def out(s):
                h, i = steps[s]
                hh = slice((h % 2) * HD, (h % 2 + 1) * HD)
                dve.wait_ge(weighted, s + 1)
                nc.vector.tensor_copy(tiles[h // 2][hh, i * P:(i + 1) * P],
                                      core.ps[hh, 6 + s % 2, 0:P]).then_inc(out_done, 1)
            top(0)
            for s in range(N):
                normalise(s)
                if s + 1 < N:
                    top(s + 1)
                if s:
                    out(s - 1)
            out(N - 1)


def gla_stage(core, nc, name):
    NCH = T // CH
    orders = [list(range(NCH)), list(range(CTX // CH - 1, -1, -1)) + list(range(NCH - 1, CTX // CH - 1, -1))]
    b = lambda n: core.sb(T0 + n * T, T)
    F, KK, CU = b(0), b(1), b(2)
    QE, KE, QS, KDC = [b(3), b(4)], [b(5), b(6)], [b(7), b(8)], [b(9), b(10)]
    SCAN = b(11)
    o = TW0
    S = core.sb(o, NCH * P); o += NCH * P
    V = [core.sb(o, T), core.sb(o + T, T)]; o += 2 * T
    KDT = core.sb(o, T); o += T
    SM = [core.sb(o + d * T, T) for d in range(2)]; o += 2 * T
    TRI = [core.sb(o + d * P, P) for d in range(2)]; o += 2 * P
    DEC = [core.sb(o + d * 16, NCH) for d in range(2)]; o += 32
    VB = core.sb(T0 + 12 * T, 2 * T)
    assert o <= C0 and T0 + 14 * T <= TW0
    (tables_in, gates_done, v_turned, v_done, f_done, k_done, lf_done, cum_done, e_done, prod_done, scored, masked,
     kd_turned, kd_copied, states_in, states_done, outs_done, out_copied, vb_done, chain_s) = core.sems(20)
    runs = [(h, d) for h in range(4) for d in range(2)]
    flat = core.ps[:, :, :].rearrange("p b n -> p (b n)")
    ch3 = lambda ap: ap.rearrange("p (c t) -> p c t", t=CH)
    at_ref = [CH // 2, CH - 1 - CH // 2]
    at_end = [CH - 1, 0]

    with nc.Block() as block:
        @block.sync
        def _(sp):
            sp.dma_start(SCAN, core.const("scan")).then_inc(tables_in, 16)
            sp.dma_start(TRI[0], core.const("tri_fw")).then_inc(tables_in, 16)
            sp.dma_start(TRI[1], core.const("tri_bw")).then_inc(tables_in, 16)

        @block.scalar
        def _(act):
            nc.scalar.activation(core.sb(U0 + 10 * T, 8 * T), core.sb(U0 + 10 * T, 8 * T), ACT.Sigmoid).then_inc(gates_done, 1)
            nc.scalar.activation(core.sb(U0 + 6 * T, 4 * T), core.sb(U0 + 6 * T, 4 * T), ACT.Silu)
            nc.scalar.activation(core.sb(U0 + 22 * T, 4 * T), core.sb(U0 + 22 * T, 4 * T), ACT.Silu).then_inc(gates_done, 1)
            for r, (h, d) in enumerate(runs):
                act.wait_ge(f_done, r + 1)
                if r:
                    act.wait_ge(prod_done, 4 * r)
                nc.scalar.activation(KK, F, ACT.Identity, bias=core.col(ONE), scale=-1.0)
                nc.scalar.activation(F, F, ACT.Ln).then_inc(lf_done, 1)
                act.wait_ge(cum_done, r + 1)
                if r >= 2:
                    act.wait_ge(outs_done, 2 * (r - 1))
                nc.scalar.activation(DEC[d], ch3(CU)[:, :, at_end[d]], ACT.Exp)
                nc.scalar.activation(QS[r % 2], CU, ACT.Exp).then_inc(e_done, 1)
                act.wait_ge(cum_done, r + 1)
                act.wait_ge(k_done, 2 * r + 2)
                nc.scalar.activation(KE[r % 2], QE[r % 2], ACT.Exp, scale=-1.0).then_inc(e_done, 1)
                act.wait_ge(e_done, 4 * r + 2)
                nc.scalar.activation(QE[r % 2], QE[r % 2], ACT.Exp).then_inc(e_done, 1)
                nc.scalar.activation(KDC[r % 2], KDC[r % 2], ACT.Exp).then_inc(e_done, 1)

        @block.gpsimd
        def _(pool):
            for r, (h, d) in enumerate(runs):
                pool.wait_ge(cum_done, r + 1)
                if r >= 2:
                    pool.wait_ge(outs_done, 2 * (r - 1))
                cu = ch3(CU)
                ref = cu[:, :, at_ref[d]:at_ref[d] + 1].broadcast_to([P, NCH, CH])
                end = cu[:, :, at_end[d]:at_end[d] + 1].broadcast_to([P, NCH, CH])
                nc.gpsimd.tensor_tensor(ch3(QE[r % 2]), cu, ref, ALU.subtract).then_inc(k_done, 1)
                nc.gpsimd.tensor_tensor(ch3(KDC[r % 2]), end, cu, ALU.subtract).then_inc(k_done, 1)
                if d == 0:
                    pool.wait_ge(v_done, h + 1)
                    if h:
                        pool.wait_ge(states_in, 2 * h)
                    for e in range(2):
                        ins = nc.gpsimd.tensor_scalar(VB.rearrange("p (c e d) -> p c e d", e=2, d=P)[:, :, e],
                                                      V[h % 2].rearrange("p (c d) -> p c d", d=P),
                                                      core.col(BD0 + e * (P - 1)), None, ALU.mult)
                    ins.then_inc(vb_done, 1)

        @block.vector
        def _(dve):
            chain = Chain(dve, chain_s)
            chain(nc.vector.memset(SM[0], 0.0))
            chain(nc.vector.memset(SM[1], 0.0))
            dve.wait_ge(tables_in, 48)
            dve.wait_ge(gates_done, 1)
            rev = lambda ap: bass.AP(tensor=ap.tensor, offset=ap.offset + T - 1, ap=[ap.ap[0], [-1, T]])

            def gates(r):
                h, d = runs[r]
                if r:
                    dve.wait_ge(cum_done, r)
                nc.vector.tensor_scalar(F, core.u(10 + 4 * d + h), core.col(LBV0 + 4 + h), core.col(LBV0 + h),
                                        ALU.mult, ALU.add).then_inc(f_done, 1)
                dve.wait_ge(lf_done, r + 1)
                if r:
                    dve.wait_ge(e_done, 4 * r)
                    dve.wait_ge(k_done, 2 * r)
                if d == 0:
                    nc.vector.tensor_tensor_scan(CU, SCAN, F, 0.0, ALU.mult, ALU.add).then_inc(cum_done, 1)
                else:
                    nc.vector.tensor_tensor_scan(rev(CU), SCAN, rev(F), 0.0, ALU.mult, ALU.add).then_inc(cum_done, 1)

            def products(r):
                h, d = runs[r]
                dve.wait_ge(gates_done, 2)
                q = core.u(6 + h)
                for n, (e, x, buf) in enumerate(((1, q, QS), (2, KK, KE), (3, q, QE), (4, KK, KDC))):
                    dve.wait_ge(e_done, 4 * r + e)
                    nc.vector.tensor_tensor(buf[r % 2], buf[r % 2], x, ALU.mult).then_inc(prod_done, 1)

            def values(h):
                dve.wait_ge(v_turned, h + 1)
                nc.vector.tensor_copy(V[h % 2], flat[:, 0:T]).then_inc(v_done, 1)

            def rest(r):
                h, d = runs[r]
                dve.wait_ge(scored, r + 1)
                if r >= 2:
                    dve.wait_ge(outs_done, 2 * (r - 1))
                for e in range(2):
                    part = slice(e * CH, (e + 1) * CH)
                    mask = TRI[d][part, e * CH:(e + 1) * CH].bitcast(U32).rearrange("p (o t) -> p o t", o=1)
                    ins = nc.vector.copy_predicated(
                        SM[d][part].rearrange("p (c e t) -> p c e t", e=2, t=CH)[:, :, e], mask.broadcast_to([CH, 6, CH]),
                        core.ps[part, 0, 0:384].rearrange("p (c t) -> p c t", t=CH))
                ins.then_inc(masked, 1)
                dve.wait_ge(kd_turned, r + 1)
                if r:
                    dve.wait_ge(states_in, r)
                nc.vector.tensor_copy(KDT, flat[:, 0:T]).then_inc(kd_copied, 1)
                dve.wait_ge(states_in, r + 1)
                if r:
                    dve.wait_ge(outs_done, 2 * r)
                order = orders[d]
                for n in range(1, NCH):
                    c = order[n - 1]
                    ds = flat[:, 1536 + c * P:1536 + (c + 1) * P]
                    if n == 1:
                        ins = nc.vector.tensor_copy(S[:, P:2 * P], ds)
                    else:
                        dve.wait_ge(states_done, r * (NCH - 1) + n - 1)
                        ins = nc.vector.scalar_tensor_tensor(out=S[:, n * P:(n + 1) * P], in0=S[:, (n - 1) * P:n * P],
                                                             scalar=DEC[d][:, c:c + 1], in1=ds, op0=ALU.mult,
                                                             op1=ALU.add)
                    ins.then_inc(states_done, 1)
                if d == 1:
                    dve.wait_ge(outs_done, 2 * r + 2)
                    nc.vector.tensor_copy(core.u(18 + h), flat[:, 3072:3072 + T]).then_inc(out_copied, 1)

            chain.wait()
            values(0)
            gates(0)
            products(0)
            for r in range(8):
                if r + 1 < 8:
                    gates(r + 1)
                    products(r + 1)
                rest(r)
                if r % 2 == 0 and r // 2 + 1 < 4:
                    values(r // 2 + 1)

        @block.tensor
        def _(pe):
            def values(h):
                if h:
                    pe.wait_ge(kd_copied, 2 * h - 1)
                for t in range(6):
                    mm = nc.tensor.transpose(flat[:, t * P:(t + 1) * P],
                                             core.u(18 + h)[:, t * P:(t + 1) * P], core.ident())
                mm.then_inc(v_turned, 1)

            values(0)
            for r, (h, d) in enumerate(runs):
                v = V[h % 2]
                pe.wait_ge(prod_done, 4 * r + 4)
                if r:
                    pe.wait_ge(kd_copied, r)
                pe.wait_ge(v_done, min(h + 1 + r % 2, 4))
                for c in range(NCH):
                    for e in range(2):
                        s0 = c * CH + e * CH // 2
                        a, w = ((CH // 2, CH // 2) if (d, e) == (0, 1) else (0, CH // 2) if (d, e) == (1, 0) else (0, CH))
                        t0 = c * CH + a
                        p0 = (c % 2) * CH + e * CH // 2
                        o0 = (c // 2) * CH + a
                        mm = nc.tensor.matmul(core.ps[p0:p0 + CH // 2, 0, o0:o0 + w], KE[r % 2][:, s0:s0 + CH // 2],
                                              QE[r % 2][:, t0:t0 + w], start=True, stop=True)
                mm.then_inc(scored, 1)
                pe.wait_ge(masked, r + 1)
                for t in range(6):
                    mm = nc.tensor.transpose(flat[:, t * P:(t + 1) * P], KDC[r % 2][:, t * P:(t + 1) * P],
                                             core.ident())
                mm.then_inc(kd_turned, 1)
                pe.wait_ge(kd_copied, r + 1)
                if r:
                    pe.wait_ge(states_done, r * (NCH - 1))
                pe.wait_ge(vb_done, h + 1)
                for c in range(6):
                    mm = nc.tensor.matmul(flat[:, 1536 + 2 * c * P:1536 + 2 * (c + 1) * P], KDT[:, c * P:(c + 1) * P],
                                          VB[:, 2 * c * P:2 * (c + 1) * P], start=True, stop=True)
                mm.then_inc(states_in, 1)
                if d == 0 and h:
                    pe.wait_ge(out_copied, h)
                for c in range(6):
                    cc = slice(c * P, (c + 1) * P)
                    mm = nc.tensor.matmul(flat[:, 3072 + c * P:3072 + (c + 1) * P], v[:, cc], SM[d][:, cc],
                                          start=(d == 0 and c in (0, 4)), stop=False, skip_group_check=True)
                mm.then_inc(outs_done, 1)
                for n in range(1, NCH):
                    c = orders[d][n]
                    pe.wait_ge(states_done, r * (NCH - 1) + n)
                    mm = nc.tensor.matmul(flat[:, 3072 + c * CH:3072 + (c + 1) * CH], S[:, n * P:(n + 1) * P],
                                          QS[r % 2][:, c * CH:(c + 1) * CH], start=False, stop=(d == 1),
                                          skip_group_check=True)
                mm.then_inc(outs_done, 1)
                if r % 2 == 0 and h + 1 < 4:
                    values(h + 1)


def even_mixer(core, nc, a):
    ctx_seg, lat_seg = (0, CTX), (CTX, SEQ)
    both = [lat_seg, ctx_seg]
    qk = [core.u(t) for t in range(5)]
    group_norm(core, nc, "qk", [[(qk[t], qk[t], PV0 + ROW_QKG + (t == 4), None)] for t in range(5)],
               core.sb(BD0, P), HD, both, EPS6)
    o = TW0
    cos, sin = core.sb(o, SEQ), core.sb(o + SEQ, SEQ); o += 2 * SEQ
    rot, dup0, dup1 = core.sb(o, P), core.sb(o + P, P), core.sb(o + 2 * P, P); o += 3 * P
    wmask = core.sb(o, 3 * P); o += 3 * P
    kdup = [core.sb(o, T), core.sb(o + T, T)]; o += 2 * T
    vtok = core.sb(o, T); o += T
    rope_stage(core, nc, qk, [(cos, "cosA"), (sin, "sinA"), (rot, "rot"), (dup0, "dup0"), (dup1, "dup1"),
                              (wmask, "wmask")], core.u(5), kdup, vtok, cos, sin, rot, [dup0, dup1])
    window_stage(core, nc, qk[:4], kdup, vtok, wmask)
    gla_stage(core, nc, "gla")
    group_norm(core, nc, "gla_norm", [[(core.u(18 + h), core.u(18 + h), PV0 + ROW_OG, core.u(22 + h))] for h in range(4)],
               core.sb(ONES0, P), P, both, EPS6)


def retention_stage(core, nc, h, out0):
    o = TW0
    V = core.sb(o, 6 * ODD_DV); o += 6 * ODD_DV
    ST = core.sb(o, 6 * SEQ); o += 6 * SEQ
    W = core.sb(o, 12 * P); o += 12 * P
    tmp = [core.sb(o + n * SEQ, SEQ) for n in range(4)]; o += 4 * SEQ
    cos, sin = core.sb(o, SEQ), core.sb(o + SEQ, SEQ); o += 2 * SEQ
    assert o <= C0
    tables_in, mults, mults_p, roped, v_turned, v_copied, scored, weighted, summed = core.sems(9)
    n_tables = 3
    with nc.Block() as block:
        @block.sync
        def _(sp):
            sp.dma_start(cos, core.const("cosR")).then_inc(tables_in, 16)
            sp.dma_start(sin, core.const("sinR")).then_inc(tables_in, 16)
            sp.dma_start(W, core.const(f"ret{h}")).then_inc(tables_in, 16)

        def rope(eng, x0, x1, t0, t1, done_sem):
            eng.wait_ge(tables_in, 16 * n_tables)
            eng.tensor_tensor(t0, x1, sin, ALU.mult).then_inc(done_sem, 1)
            eng.tensor_tensor(t1, x0, sin, ALU.mult).then_inc(done_sem, 1)
            eng.wait_ge(done_sem, 2)
            eng.tensor_tensor(x0, x0, cos, ALU.mult).then_inc(done_sem, 1)
            eng.tensor_tensor(x1, x1, cos, ALU.mult).then_inc(done_sem, 1)
            eng.wait_ge(done_sem, 4)
            eng.tensor_tensor(x0, x0, t0, ALU.subtract).then_inc(roped, 1)
            eng.tensor_tensor(x1, x1, t1, ALU.add).then_inc(roped, 1)

        @block.gpsimd
        def _(pool):
            rope(nc.gpsimd, core.u(0)[:, LAT], core.u(1)[:, LAT], tmp[0], tmp[1], mults_p)

        @block.vector
        def _(dve):
            rope(nc.vector, core.u(2)[:, LAT], core.u(3)[:, LAT], tmp[2], tmp[3], mults)
            for j in range(6):
                dve.wait_ge(scored, j + 1)
                w0 = 3 * P - (j - 2) * P if j >= 2 else 7 * P + P - j * P
                nc.vector.tensor_tensor(ST[:, j * SEQ:(j + 1) * SEQ], core.ps[:, 6 + j % 2, :], W[:, w0:w0 + SEQ],
                                        ALU.mult).then_inc(weighted, 1)
            for e in range(4):
                dve.wait_ge(summed, e + 1)
                nc.vector.tensor_copy(core.sb(out0 + e * SEQ, SEQ), core.ps[:, e, :])

        @block.tensor
        def _(pe):
            for t in range(6):
                for e in range(4):
                    mm = nc.tensor.transpose(core.ps[:, t, e * P:(e + 1) * P], core.u(4 + e)[:, t * P:(t + 1) * P],
                                             core.ident())
                mm.then_inc(v_turned, 1)
            pe.wait_ge(roped, 4)
            for j in range(6):
                if j >= 2:
                    pe.wait_ge(weighted, j - 1)
                for k in range(2):
                    mm = nc.tensor.matmul(core.ps[:, 6 + j % 2, :], core.u(2 + k)[:, j * P:(j + 1) * P],
                                          core.u(k)[:, LAT], start=(k == 0), stop=(k == 1))
                mm.then_inc(scored, 1)
            pe.wait_ge(v_copied, 6)
            for e in range(4):
                for j in range(6):
                    if e == 0:
                        pe.wait_ge(weighted, j + 1)
                    mm = nc.tensor.matmul(core.ps[:, e, :], V[:, j * ODD_DV + e * P:j * ODD_DV + (e + 1) * P],
                                          ST[:, j * SEQ:(j + 1) * SEQ], start=(j == 0), stop=(j == 5))
                mm.then_inc(summed, 1)

        @block.scalar
        def _(act):
            for t in range(6):
                act.wait_ge(v_turned, t + 1)
                nc.scalar.activation(V[:, t * ODD_DV:(t + 1) * ODD_DV], core.ps[:, t, :], ACT.Copy).then_inc(v_copied, 1)
            for e in range(4):
                nc.scalar.activation(core.u(8 + e)[:, LAT], core.u(8 + e)[:, LAT], ACT.Silu)


def odd_mixer(core, nc, a, both, lat):
    OUT0 = U0 + 12 * T
    K0, V0, G0 = ODD_H * ODD_DK, 2 * ODD_H * ODD_DK, 2 * ODD_H * ODD_DK + ODD_H * ODD_DV
    view = lambda n: core.sb(OUT0 + n * SEQ - CTX, T)
    m = M0 + 96
    projections = []
    for h in range(ODD_H):
        kv = [K0 + h * ODD_DK, V0 + h * ODD_DV, V0 + h * ODD_DV + GW]
        qg = [h * ODD_DK, G0 + h * ODD_DV, G0 + h * ODD_DV + GW]
        tiles_kv, tiles_qg = [2, 4, 6], [0, 8, 10]
        place = lambda tiles: lambda g, f: U0 + (tiles[g] + f) * T
        projections.append((
            Dense(core, a["odd_w_in"][0], core.h, KD, 3, (lambda c: lambda ib, j: c[ib + j])(kv), both,
                  Copy(core, nc, U0, both, place(tiles_kv))),
            Dense(core, a["odd_w_in"][0], core.h, KD, 3, (lambda c: lambda ib, j: c[ib + j])(qg), lat,
                  Copy(core, nc, U0, lat, place(tiles_qg)))))
    out = Dense(core, a["odd_w_out"][0], view, ODD_H * ODD_DV // P, 4, lambda ib, j: ib * GW + j * GW, lat,
                Residual(core, nc, m + 2 * 16, lat), split=True)
    for h in range(ODD_H):
        kv, qg = projections[h]
        kv.run(f"kv{h}", after=qg)
        qg.run(f"qg{h}")
        retention_stage(core, nc, h, OUT0 + 4 * h * SEQ)
        ov = [view(4 * h + e) for e in range(4)]
        group_norm(core, nc, f"ret_norm{h}", [[(ov[e], ov[e], ONE, core.u(8 + e)) for e in range(4)]],
                   core.sb(ONES0, P), ODD_DV, lat, EPS6, scratch=TW0)
    out.run("odd_out")


def u2(core, t):
    return core.sb(U0 + t * SEQ, SEQ)


def lat_view(core, t):
    return core.sb(U0 + t * SEQ - CTX, T)


def taps(n):
    return [n // 2] + [t for t in range(n) if t != n // 2]


def conv_stage(core, nc, l):
    NB = 6
    diag = [core.sb(S0 + b * P, P) for b in range(NB)]
    hb = [core.sb(S0 + NB * P + q * SEQ, SEQ) for q in range(2)]
    cv = [core.sb(S0 + NB * P + (2 + q) * SEQ, SEQ) for q in range(2)]
    sq = [core.sb(S0 + NB * P + (4 + q) * SEQ, SEQ) for q in range(2)]
    rstd = core.sb(S0 + NB * P + 6 * SEQ, SEQ)
    jobs = [(core_q, t) for core_q in range(2) for t in taps(CONV_K)]
    work = [("dw", q, t) for q, t in jobs] + [("sc", q, t) for q in range(9) for t in taps(3)]
    gated, glu, diag_made, tap_done, conv_done, biased, mean_done, centred, sq_done, var_done, std_done, normed, chain_s = \
        core.sems(13)
    n_sc = 9
    with nc.Block() as block:
        @block.scalar
        def _(act):
            for q in range(2):
                nc.scalar.activation(u2(core, 2 + q), u2(core, 2 + q), ACT.Sigmoid).then_inc(gated, 1)
            for q in range(2):
                act.wait_ge(conv_done, q + 1)
                nc.scalar.activation(cv[q], core.ps[:, q, :], ACT.Identity, bias=core.col(PV0 + ROW_DWB + 2 * l + q),
                                     scale=1.0).then_inc(biased, 1)
            for q in range(2):
                act.wait_ge(centred, q + 1)
                nc.scalar.activation(sq[q], cv[q], ACT.Square).then_inc(sq_done, 1)
            for q in range(n_sc):
                act.wait_ge(conv_done, 3 + q)
                nc.scalar.activation(u2(core, 13 + q), core.ps[:, 4 + q % 4, :], ACT.Silu).then_inc(biased, 1)
            act.wait_ge(var_done, 1)
            nc.scalar.activation(rstd, core.ps[:, 3, :], ACT.Sqrt, bias=core.col(EPS5),
                                 scale=1.0 / CONV_CH).then_inc(std_done, 1)
            for q in range(2):
                act.wait_ge(normed, q + 1)
                nc.scalar.activation(u2(core, q), u2(core, q), ACT.Silu, bias=core.col(PV0 + ROW_LNB + 2 * l + q),
                                     scale=1.0)
            for q in range(3):
                nc.scalar.activation(u2(core, 22 + q), u2(core, 22 + q), ACT.Silu)

        @block.gpsimd
        def _(pool):
            for n, (kind, q, t) in enumerate(work):
                if n >= NB:
                    pool.wait_ge(tap_done, n - NB + 1)
                c = PV0 + (ROW_DW + (l * CONV_K + t) * 2 + q if kind == "dw" else ROW_SC + (l * 3 + t) * 9 + q)
                nc.gpsimd.tensor_scalar(diag[n % NB], core.ident(), core.col(c), None, ALU.mult).then_inc(diag_made, 1)

        @block.tensor
        def _(pe):
            for n, (kind, q, t) in enumerate(work):
                K = CONV_K if kind == "dw" else 3
                src = hb[q] if kind == "dw" else u2(core, 13 + q)
                bank = q if kind == "dw" else 4 + q % 4
                off = t - K // 2
                if t == K // 2:
                    if kind == "dw":
                        pe.wait_ge(glu, q + 1)
                    elif q >= 4:
                        pe.wait_ge(biased, 2 + q - 3)
                    if kind == "sc" and q == 0:
                        for f, (sem, src2, bank2) in enumerate(((biased, cv, 2),)):
                            pe.wait_ge(sem, 2)
                            for k in range(2):
                                mm = nc.tensor.matmul(core.ps[:, bank2, :], core.sb(ONES0, P), src2[k], start=(k == 0),
                                                      stop=(k == 1))
                            mm.then_inc(mean_done, 1)
                    if kind == "sc" and q == 6:
                        pe.wait_ge(sq_done, 2)
                        for k in range(2):
                            mm = nc.tensor.matmul(core.ps[:, 3, :], core.sb(ONES0, P), sq[k], start=(k == 0), stop=(k == 1))
                        mm.then_inc(var_done, 1)
                a, b = max(0, -off), SEQ - max(0, off)
                pe.wait_ge(diag_made, n + 1)
                mm = nc.tensor.matmul(core.ps[:, bank, a:b], diag[n % NB], src[:, a + off:b + off],
                                      start=(t == K // 2), stop=(t == K - 1), skip_group_check=True)
                mm.then_inc(tap_done, 1)
                if t == K - 1:
                    pe.wait_ge(tap_done, n + 1)
                    pe.sem_inc(conv_done, 1)

        @block.vector
        def _(dve):
            for q in range(2):
                dve.wait_ge(gated, q + 1)
                nc.vector.tensor_tensor(hb[q], u2(core, q), u2(core, 2 + q), ALU.mult).then_inc(glu, 1)
            dve.wait_ge(mean_done, 1)
            for q in range(2):
                nc.vector.scalar_tensor_tensor(out=cv[q], in0=core.ps[:, 2, :], scalar=-1.0 / CONV_CH, in1=cv[q],
                                               op0=ALU.mult, op1=ALU.add).then_inc(centred, 1)
            dve.wait_ge(std_done, 1)
            nc.vector.reciprocal(rstd, rstd).then_inc(chain_s, 1)
            dve.wait_ge(chain_s, 1)
            for q in range(2):
                nc.vector.scalar_tensor_tensor(out=u2(core, q), in0=cv[q], scalar=core.col(PV0 + ROW_LNW + 2 * l + q),
                                               in1=rstd, op0=ALU.mult, op1=ALU.mult).then_inc(normed, 1)


def diff_stage(core, nc, a, l):
    DD = 32
    scale = DD ** -0.5
    lam0 = 0.8 - 0.6 * math.exp(-0.3 * l)
    slopes = [2.0 ** -2, 2.0 ** -4, 2.0 ** -6, 2.0 ** -8, 2.0 ** -1, 2.0 ** -3]
    o = S0
    dist = core.sb(o, 7 * P); o += 7 * P
    dist16 = core.sb(o, 7 * P // 2).bitcast(F16); o += 7 * P // 2
    si = [core.sb(o + n * P // 2, P // 2).bitcast(F16) for n in range(2)]; o += P
    pr = [core.sb(o + n * 2 * SEQ, 2 * SEQ) for n in range(2)]; o += 4 * SEQ
    at = [core.sb(o + n * SEQ, SEQ) for n in range(2)]; o += 2 * SEQ
    both = [core.sb(o + n * SEQ, SEQ) for n in range(2)]; o += 2 * SEQ
    vt = core.sb(o, 4 * DIFF_W); o += 4 * DIFF_W
    lamv = core.sb(o, 4 * DD); o += 4 * DD
    lamp = core.sb(o, 2 * DD); o += 2 * DD
    sc = lambda s, c, w=2: core.sb(GX0 + (s % 2) * 8 + c, w)
    steps = [(h, i) for h in range(6) for i in range(4)]
    N = len(steps)
    (loads_in, lam_s, v_turned, v_copied, slope_made, q_scaled, scored, maxed, exped, subtracted, turned,
     turned_copied, weighted, out_done, chain_s) = core.sems(15)
    with nc.Block() as block:
        @block.sync
        def _(sp):
            sp.dma_start(dist, core.const("dist")).then_inc(loads_in, 16)
            for n, name in enumerate(("diff_lambda_q1_2", "diff_lambda_k1_2", "diff_lambda_q2_2", "diff_lambda_k2_2")):
                sp.dma_start(lamv[:, n * DD:(n + 1) * DD], a[name][l].partition_broadcast(P)).then_inc(loads_in, 16)

        @block.gpsimd
        def _(pool):
            for t in range(3):
                nc.gpsimd.tensor_scalar(u2(core, 4 + t), u2(core, 4 + t), scale, None, ALU.mult).then_inc(q_scaled, 1)
            pool.wait_ge(loads_in, 80)
            nc.gpsimd.tensor_copy(dist16, dist).then_inc(q_scaled, 1)
            for h in range(6):
                if h >= 2:
                    pool.wait_ge(scored, 4 * (h - 1))
                nc.gpsimd.tensor_scalar(si[h % 2], core.ident(), -slopes[h], None, ALU.mult).then_inc(slope_made, 1)

        @block.tensor
        def _(pe):
            for b in range(3):
                for q in range(4):
                    mm = nc.tensor.transpose(core.ps[:, 4 + b, q * P:(q + 1) * P],
                                             u2(core, 10 + b)[:, q * P:(q + 1) * P], core.ident())
            mm.then_inc(v_turned, 1)
            pe.wait_ge(q_scaled, 4)

            def scores(s):
                h, i = steps[s]
                if s >= 2:
                    pe.wait_ge(exped, 2 * (s - 1))
                pe.wait_ge(slope_made, h + 1)
                for m in range(2):
                    mp = 2 * h + m
                    pp = slice((mp % 4) * DD, (mp % 4 + 1) * DD)
                    bank = core.ps[:, (s % 2) * 2 + m, :]
                    nc.tensor.matmul(bank, si[h % 2], dist16[:, 3 * P - i * P:3 * P - i * P + SEQ], start=True, stop=False)
                    mm = nc.tensor.matmul(bank, u2(core, 4 + mp // 4)[pp, i * P:(i + 1) * P],
                                          u2(core, 7 + mp // 4)[pp, :], start=False, stop=True)
                mm.then_inc(scored, 1)

            def turn(s):
                pe.wait_ge(subtracted, s + 1)
                if s >= 2:
                    pe.wait_ge(turned_copied, s - 1)
                if s == 0:
                    pe.wait_ge(v_copied, 1)
                for j in range(4):
                    mm = nc.tensor.transpose(core.ps[:, 4 + s % 2, j * P:(j + 1) * P],
                                             both[s % 2][:, j * P:(j + 1) * P], core.ident())
                mm.then_inc(turned, 1)

            def weigh(s):
                h, i = steps[s]
                pe.wait_ge(turned_copied, s + 1)
                if s >= 2:
                    pe.wait_ge(out_done, s - 1)
                oo = core.ps[(h % 2) * HD:(h % 2 + 1) * HD, 6 + s % 2, 0:P]
                for j in range(4):
                    mm = nc.tensor.matmul(oo, vt[:, j * DIFF_W + h * HD:j * DIFF_W + (h + 1) * HD],
                                          at[s % 2][:, j * P:(j + 1) * P], start=(j == 0), stop=(j == 3))
                mm.then_inc(weighted, 1)
            scores(0)
            for s in range(N):
                if s + 1 < N:
                    scores(s + 1)
                if s:
                    weigh(s - 1)
                turn(s)
            weigh(N - 1)

        @block.scalar
        def _(act):
            act.wait_ge(lam_s, 1)
            nc.scalar.activation(core.sb(GX0 + 32, 2), core.sb(GX0 + 32, 2), ACT.Exp).then_inc(lam_s, 1)

            def exps(s):
                act.wait_ge(maxed, s + 1)
                if s >= 2:
                    act.wait_ge(subtracted, s - 1)
                for m in range(2):
                    nc.scalar.activation(pr[s % 2][:, m * SEQ:(m + 1) * SEQ], core.ps[:, (s % 2) * 2 + m, :], ACT.Exp,
                                         bias=sc(s, 2 + m, 1), scale=1.0, accum_out=sc(s, 4 + m, 1)).then_inc(exped, 1)

            def copy(s):
                act.wait_ge(turned, s + 1)
                if s >= 2:
                    act.wait_ge(weighted, s - 1)
                nc.scalar.activation(at[s % 2], core.ps[:, 4 + s % 2, :], ACT.Copy).then_inc(turned_copied, 1)
            exps(0)
            for s in range(N):
                if s + 1 < N:
                    exps(s + 1)
                copy(s)

        @block.vector
        def _(dve):
            chain = Chain(dve, chain_s)
            dve.wait_ge(v_turned, 1)
            for b in range(3):
                ins = nc.vector.tensor_copy(vt.rearrange("p (q c) -> p q c", c=DIFF_W)[:, :, b * P:(b + 1) * P],
                                            core.ps[:, 4 + b, :].rearrange("p (q c) -> p q c", c=P))
            ins.then_inc(v_copied, 1)
            dve.wait_ge(loads_in, 80)
            l4 = lamv.rearrange("p (n d) -> p n d", d=DD)
            for n in range(2):
                chain(nc.vector.tensor_tensor(lamp[:, n * DD:(n + 1) * DD], l4[:, 2 * n], l4[:, 2 * n + 1], ALU.mult))
            chain.wait()
            nc.vector.reduce_sum(core.sb(GX0 + 32, 2), lamp.rearrange("p (n d) -> p n d", d=DD), AXX).then_inc(lam_s, 1)
            dve.wait_ge(lam_s, 2)
            chain(nc.vector.tensor_tensor(core.col(NLAM), core.col(GX0 + 33), core.col(GX0 + 32), ALU.subtract))
            chain.wait()
            chain(nc.vector.tensor_scalar(core.col(NLAM), core.col(NLAM), -lam0, None, ALU.add))
            chain(nc.vector.tensor_scalar(core.col(SUBG), core.col(PV0 + ROW_SUB + l), 1.0 - lam0, None, ALU.mult))

            def top(s):
                dve.wait_ge(scored, s + 1)
                if s >= 2:
                    dve.wait_ge(subtracted, s - 1)
                chain(nc.vector.reduce_max(sc(s, 0), core.ps[:, (s % 2) * 2:(s % 2) * 2 + 2, :], AXX))
                chain.wait()
                nc.vector.tensor_scalar(sc(s, 2), sc(s, 0), -1.0, None, ALU.mult).then_inc(maxed, 1)

            def subtract(s):
                dve.wait_ge(exped, 2 * s + 2)
                chain(nc.vector.reciprocal(sc(s, 6), sc(s, 4)))
                chain.wait()
                chain(nc.vector.tensor_scalar(pr[s % 2][:, SEQ:], pr[s % 2][:, SEQ:], sc(s, 7, 1), core.col(NLAM),
                                              ALU.mult, ALU.mult))
                chain.wait()
                if s >= 2:
                    dve.wait_ge(turned, s - 1)
                nc.vector.scalar_tensor_tensor(out=both[s % 2], in0=pr[s % 2][:, 0:SEQ], scalar=sc(s, 6, 1),
                                               in1=pr[s % 2][:, SEQ:], op0=ALU.mult, op1=ALU.add
                                               ).then_inc(subtracted, 1)

            def out(s):
                h, i = steps[s]
                hh = slice((h % 2) * HD, (h % 2 + 1) * HD)
                dve.wait_ge(weighted, s + 1)
                nc.vector.tensor_copy(u2(core, 4 + h // 2)[hh, i * P:(i + 1) * P],
                                      core.ps[hh, 6 + s % 2, 0:P]).then_inc(out_done, 1)
            top(0)
            for s in range(N):
                subtract(s)
                if s + 1 < N:
                    top(s + 1)
                if s:
                    out(s - 1)
            out(N - 1)


class DeltaPlan:

    def __init__(self, core):
        o = S0

        def take(w):
            nonlocal o
            o += w
            return core.sb(o - w, w)
        self.kt, self.vt = take(4 * DELTA_W), take(4 * DELTA_W)
        self.cum = [take(P), take(P)]
        self.lev = [[take(P) for _ in range(7)] for _ in range(2)]
        self.beta, self.g, self.gsum, self.eg, self.ekd, self.gl, self.bge, self.z, self.r = [take(48) for _ in range(9)]
        self.dtb, self.al = take(12), take(12)
        self.run = []
        for _ in range(2):
            self.run.append({n: take(w) for n, w in (
                ("a", 512), ("x", 512), ("u", 512), ("pt", 512), ("bm", 512), ("at", 512), ("nw", 512), ("qg", 512),
                ("rv", 256), ("rw", 256), ("kd", 256), ("vn", 256), ("s", 256))})
        self.d = [take(512) for _ in range(2)]
        assert o <= C0


def delta_gates_stage(core, nc, a, l, pl):
    loads_in, turned, copied, betas, zs, lns, gs, sums, chain_s, chain_a = core.sems(10)
    v4 = lambda ap: ap.rearrange("p (c n) -> p c n", n=12)
    with nc.Block() as block:
        @block.sync
        def _(sp):
            for d, n in enumerate(("fw", "bw")):
                sp.dma_start(pl.cum[d], core.const("cum_" + n)).then_inc(loads_in, 16)
                for lv in range(7):
                    sp.dma_start(pl.lev[d][lv], core.const(f"lev_{n}{lv}")).then_inc(loads_in, 16)
            sp.dma_start(pl.dtb, a["delta_dt_bias_2"][l].rearrange("a b -> (a b)").partition_broadcast(P)).then_inc(loads_in, 16)
            sp.dma_start(pl.al, a["delta_A_log_2"][l].rearrange("a b -> (a b)").partition_broadcast(P)).then_inc(loads_in, 16)

        @block.tensor
        def _(pe):
            for c in range(4):
                mm = nc.tensor.transpose(core.ps[:, 6, c * 24:(c + 1) * 24], u2(core, DT)[0:24, c * P:(c + 1) * P],
                                         core.sb(IDENT0, 24, 24))
            mm.then_inc(turned, 1)
            for b in range(6):
                for c in range(4):
                    mm = nc.tensor.transpose(core.ps[:, b, c * P:(c + 1) * P], u2(core, 16 + b)[:, c * P:(c + 1) * P],
                                             core.ident())
                mm.then_inc(turned, 1)
            pe.wait_ge(gs, 1)
            pe.wait_ge(loads_in, 16 * 18)
            for d in range(2):
                nc.tensor.matmul(core.ps[:, 7, d * 24:(d + 1) * 24].rearrange("p (c n) -> p c n", n=6), pl.cum[d],
                                 v4(pl.g)[:, :, d * 6:(d + 1) * 6], start=(d == 0), stop=False, skip_group_check=True)
            nc.tensor.matmul(core.ps[:, 7, 48:96], core.sb(ONES0, P), pl.g, start=False, stop=True,
                             skip_group_check=True).then_inc(sums, 1)

        @block.vector
        def _(dve):
            chain = Chain(dve, chain_s)
            dve.wait_ge(loads_in, 16 * 18)
            dve.wait_ge(chain_a, 1)
            gate = core.ps[:, 6, 0:96].rearrange("p (c n) -> p c n", n=24)
            dtb = pl.dtb.rearrange("p (o n) -> p o n", o=1).broadcast_to([P, 4, 12])
            al = pl.al.rearrange("p (o n) -> p o n", o=1).broadcast_to([P, 4, 12])
            chain(nc.vector.tensor_tensor(v4(pl.z), gate[:, :, 12:24], dtb, ALU.add))
            chain.wait()
            chain(nc.vector.tensor_scalar(pl.r, pl.z, 0.0, None, ALU.max))
            chain.wait()
            nc.vector.scalar_tensor_tensor(out=pl.z, in0=pl.r, scalar=-2.0, in1=pl.z, op0=ALU.mult,
                                           op1=ALU.add).then_inc(zs, 1)
            dve.wait_ge(lns, 1)
            chain(nc.vector.tensor_tensor(pl.r, pl.r, pl.z, ALU.add))
            chain.wait()
            nc.vector.scalar_tensor_tensor(out=v4(pl.g), in0=v4(pl.r), scalar=-1.0, in1=al, op0=ALU.mult,
                                           op1=ALU.mult).then_inc(gs, 1)
            for b in range(6):
                dst = (pl.kt if b < 3 else pl.vt).rearrange("p (c n) -> p c n", n=DELTA_W)
                dve.wait_ge(turned, b + 2)
                nc.vector.tensor_copy(dst[:, :, (b % 3) * P:(b % 3 + 1) * P],
                                      core.ps[:, b, :].rearrange("p (c n) -> p c n", n=P))
            dve.wait_ge(sums, 1)
            for d in range(2):
                chain(nc.vector.tensor_copy(v4(pl.gsum)[:, :, d * 6:(d + 1) * 6],
                                            core.ps[:, 7, d * 24:(d + 1) * 24].rearrange("p (c n) -> p c n", n=6)))
            chain.wait()
            nc.vector.tensor_tensor(pl.ekd, core.ps[:, 7, 48:96], pl.gsum, ALU.subtract).then_inc(sums, 1)
            dve.wait_ge(chain_a, 2)
            nc.vector.tensor_tensor(pl.bge, pl.beta, pl.eg, ALU.mult)

        @block.scalar
        def _(act):
            act.wait_ge(turned, 1)
            nc.scalar.activation(v4(pl.beta), core.ps[:, 6, 0:96].rearrange("p (c n) -> p c n", n=24)[:, :, 0:12],
                                 ACT.Sigmoid).then_inc(chain_a, 1)
            act.wait_ge(loads_in, 16 * 18)
            act.wait_ge(zs, 1)
            nc.scalar.activation(pl.al, pl.al, ACT.Exp).then_inc(betas, 1)
            nc.scalar.activation(pl.z, pl.z, ACT.Exp).then_inc(betas, 1)
            act.wait_ge(betas, 2)
            nc.scalar.activation(pl.z, pl.z, ACT.Ln, bias=core.col(ONE), scale=1.0).then_inc(lns, 1)
            act.wait_ge(sums, 2)
            nc.scalar.activation(pl.eg, pl.gsum, ACT.Exp).then_inc(chain_a, 1)
            nc.scalar.activation(pl.ekd, pl.ekd, ACT.Exp)
            nc.scalar.activation(pl.gl, core.ps[:, 7, 48:96], ACT.Exp)


def delta_stage(core, nc, pl):
    LV = 7
    pairs = [(h, d) for h in range(6) for d in range(2)]
    (rows, exps_in, d_done, grams, a_done, at_done, bm_done, pt_done, pt_copied, xu_done, x_done, u_done, ops_done,
     w_turned, nw_done, vn_sum, vn_copied, ds_done, s_done, o_done, o_copied, chain_s, row_used, xinit, x_ready) = core.sems(25)
    c4 = lambda ap: ap.rearrange("p (c n) -> p c n", c=4)
    bc = lambda ap, w: ap.rearrange("p (c o) -> p c o", o=1).broadcast_to([P, 4, w])
    mat = lambda ap: ap.rearrange("p (o n) -> p o n", o=1).broadcast_to([P, 4, P])
    cols = lambda t, h, d: t.rearrange("p (c n) -> p c n", n=12)[:, :, d * 6 + h]
    bank = lambda d, n: core.ps[:, 3 * d + n, :]
    cc = lambda c: slice(c * P, (c + 1) * P)

    def half(h):
        return slice((h % 2) * HD, (h % 2 + 1) * HD)

    def order(d):
        return range(4) if d == 0 else range(3, -1, -1)

    with nc.Block() as block:
        @block.tensor
        def _(pe):
            for h in range(6):
                hh = half(h)
                q, k = u2(core, 13 + h // 2), u2(core, 16 + h // 2)
                for d in range(2):
                    r = 2 * h + d
                    if h:
                        pe.wait_ge(s_done, 8 * h)
                    for c in range(4):
                        g = cols(pl.g, h, d)[:, c:c + 1].broadcast_to([P, P])
                        mm = nc.tensor.matmul(bank(d, 0)[:, cc(c)], g, pl.cum[d], start=True, stop=True)
                    mm.then_inc(rows, 1)
                    for c in range(4):
                        nc.tensor.matmul(bank(d, 1)[:, cc(c)], k[hh, cc(c)], k[hh, cc(c)], start=True, stop=True)
                        mm = nc.tensor.matmul(bank(d, 2)[:, cc(c)], k[hh, cc(c)], q[hh, cc(c)], start=True, stop=True)
                    mm.then_inc(grams, 1)
                for lv in range(LV):
                    for d in range(2):
                        r, R = 2 * h + d, pl.run[d]
                        n = r * LV + lv
                        nn = 2 * (h * LV + lv) + d
                        pe.wait_ge(bm_done, nn + 1)
                        if lv == 0:
                            pe.wait_ge(row_used, 2 * (r + 1))
                            pe.wait_ge(a_done, r + 1)
                            pe.wait_ge(at_done, r + 1)
                        else:
                            pe.wait_ge(u_done, nn - 1)
                        for c in range(4):
                            rhs = core.ident() if lv == 0 else R["u"][:, cc(c)]
                            mm = nc.tensor.matmul(bank(d, 0)[:, cc(c)], R["bm"][:, cc(c)], rhs, start=True, stop=True)
                        mm.then_inc(pt_done, 1)
                    if lv == 0:
                        continue
                    for d in range(2):
                        r, R = 2 * h + d, pl.run[d]
                        nn = 2 * (h * (LV - 1) + lv - 1) + d
                        pe.wait_ge(pt_copied, nn + 1)
                        if lv == 1:
                            pe.wait_ge(x_ready, r + 1)
                        else:
                            pe.wait_ge(x_done, 2 * (h * (LV - 2) + lv - 2) + d + 1)
                        for c in range(4):
                            mm = nc.tensor.matmul(bank(d, 2)[:, cc(c)], R["x"][:, cc(c)], R["pt"][:, cc(c)],
                                                  start=True, stop=True)
                        mm.then_inc(xu_done, 1)
                        if lv < LV - 1:
                            for c in range(4):
                                mm = nc.tensor.matmul(bank(d, 1)[:, cc(c)], R["pt"][:, cc(c)], R["x"][:, cc(c)],
                                                      start=True, stop=True)
                            mm.then_inc(xu_done, 1)
                for d in range(2):
                    r, R = 2 * h + d, pl.run[d]
                    pe.wait_ge(u_done, 2 * (h * LV + LV - 1) + d + 1)
                    pe.wait_ge(ops_done, r + 1)
                    for c in range(4):
                        mm = nc.tensor.matmul(bank(d, 0)[hh, cc(c)], R["rw"][:, c * HD:(c + 1) * HD], R["u"][:, cc(c)],
                                              start=True, stop=True)
                    mm.then_inc(w_turned, 1)
                if h >= 2:
                    pe.wait_ge(o_copied, h - 1)
                ob = core.ps[:, 6 + h % 2, :]
                for n in range(4):
                    for d in range(2):
                        r, R = 2 * h + d, pl.run[d]
                        c = order(d)[n]
                        m = 8 * h + 2 * n + d
                        v = bank(d, 1)[:, (n % 2) * HD:(n % 2 + 1) * HD]
                        if n:
                            pe.wait_ge(nw_done, r + 1)
                            pe.wait_ge(s_done, m - 1)
                        mm = nc.tensor.matmul(v, R["u"][:, cc(c)], R["rv"][:, c * HD:(c + 1) * HD], start=True,
                                              stop=(n == 0))
                        if n:
                            mm = nc.tensor.matmul(v, R["nw"][hh, cc(c)], R["s"][hh, (n - 1) * HD:n * HD], start=False,
                                                  stop=True)
                        mm.then_inc(vn_sum, 1)
                    for d in range(2):
                        r, R = 2 * h + d, pl.run[d]
                        c = order(d)[n]
                        m = 8 * h + 2 * n + d
                        pe.wait_ge(vn_copied, m + 1)
                        vn = R["vn"][:, n * HD:(n + 1) * HD]
                        nc.tensor.matmul(bank(d, 2)[hh, (n % 2) * HD:(n % 2 + 1) * HD], R["kd"][:, c * HD:(c + 1) * HD], vn,
                                         start=True, stop=True).then_inc(ds_done, 1)
                        mm = nc.tensor.matmul(ob[hh, cc(c)], vn, R["at"][:, cc(c)], start=(n == 0 and d == 0),
                                              stop=False, skip_group_check=True)
                        if n:
                            mm = nc.tensor.matmul(ob[hh, cc(c)], R["s"][hh, (n - 1) * HD:n * HD], R["qg"][hh, cc(c)],
                                                  start=False, stop=(n == 3), skip_group_check=True)
                mm.then_inc(o_done, 1)

        @block.scalar
        def _(act):
            for h in range(6):
                hh = half(h)
                for d in range(2):
                    r, R = 2 * h + d, pl.run[d]
                    act.wait_ge(rows, r + 1)
                    nc.scalar.activation(R["qg"][hh], bank(d, 0)[hh], ACT.Exp).then_inc(row_used, 1)
                    act.wait_ge(d_done, 2 * r + 2)
                    nc.scalar.activation(R["a"], R["a"], ACT.Exp, scale=-1.0).then_inc(exps_in, 1)
                    nc.scalar.activation(R["at"], R["at"], ACT.Exp).then_inc(exps_in, 1)
                for lv in range(1, LV):
                    for d in range(2):
                        R = pl.run[d]
                        act.wait_ge(pt_done, 2 * (h * LV + lv) + d + 1)
                        nc.scalar.activation(R["pt"], bank(d, 0), ACT.Copy).then_inc(pt_copied, 1)
                for d in range(2):
                    r, R = 2 * h + d, pl.run[d]
                    act.wait_ge(w_turned, r + 1)
                    nc.scalar.activation(R["nw"][hh], bank(d, 0)[hh], ACT.Copy, scale=-1.0).then_inc(nw_done, 1)
                act.wait_ge(o_done, h + 1)
                nc.scalar.activation(u2(core, 19 + h // 2)[hh], core.ps[hh, 6 + h % 2, :], ACT.Copy).then_inc(o_copied, 1)

        @block.gpsimd
        def _(pool):
            for h in range(6):
                hh = half(h)
                for d in range(2):
                    r, R = 2 * h + d, pl.run[d]
                    pool.wait_ge(chain_s, r + 1)
                    nc.gpsimd.tensor_scalar(R["a"], pl.d[d], 0.0, None, ALU.max).then_inc(d_done, 1)
                    nc.gpsimd.tensor_scalar(R["at"], pl.d[d], 0.0, None, ALU.min).then_inc(d_done, 1)
                for d in range(2):
                    r, R = 2 * h + d, pl.run[d]
                    pool.wait_ge(exps_in, 2 * r + 1)
                    nc.gpsimd.tensor_tensor(c4(R["a"]), c4(R["a"]), bc(cols(pl.beta, h, d), P), ALU.mult).then_inc(xinit, 1)
                    pool.wait_ge(exps_in, 2 * r + 2)
                    nc.gpsimd.tensor_tensor(c4(R["at"]), c4(R["at"]), mat(pl.cum[d]), ALU.mult).then_inc(xinit, 1)
                for lv in range(LV):
                    for d in range(2):
                        r, R = 2 * h + d, pl.run[d]
                        nn = 2 * (h * LV + lv) + d
                        if lv == 0:
                            pool.wait_ge(a_done, r + 1)
                        else:
                            pool.wait_ge(pt_done, nn - 1)
                            if lv == 1:
                                pool.wait_ge(x_ready, r + 1)
                        nc.gpsimd.tensor_tensor(c4(R["bm"]), c4(R["a"]), mat(pl.lev[d][lv]), ALU.mult).then_inc(bm_done, 1)
                        if lv == 0:
                            pool.wait_ge(bm_done, nn + 1)
                            nc.gpsimd.tensor_tensor(c4(R["x"]), mat(core.ident()), c4(R["bm"]),
                                                    ALU.subtract).then_inc(x_ready, 1)
                            kt = c4(pl.kt)[:, :, h * HD:(h + 1) * HD]
                            vt = c4(pl.vt)[:, :, h * HD:(h + 1) * HD]
                            nc.gpsimd.tensor_tensor(c4(R["rv"]), vt, bc(cols(pl.beta, h, d), HD), ALU.mult)
                            nc.gpsimd.tensor_tensor(c4(R["rw"]), kt, bc(cols(pl.bge, h, d), HD), ALU.mult)
                            nc.gpsimd.tensor_tensor(c4(R["kd"]), kt, bc(cols(pl.ekd, h, d), HD),
                                                    ALU.mult).then_inc(ops_done, 1)

        @block.vector
        def _(dve):
            for h in range(6):
                hh = half(h)
                for d in range(2):
                    r, R = 2 * h + d, pl.run[d]
                    dve.wait_ge(row_used, 2 * r + 1)
                    if h:
                        dve.wait_ge(d_done, 4 * h)
                    nc.vector.tensor_tensor(c4(pl.d[d]), c4(bank(d, 0)), bc(cols(pl.gsum, h, d), P),
                                            ALU.subtract).then_inc(chain_s, 1)
                    q = u2(core, 13 + h // 2)
                    nc.vector.tensor_tensor(R["qg"][hh], R["qg"][hh], q[hh], ALU.mult).then_inc(row_used, 1)
                for d in range(2):
                    r, R = 2 * h + d, pl.run[d]
                    dve.wait_ge(xinit, 2 * r + 1)
                    dve.wait_ge(grams, r + 1)
                    nc.vector.tensor_tensor(R["a"], R["a"], bank(d, 1), ALU.mult).then_inc(a_done, 1)
                    dve.wait_ge(xinit, 2 * r + 2)
                    nc.vector.tensor_tensor(R["at"], R["at"], bank(d, 2), ALU.mult).then_inc(at_done, 1)
                for lv in range(LV):
                    for d in range(2):
                        r, R = 2 * h + d, pl.run[d]
                        nn = 2 * (h * LV + lv) + d
                        if lv == 0:
                            dve.wait_ge(pt_done, nn + 1)
                            nc.vector.tensor_tensor(c4(R["u"]), mat(core.ident()), c4(bank(d, 0)),
                                                    ALU.subtract).then_inc(u_done, 1)
                            continue
                        per = 2 * (LV - 1) - 1
                        base = 2 * h * per + (lv - 1) * 4
                        if lv < LV - 1:
                            dve.wait_ge(xu_done, base + 2 * d + 2)
                            nc.vector.tensor_tensor(R["x"], R["x"], bank(d, 1), ALU.subtract).then_inc(x_done, 1)
                        else:
                            dve.wait_ge(xu_done, base + d + 1)
                        nc.vector.tensor_tensor(R["u"], R["u"], bank(d, 2), ALU.subtract).then_inc(u_done, 1)
                for n in range(4):
                    for d in range(2):
                        r, R = 2 * h + d, pl.run[d]
                        m = 8 * h + 2 * n + d
                        dve.wait_ge(vn_sum, m + 1)
                        nc.vector.tensor_copy(R["vn"][:, n * HD:(n + 1) * HD],
                                              bank(d, 1)[:, (n % 2) * HD:(n % 2 + 1) * HD]).then_inc(vn_copied, 1)
                    for d in range(2):
                        r, R = 2 * h + d, pl.run[d]
                        c = order(d)[n]
                        m = 8 * h + 2 * n + d
                        dve.wait_ge(ds_done, m + 1)
                        ds = bank(d, 2)[hh, (n % 2) * HD:(n % 2 + 1) * HD]
                        if n == 0:
                            nc.vector.tensor_copy(R["s"][hh, 0:HD], ds).then_inc(s_done, 1)
                        else:
                            dve.wait_ge(s_done, m - 1)
                            gl = cols(pl.gl, h, d)[hh, c:c + 1]
                            nc.vector.scalar_tensor_tensor(out=R["s"][hh, n * HD:(n + 1) * HD],
                                                           in0=R["s"][hh, (n - 1) * HD:n * HD], scalar=gl, in1=ds,
                                                           op0=ALU.mult, op1=ALU.add).then_inc(s_done, 1)


def second_layer(core, nc, a, l, lat, plain):
    view = lambda t: lat_view(core, t)
    y_view = lambda k: core.sb(Y0 - CTX + k * SEQ, T)
    y_at = lambda g, f: Y0 - CTX + g * 2 * SEQ + f * SEQ
    cat = (0, 1, 4, 5, 6, 19, 20, 21)
    norm_stage(core, nc, lat, PV0 + ROW_PREMIX + 8 * l)
    Dense(core, a["w_in_2"][l], core.h, KD, 13, plain(0), lat,
          Copy(core, nc, U0, lat, lambda g, f: U0 - CTX + g * 2 * SEQ + f * SEQ), widths={12: IN2 - 12 * GW}).run(f"in2_{l}")
    conv_stage(core, nc, l)
    group_norm(core, nc, "l2", [[(view(13 + t), view(13 + t), EIGHTH if t < 3 else ONE, None)] for t in range(6)],
               core.sb(BD0, P), 1.0, lat, EPS6)
    pl = DeltaPlan(core)
    delta_gates_stage(core, nc, a, l, pl)
    delta_stage(core, nc, pl)
    diff_stage(core, nc, a, l)
    group_norm(core, nc, "sub", [[(view(4 + t), view(4 + t), SUBG, None)] for t in range(3)],
               core.sb(BD0, P), HD, lat, EPS5)
    out = Dense(core, a["w_out_2"][l], lambda k: view(cat[k]), KD, 4, plain(0), lat,
                Copy(core, nc, 0, lat, y_at), split=True)
    group_norm(core, nc, "dn", [[(view(19 + t), view(19 + t), PV0 + ROW_DN + l, view(22 + t))] for t in range(3)],
               core.sb(BD0, P), HD, lat, EPS6, sync=out.preload)
    out.run(f"out2_{l}")
    up = Dense(core, a["w_ff1_2"][l], core.h, KD, D_FF // GW, plain(0), lat, SquaredRelu(core, nc, U0, lat))
    down = Dense(core, a["w_ff2_2"][l], view, D_FF // P, 4, plain(0), lat,
                 Copy(core, nc, 0, lat, y_at), split=True)
    norm_stage(core, nc, lat, PV0 + ROW_POSTMIX + 8 * l, src=y_view, residual=True)
    norm_stage(core, nc, lat, PV0 + ROW_PREMLP + 8 * l, extra_sync=up.preload)
    up.run(f"ff1_{l}", after=down)
    down.run(f"ff2_{l}")
    norm_stage(core, nc, lat, PV0 + ROW_POSTMLP + 8 * l, src=y_view, residual=True)


def build(nc, a, y):
    table, at = constants()
    core = Core(nc, table, at)

    ctx_seg, lat_seg = (0, CTX), (CTX, SEQ)
    both, lat = [lat_seg, ctx_seg], [lat_seg]

    def plain(start):
        return lambda ib, j: start + ib * GW + j * GW

    def gate_up(ib, j):
        return HID * (j % 2) + ib * (GW // 2) + (j // 2) * GW

    def ffn1(l, segs):
        m = M0 + 96 * l
        norm_stage(core, nc, segs, PV0 + ROW_NG + l * 16 + 8, shift=m + 3 * 16, scale=m + 4 * 16)
        down = Dense(core, a["ffn_w_out"][l], core.u, HID // P, 4, plain(0), segs,
                     Residual(core, nc, m + 5 * 16, segs), split=True)
        Dense(core, a["ffn_w_in"][l], core.h, KD, 2 * HID // GW, gate_up, segs,
              Swiglu(core, nc, U0, segs)).run(f"up{l}", after=down)
        down.run(f"down{l}")

    def mixer_norm(l):
        m = M0 + 96 * l
        norm_stage(core, nc, both, PV0 + ROW_NG + l * 16, shift=m, scale=m + 16)

    params_stage(core, nc, a, a["x"][0], a["ctx"][0])
    modulation_stage(core, nc, a["mod_w"])
    mixer_norm(0)
    Dense(core, a["even_w_in"][0], core.h, KD, EVEN_IN // GW, plain(0), both,
          Copy(core, nc, U0, both)).run("even_in")
    even_mixer(core, nc, a)
    cat = (0, 1, 2, 3, 18, 19, 20, 21)
    Dense(core, a["even_w_out"][0], lambda k: core.u(cat[k]), KD, 4, plain(0), both,
          Residual(core, nc, M0 + 2 * 16, both), split=True).run("even_out")
    ffn1(0, both)
    mixer_norm(1)
    odd_mixer(core, nc, a, both, lat)
    ffn1(1, lat)
    for l in range(2):
        second_layer(core, nc, a, l, lat, plain)
    store_stage(core, nc, y)


_INS = ["x", "c", "ctx", "c_ctx", "mod_w", "mod_b", "norm_g", "ffn_w_in", "ffn_w_out", "even_w_in",
        "even_w_out", "attn_qk_norm_g", "attn_sink", "hgrn_out_norm_g", "hgrn_lb", "odd_w_in", "odd_w_out",
        "w_in_2", "w_out_2", "pre_mix_w_2", "post_mix_w_2", "pre_mlp_w_2", "post_mlp_w_2", "w_ff1_2", "w_ff2_2",
        "conv_dw_w_2", "conv_dw_b_2", "conv_ln_w_2", "conv_ln_b_2", "diff_lambda_q1_2", "diff_lambda_k1_2",
        "diff_lambda_q2_2", "diff_lambda_k2_2", "diff_subln_w_2", "delta_conv_w_2", "delta_A_log_2",
        "delta_dt_bias_2", "delta_norm_w_2"]
_OUT = (1, SEQ, D)


def kernel(**inputs):
    import numpy as _np
    import concourse.bacc as _bacc
    from concourse import mybir as _mybir
    from concourse.bass_utils import run_bass_kernel_spmd as _run

    nc = _bacc.Bacc("TRN2", target_bir_lowering=False, num_devices=1)
    arrays, args = {}, {}
    for name in _INS:
        a = _np.ascontiguousarray(inputs[name])
        arrays[f"in_{name}"] = a
        args[name] = nc.dram_tensor(f"in_{name}", a.shape, _mybir.dt.from_np(a.dtype), kind="ExternalInput").ap()
    out = nc.dram_tensor("out_0", _OUT, _mybir.dt.float32, kind="ExternalOutput").ap()
    build(nc, args, out[0])
    r = _run(nc, [arrays], core_ids=[0])
    return r.results[0]["out_0"]
```

```python
from contextlib import ExitStack
import math

import numpy as np

import concourse.bass as bass
from concourse import mybir

ALU = mybir.AluOpType
ACT = mybir.ActivationFunctionType
AXX = mybir.AxisListType.X
F32 = mybir.dt.float32
F32R = mybir.dt.float32r
F16, BF16 = mybir.dt.float16, mybir.dt.bfloat16
U32 = mybir.dt.uint32

P = 128
D = 1024
KD = D // P
CTX, SEQ = 256, 512
T = CTX + SEQ
LAT = slice(CTX, T)
GRID_W = 64
HID = 2816
EVEN_IN = 3328
ODD_DK, ODD_DV, ODD_H = 256, 512, 4
HD = 64
CH = 64
D_FF = 4096
CONV_CH, DIFF_W, DELTA_W = 256, 384, 384
CONV_K = 31
IN2 = 2 * CONV_CH + 3 * DIFF_W + 4 * DELTA_W + 24
NEG = -1.0e30
SET = 26

GW = 256
SLOTS = 2
SLOT_W = KD * GW
X0 = 0
H0 = X0 + KD * T
RING0 = H0 + 2 * KD * T
SPLIT0 = RING0 + SLOTS * SLOT_W
C0 = SPLIT0 + 2 * SLOTS * SLOT_W
IDENT0, ONES0, BD0 = C0, C0 + P, C0 + 2 * P
PV0 = C0 + 3 * P
PV_W = 5 * P
M0 = PV0 + PV_W
M_W = 2 * 48 * 2
SM0 = M0 + M_W
SM_W = 256
U0 = SM0 + SM_W
U_W = 26 * T
ARENA = 53200
assert U0 + U_W <= ARENA and U0 + (D_FF // P + KD) * SEQ <= ARENA
T0 = H0
TW0 = RING0
Y0 = U0 + D_FF // P * SEQ

ROW_C, ROW_CC, ROW_NG, ROW_LB, ROW_OG, ROW_QKG = 0, 8, 16, 48, 56, 57
ROW2 = 2 * P
ROW_PREMIX, ROW_POSTMIX, ROW_PREMLP, ROW_POSTMLP = ROW2, ROW2 + 16, ROW2 + 32, ROW2 + 48
ROW_DWB, ROW_LNW, ROW_LNB, ROW_SUB, ROW_DN = ROW2 + 64, ROW2 + 68, ROW2 + 72, ROW2 + 76, ROW2 + 78
ROW_DW, ROW_SC = 3 * P, 4 * P

EPS6, EPS5, ZERO, ONE = SM0, SM0 + 1, SM0 + 2, SM0 + 3
COND0 = SM0 + 4
A0 = SM0 + 20
LBV0 = SM0 + 36
SINK0 = SM0 + 44
EIGHTH, SUBG, NLAM = SM0 + 76, SM0 + 77, SM0 + 78
GX0 = SM0 + 80


def constants():
    p = np.arange(P)
    c = {}
    c["ident"] = np.eye(P)
    c["ones"] = np.ones((P, P))
    c["bd"] = (p[:, None] // HD == p[None, :] // HD) * 1.0
    rot = np.zeros((P, P))
    for m in range(P):
        b, r = m // HD * HD, m % HD
        if r < HD // 2:
            rot[b + r + HD // 2, m] = -1.0
        else:
            rot[b + r - HD // 2, m] = 1.0
    c["rot"] = rot
    for v in range(2):
        c[f"dup{v}"] = (p[:, None] == v * HD + p[None, :] % HD) * 1.0
    s, q = p[None, :], p[:, None]
    c["wmask"] = np.concatenate([np.where(s >= q, 0, NEG), np.zeros((P, P)), np.where(s <= q, 0, NEG)], 1)
    t = np.arange(SEQ)
    n_freq = HD // 4
    inv = 10000.0 ** (-np.arange(n_freq, dtype=np.float32) / np.float32(n_freq))
    inv = inv.astype(np.float32)
    ang = np.concatenate([(t // GRID_W).astype(np.float32)[:, None] * inv,
                          (t % GRID_W).astype(np.float32)[:, None] * inv], 1).astype(np.float32)
    c["cosA"] = np.cos(ang.astype(np.float64)).T[p % (HD // 2)]
    c["sinA"] = np.sin(ang.astype(np.float64)).T[p % (HD // 2)]
    cols = np.arange(T)
    c["scan"] = np.tile(np.where(cols % CH == 0, 0.0, 1.0), (P, 1))
    same = p[:, None] // CH == p[None, :] // CH
    c["tri_fw"], c["tri_bw"] = (same & (p[:, None] <= p[None, :])) * 1, (same & (p[:, None] >= p[None, :])) * 1
    theta = (1.0 / (10000.0 ** np.linspace(0.0, 1.0, ODD_DK // 2))).astype(np.float32)
    ang = (t.astype(np.float32)[:, None] * theta).astype(np.float32).astype(np.float64)
    c["cosR"], c["sinR"] = np.cos(ang).T, np.sin(ang).T
    lg = np.log(1.0 - 2.0 ** (-5.0 - np.arange(ODD_H)))
    for h in range(ODD_H):
        gf, gb = lg[h], lg[ODD_H - 1 - h]
        d = np.arange(7 * P)[None, :] - p[:, None] - 3 * P
        w = np.where(d >= 0, np.exp(gf * np.maximum(d, 0)), 0) + np.where(d <= 0, np.exp(gb * np.maximum(-d, 0)), 0)
        d = np.arange(5 * P)[None, :] - p[:, None] - P
        wc = np.exp(gf * (d + CTX)) + np.exp(gb * (SEQ - d))
        c[f"ret{h}"] = np.concatenate([w, wc], 1) * ODD_DK ** -0.5
    c["dist"] = np.abs(p[:, None] - (np.arange(7 * P)[None, :] - 3 * P))
    c["cum_fw"] = (p[:, None] <= p[None, :]) * 1.0
    c["cum_bw"] = (p[:, None] >= p[None, :]) * 1.0
    for lv in range(7):
        b = 1 << lv
        r, q2 = p[:, None] // b, p[None, :] // b
        low = (r % 2 == 1) & (q2 == r - 1)
        c[f"lev_fw{lv}"] = low * 1.0
        c[f"lev_bw{lv}"] = low.T * 1.0
    names = list(c)
    at, off = {}, 0
    for n in names:
        c[n] = np.asarray(c[n])
        at[n] = (off, c[n].shape[1])
        off += c[n].shape[1]
    table = np.concatenate([c[n].astype(np.int32).view(np.float32) if n.startswith("tri_") else
                            c[n].astype(np.float32) for n in names], 1)
    return np.ascontiguousarray(table), at


S0 = H0
DT = IN2 // P


class Chain:

    def __init__(self, eng, sem):
        self.eng, self.sem, self.n = eng, sem, 0

    def __call__(self, ins):
        ins.then_inc(self.sem, 1)
        self.n += 1
        return self.n

    def wait(self, n=None):
        n = self.n if n is None else n
        if n > 0:
            self.eng.wait_ge(self.sem, n)


def rounds(eng, n, body):
    if n == 1:
        body(0)
    elif n > 1:
        with eng.Fori(0, n) as i:
            body(i)


class Core:

    def __init__(self, nc, table, at):
        self.nc = nc
        base = -(-nc.sbuf_base // 32) * 32

        def at_word(name, first, end, dtype=F32):
            return nc.alloc_sbuf_tensor_at(name, [P, end - first], dtype, offset=base + 4 * first)
        self.parts = [(0, H0, at_word("stream", 0, H0)), (H0, C0, at_word("work", H0, C0)),
                      (C0, ARENA, at_word("kept", C0, ARENA))]
        self.h_halves = at_word("h_halves", H0, RING0, F32R)
        self.w_halves = at_word("w_halves", SPLIT0, C0, F32R)
        self.ps = nc.alloc_psum_tensor("banks", [P, 8, 512], F32)
        self.ring_ready = [nc.alloc_semaphore(f"ring_ready{s}") for s in range(SLOTS)]
        self.ring_count = [0] * SLOTS
        self.table = nc.inline_tensor(table, "tables").ap()
        self.at = at
        self.sets = [[nc.alloc_semaphore(f"stage{r}_{n}") for n in range(SET)] for r in range(3)]
        self.stages = 0

    def sb(self, first, width, rows=P):
        if isinstance(first, int):
            lo, _, part = [p for p in self.parts if p[0] <= first < p[1]][0]
            return part[0:rows, first - lo:first - lo + width]
        return self.parts[2][2][:, bass.ds(first - C0, width)]

    def stream(self, first, width):
        part = self.parts[0][2]
        return part[:, first:first + width] if isinstance(first, int) else part[:, bass.ds(first, width)]

    def x(self, k):
        return self.sb(X0 + k * T, T)

    def h(self, k, low=0):
        return self.h_halves[:, (low * KD + k) * T:(low * KD + k + 1) * T]

    def u(self, k):
        return self.sb(U0 + k * T, T)

    def ident(self):
        return self.sb(IDENT0, P)

    def col(self, c):
        return self.sb(c, 1)

    def const(self, name):
        o, w = self.at[name]
        return self.table[:, o:o + w]

    def slot(self, s):
        return self.sb(RING0 + s * SLOT_W, SLOT_W).rearrange("p (k n) -> p k n", k=KD)

    def half(self, s, low):
        return self.w_halves[:, (2 * s + low) * SLOT_W:(2 * s + low + 1) * SLOT_W]

    def sems(self, n):
        r = self.stages % 3
        if self.stages > 0:
            last = self.sets[(r + 2) % 3]
            self.nc.sync.sem_clear(range(last[0].num, last[0].num + self.used))
        self.used = n
        self.stages += 1
        return self.sets[r][:n]


def halves_high(core, act, dst, src):
    return core.nc.scalar.activation(dst, src, ACT.Copy)


def halves_low(core, dve, dst, src, high):
    return core.nc.vector.tensor_tensor(dst, src, high.bitcast(F32), ALU.subtract)


class Dense:

    def __init__(self, core, w, rhs, k_tiles, groups, col, segs, finish, split=False, widths=None):
        self.core, self.rhs, self.groups, self.col, self.segs, self.finish = core, rhs, groups, col, segs, finish
        self.w = w.rearrange("(k p) n -> p k n", p=P)
        self.K = k_tiles
        n = -(-k_tiles // KD)
        self.chunks = [(c * KD, min(k_tiles, (c + 1) * KD)) for c in range(n)]
        self.body = 4 if n % 2 else 2
        self.split, self.once = split, k_tiles <= KD
        self.widths = widths or {}
        self.base, self.retired, self.started = None, False, False

    def width(self, g):
        return self.widths.get(g, GW)

    def load(self, sp, i, u):
        core, C = self.core, len(self.chunks)
        j, c = divmod(u, C)
        a, b = self.chunks[c]
        wd = self.width(i * self.body + j) if isinstance(i, int) else GW
        cols = self.col(i * self.body, j)
        src = self.w[:, a:b, cols:cols + wd] if isinstance(cols, int) else self.w[:, a:b, bass.ds(cols, wd)]
        s = u % SLOTS
        sp.dma_start(core.slot(s)[:, 0:b - a, 0:wd], src).then_inc(core.ring_ready[s], 16)

    def preload(self, sp):
        self.base = list(self.core.ring_count)
        for u in range(min(SLOTS, self.groups * len(self.chunks))):
            self.load(sp, 0, u)

    def first_high(self, act):
        act.wait_ge(self.core.ring_ready[0], self.base[0] + 16)
        self.started = True
        return halves_high(self.core, act, self.core.half(0, 0), self.core.sb(RING0, SLOT_W))

    def first_low(self, dve):
        return halves_low(self.core, dve, self.core.half(0, 1), self.core.sb(RING0, SLOT_W), self.core.half(0, 0))

    def run(self, name, after=None):
        core, nc, C, B, G, K = self.core, self.core.nc, len(self.chunks), self.body, self.groups, self.K
        units, finish = G * C, self.finish
        releases = sum(finish.releases)
        (group_summed, chunk_used, relu_done, even_free, odd_free, high_done, low_done, rhs_high, rhs_low,
         rhs_used) = core.sems(10)
        free = [even_free, odd_free]
        fly = self.split and not self.once
        preloaded = self.base is not None
        lo, width = min(s[0] for s in self.segs), sum(s[1] for s in self.segs)

        def banks(j, f):
            return [core.ps[:, 4 * n + (j % 2) * 2 + f, 0:w] for n, (_, w) in enumerate(self.segs)]

        def wait_unit(eng, i, u):
            j, c = divmod(u, C)
            if c < C - 1:
                eng.wait_ge(chunk_used, (i * B + j) * (C - 1) + c + 1)
            else:
                eng.wait_ge(group_summed, (i * B + j) * 2 + 2)

        def units_of(eng, n, body):
            rounds(eng, n // (B * C), lambda i: [body(i, u) for u in range(B * C)])
            for u in range(n % (B * C)):
                body(n // (B * C), u)

        def at(i, v):
            return (i + v // (B * C), v % (B * C)) if isinstance(i, int) else (i, v)

        def unit_words(v):
            a, b = self.chunks[v % C]
            return (b - a) * GW

        def first_tile(v):
            return v // C * K + self.chunks[v % C][0]

        def splitter(eng, weights, tiles, halves_done):
            def run(evacuate):
                if self.split:
                    tiles(0, 0, 0)
                if self.started:
                    eng.sem_inc(halves_done, 1)
                else:
                    weights(0, 0)
                if self.split:
                    for k in range(1, self.chunks[0][1]):
                        tiles(0, k, k)
                if units > 1:
                    weights(0, 1)

                def step(i, u):
                    if fly:
                        a, b = self.chunks[(u + 1) % C]
                        for k in range(a, b):
                            tiles(i, first_tile(u + 1) + k - a, k)
                    wait_unit(eng, i, u)
                    if u % C == C - 1:
                        evacuate(i, u // C)
                    weights(i, u + 2)
                n = max(0, units - 2)
                units_of(eng, n, step)
                for u in range(n, units):
                    i, v = divmod(u, B * C)
                    if fly and u < units - 1:
                        a, b = self.chunks[(v + 1) % C]
                        for k in range(a, b):
                            tiles(i, first_tile(v + 1) + k - a, k)
                    wait_unit(eng, i, v)
                    if v % C == C - 1:
                        evacuate(i, v // C)
            return run

        with nc.Block() as block:
            @block.sync
            def _(sp):
                if not preloaded:
                    self.preload(sp)

                def refill(i, u):
                    sp.wait_ge(low_done, i * B * C + u + 1)
                    self.load(sp, *at(i, u + SLOTS))
                units_of(sp, max(0, units - SLOTS), refill)
                if after is not None:
                    sp.wait_ge(low_done, units)
                    self.retire()
                    after.preload(sp)

            @block.tensor
            def _(pe):
                def group(i, j):
                    r = i * (B // 2) + j // 2
                    pe.wait_ge(free[j % 2], (r + 1) * 2 * releases)
                    for c, (a, b) in enumerate(self.chunks):
                        u = j * C + c
                        pe.wait_ge(low_done, i * B * C + u + 1)
                        high, low = (core.half(u % SLOTS, n).rearrange("p (k n) -> p k n", k=KD) for n in range(2))
                        for k in range(a, b):
                            n = j * K + k
                            if fly:
                                pe.wait_ge(rhs_low, i * B * K + n + 1)
                            elif self.split:
                                pe.wait_ge(rhs_low, k + 1)
                            q = n % KD if fly else k
                            rh, rl = (core.h(q), core.h(q, 1)) if self.split else (self.rhs(k, 0), self.rhs(k, 1))
                            for f in range(2):
                                fc = slice(f * P, (f + 1) * P)
                                for s, (t0, tw) in enumerate(self.segs):
                                    tc = slice(t0, t0 + tw)
                                    o = banks(j, f)[s]
                                    nc.tensor.matmul(o, low[:, k - a, fc], rh[:, tc], start=(k == 0), stop=False)
                                    nc.tensor.matmul(o, high[:, k - a, fc], rl[:, tc], start=False, stop=False)
                                    mm = nc.tensor.matmul(o, high[:, k - a, fc], rh[:, tc], start=False, stop=(k == K - 1))
                                if k == K - 1:
                                    mm.then_inc(group_summed, 1)
                            if k == b - 1 and c < C - 1:
                                mm.then_inc(chunk_used, 1)
                            elif fly and k < K - 1:
                                mm.then_inc(rhs_used, 1)
                rounds(pe, G // B, lambda i: [group(i, j) for j in range(B)])
                for j in range(G % B):
                    group(G // B, j)

            def wait_tile(eng, i, n):
                m = n - KD
                if n < KD and isinstance(i, int) and i == 0:
                    return
                j, k = divmod(m, K) if m >= 0 else (-1, m + K)
                c = k // KD
                if k == self.chunks[c][1] - 1:
                    if c < C - 1:
                        eng.wait_ge(chunk_used, (i * B + j) * (C - 1) + c + 1)
                    else:
                        eng.wait_ge(group_summed, (i * B + j) * 2 + 2)
                else:
                    eng.wait_ge(rhs_used, (i * B + j) * (K - C) + k - c + 1)

            @block.scalar
            def _(act):
                act.sem_inc(even_free, 2 * releases)
                act.sem_inc(odd_free, 2 * releases)

                def weights(i, v):
                    s = v % SLOTS
                    act.wait_ge(core.ring_ready[s], self.base[s] + (i * (B * C // SLOTS) + v // SLOTS + 1) * 16)
                    n = unit_words(v)
                    halves_high(core, act, core.half(s, 0)[:, 0:n],
                                core.sb(RING0 + s * SLOT_W, n)).then_inc(high_done, 1)

                def tiles(i, n, k):
                    if fly:
                        wait_tile(act, i, n)
                    halves_high(core, act, core.h(n % KD)[:, lo:lo + width],
                                self.rhs(k)[:, lo:lo + width]).then_inc(rhs_high, 1)

                def evacuate(i, j):
                    if finish.scalar is not None and finish.takes(j)[0]:
                        for f in range(2):
                            finish.scalar(act, i * B + j, j, f, banks(j, f), relu_done, free[j % 2])
                splitter(act, weights, tiles, high_done)(evacuate)

            @block.vector
            def _(dve):
                def weights(i, v):
                    s = v % SLOTS
                    dve.wait_ge(high_done, i * B * C + v + 1)
                    n = unit_words(v)
                    halves_low(core, dve, core.half(s, 1)[:, 0:n], core.sb(RING0 + s * SLOT_W, n),
                               core.half(s, 0)[:, 0:n]).then_inc(low_done, 1)

                def tiles(i, n, k):
                    dve.wait_ge(rhs_high, i * B * K + n + 1)
                    halves_low(core, dve, core.h(n % KD, 1)[:, lo:lo + width], self.rhs(k)[:, lo:lo + width],
                               core.h(n % KD)[:, lo:lo + width]).then_inc(rhs_low, 1)

                def evacuate(i, j):
                    if finish.vector is not None and finish.takes(j)[1]:
                        for f in range(2):
                            if finish.after_scalar:
                                dve.wait_ge(relu_done, (i * B + j) * 2 + f + 1)
                            finish.vector(dve, i * B + j, j, f, banks(j, f), free[j % 2], even_free)
                splitter(dve, weights, tiles, low_done)(evacuate)

        if after is None:
            self.retire()

    def retire(self):
        if self.base is not None and not self.retired:
            n = self.groups * len(self.chunks)
            self.core.ring_count = [self.base[s] + 16 * ((n - s + SLOTS - 1) // SLOTS) for s in range(SLOTS)]
            self.retired = True


class Finish:
    scalar = vector = None
    after_scalar = False
    releases = (0, 0)

    def takes(self, j):
        return True, True


class Copy(Finish):

    def __init__(self, core, nc, dst, segs, where=None):
        self.releases = (1, 1) if len(segs) == 2 else (1, 0)
        self.where = where or (lambda g, f: dst + (g * 2 + f) * T)

        def scalar(act, g, j, f, banks, half, free):
            lo, w = segs[0]
            nc.scalar.activation(core.sb(self.where(g, f) + lo, w), banks[0], ACT.Copy).then_inc(free, 1)

        def vector(dve, g, j, f, banks, free, gates):
            lo, w = segs[1]
            nc.vector.tensor_copy(core.sb(self.where(g, f) + lo, w), banks[1]).then_inc(free, 1)
        self.scalar = scalar
        self.vector = vector if len(segs) == 2 else None


class Residual(Finish):

    def __init__(self, core, nc, gate, segs):
        self.releases = (0, 1)

        def vector(dve, g, j, f, banks, free, gates):
            for n, (lo, w) in enumerate(segs):
                x = core.stream((g * 2 + f) * T + lo, w)
                ins = nc.vector.scalar_tensor_tensor(out=x, in0=banks[n], scalar=core.col(gate + (g * 2 + f) * 2 + n),
                                                     in1=x, op0=ALU.mult, op1=ALU.add)
            ins.then_inc(free, 1)
        self.vector = vector


class Swiglu(Finish):

    def __init__(self, core, nc, dst, segs):
        self.releases = (1, 0)

        def tile(g, j, f):
            return dst + ((g - j % 2) + f) * T

        def scalar(act, g, j, f, banks, half, free):
            for n, (lo, w) in enumerate(segs):
                ins = nc.scalar.activation(core.sb(tile(g, j, f) + lo, w), banks[n], ACT.Silu)
            ins.then_inc(free, 1)

        def vector(dve, g, j, f, banks, free, gates):
            dve.wait_ge(gates, g + f + 2)
            for n, (lo, w) in enumerate(segs):
                o = core.sb(tile(g, j, f) + lo, w)
                ins = nc.vector.tensor_tensor(o, o, banks[n], ALU.mult)
            ins.then_inc(free, 1)
        self.scalar, self.vector = scalar, vector

    def takes(self, j):
        return j % 2 == 0, j % 2 == 1


class SquaredRelu(Finish):
    after_scalar = True

    def __init__(self, core, nc, dst, segs):
        self.releases = (0, 1)
        lo, w = segs[0]

        def scalar(act, g, j, f, banks, half, free):
            nc.scalar.activation(core.sb(dst + (g * 2 + f) * SEQ, w), banks[0], ACT.Relu).then_inc(half, 1)

        def vector(dve, g, j, f, banks, free, gates):
            o = core.sb(dst + (g * 2 + f) * SEQ, w)
            nc.vector.tensor_tensor(o, o, banks[0], ALU.mult).then_inc(free, 1)
        self.scalar, self.vector = scalar, vector


def params_stage(core, nc, a, x_in, ctx_in):
    at = lambda t, r, n, c0=0, cw=P: core.sb(T0 + t * P + c0, cw)[r:r + n]
    loads = [
        (at(0, ROW_C, 8), a["c"].rearrange("o (r p) -> (o r) p", p=P)),
        (at(0, ROW_CC, 8), a["c_ctx"].rearrange("(r p) -> r p", p=P)),
        (at(0, ROW_NG, 32), a["norm_g"].rearrange("l n (r p) -> (l n r) p", p=P)),
        (at(0, ROW_LB, 8), a["hgrn_lb"].rearrange("l (r p) -> (l r) p", p=P)),
        (at(0, ROW_OG, 1), a["hgrn_out_norm_g"]),
        (at(1, 0, 96), a["mod_b"].rearrange("l (r p) -> (l r) p", p=P)),
    ]
    for half in range(2):
        loads.append((at(0, ROW_QKG, 2, half * HD, HD), a["attn_qk_norm_g"].rearrange("o r p -> (o r) p")))
        loads.append((at(2, ROW_SUB - ROW2, 2, half * HD, HD), a["diff_subln_w_2"]))
        loads.append((at(2, ROW_DN - ROW2, 2, half * HD, HD), a["delta_norm_w_2"]))
    for row, name in ((ROW_PREMIX, "pre_mix_w_2"), (ROW_POSTMIX, "post_mix_w_2"), (ROW_PREMLP, "pre_mlp_w_2"),
                      (ROW_POSTMLP, "post_mlp_w_2"), (ROW_DWB, "conv_dw_b_2"), (ROW_LNW, "conv_ln_w_2"),
                      (ROW_LNB, "conv_ln_b_2")):
        v = a[name].rearrange("l (r p) -> (l r) p", p=P)
        loads.append((at(2, row - ROW2, v.shape[0]), v))
    loads.append((at(3, 0, 124), a["conv_dw_w_2"].rearrange("l k (r p) -> (l k r) p", p=P)))
    loads.append((at(4, 0, 54), a["delta_conv_w_2"].rearrange("l k (r p) -> (l k r) p", p=P)))
    heights = [59, 96, 80, 124, 54]
    tok = core.sb(U0, 6 * D).rearrange("p (t d) -> p t d", t=6)

    tables_in, rows_in, tokens_in, rows_turned, tokens_turned, turned_used, smalls = core.sems(7)

    with nc.Block() as block:
        @block.sync
        def _(sp):
            for name, o in (("ident", IDENT0), ("ones", ONES0), ("bd", BD0)):
                sp.dma_start(core.sb(o, P), core.const(name)).then_inc(tables_in, 16)
            for dst, src in loads:
                sp.dma_start(dst, src).then_inc(rows_in, 16)
            sp.dma_start(core.sb(SINK0, 8), a["attn_sink"][0].partition_broadcast(P)).then_inc(rows_in, 16)
            sp.dma_start(tok[:, 0:2], ctx_in.rearrange("(t p) d -> p t d", p=P)).then_inc(tokens_in, 16)
            sp.dma_start(tok[:, 2:6], x_in.rearrange("(t p) d -> p t d", p=P)).then_inc(tokens_in, 16)

        @block.tensor
        def _(pe):
            pe.wait_ge(tables_in, 48)
            pe.wait_ge(rows_in, 16 * (len(loads) + 1))
            for t, n in enumerate(heights):
                mm = nc.tensor.transpose(core.ps[:, t, 0:n], core.sb(T0 + t * P, P, n),
                                         core.sb(IDENT0, n, n))
            mm.then_inc(rows_turned, 1)
            pe.wait_ge(tokens_in, 32)
            pe.wait_ge(turned_used, 1)
            for b in range(12):
                if b >= 8:
                    pe.wait_ge(turned_used, b - 8 + 2)
                for q in range(4):
                    k, t = divmod(b * 4 + q, 6)
                    mm = nc.tensor.transpose(core.ps[:, b % 8, q * P:(q + 1) * P], tok[:, t, k * P:(k + 1) * P],
                                             core.ident())
                mm.then_inc(tokens_turned, 1)

        @block.vector
        def _(dve):
            nc.vector.memset(core.col(EPS6), 1e-6)
            nc.vector.memset(core.col(EPS5), 1e-5)
            nc.vector.memset(core.col(ZERO), 0.0)
            nc.vector.memset(core.col(ONE), 1.0)
            nc.vector.memset(core.col(EIGHTH), HD ** -0.5)
            dve.wait_ge(rows_turned, 1)
            for t, n in enumerate(heights):
                last = nc.vector.tensor_copy(core.sb(PV0 + t * P, n), core.ps[:, t, 0:n])
            last.then_inc(turned_used, 1)
            dve.wait_ge(turned_used, 1)
            nc.vector.tensor_scalar(core.sb(SINK0 + 8, 8), core.sb(SINK0, 8), -1.0, None, ALU.mult)
            nc.vector.tensor_tensor(core.sb(LBV0, 4), core.sb(PV0 + ROW_LB + 4, 4), core.sb(PV0 + ROW_LB, 4),
                                    ALU.subtract).then_inc(smalls, 1)
            for b in range(12):
                dve.wait_ge(tokens_turned, b + 1)
                nc.vector.tensor_copy(core.sb(X0 + b * 512, 512), core.ps[:, b % 8, :]).then_inc(turned_used, 1)
            dve.wait_ge(smalls, 2)
            nc.vector.tensor_scalar(core.sb(LBV0 + 4, 4), core.sb(LBV0, 4), -1.0, 1.0, ALU.mult, ALU.add)

        @block.scalar
        def _(act):
            act.wait_ge(smalls, 1)
            nc.scalar.activation(core.sb(LBV0, 4), core.sb(LBV0, 4), ACT.Sigmoid, scale=-1.0).then_inc(smalls, 1)
            cond = core.sb(COND0, 16).rearrange("p (k n) -> p k n", n=2)
            for n, row in enumerate((ROW_C, ROW_CC)):
                nc.scalar.activation(cond[:, :, n], core.sb(PV0 + row, 8), ACT.Silu).then_inc(smalls, 1)


def modulation_stage(core, nc, mod_w):
    slots, body, cols = 3, 6, 512
    per_layer = mod_w.shape[2] // cols
    slot = lambda s: core.sb(RING0 + s * KD * cols, KD * cols).rearrange("p (k n) -> p k n", k=KD)
    row = lambda b: core.sb(U0 + b * cols, cols, 2)
    (in0, in1, in2, rows_summed, rows_copied, rows_turned, bias_added) = core.sems(7)
    weights_in = [in0, in1, in2]
    layers = mod_w.shape[0]
    R = per_layer // body
    turned = lambda j: core.ps[:, 2 + j % 2, 0:8]

    def loop(eng, body_of):
        for layer in range(layers):
            if layer == 0:
                body_of(0, 0, 0)
                rounds(eng, R - 1, lambda i: body_of(0, i + 1, 1))
            else:
                rounds(eng, R, lambda i: body_of(layer, i, 1))

    with nc.Block() as block:
        @block.sync
        def _(sp):
            def body_of(layer, i, later):
                for j in range(body):
                    g = (layer * R + i) * body + j
                    if later or j >= slots:
                        sp.wait_ge(rows_summed, g - slots + 1)
                    w = mod_w[layer].rearrange("(k p) n -> p k n", p=P)
                    sp.dma_start(slot(j % slots), w[:, :, bass.ds((i * body + j) * cols, cols)]
                                 ).then_inc(weights_in[j % slots], 16)
            loop(sp, body_of)

        @block.tensor
        def _(pe):
            def turn(g, j):
                for q in range(4):
                    mm = nc.tensor.transpose(turned(j)[:, 2 * q:2 * q + 2], row(j % 2)[:, q * P:(q + 1) * P],
                                             core.sb(IDENT0, 2, 2))
                mm.then_inc(rows_turned, 1)

            def body_of(layer, i, later):
                for j in range(body):
                    r = layer * R + i
                    g = r * body + j
                    pe.wait_ge(weights_in[j % slots], (r * (body // slots) + j // slots + 1) * 16)
                    if later or j >= 2:
                        pe.wait_ge(rows_copied, g - 1)
                    if later or j >= 4:
                        pe.wait_ge(bias_added, g - 3)
                    for k in range(KD):
                        mm = nc.tensor.matmul(core.ps[0:2, j % 2, 0:cols], core.sb(COND0 + 2 * k, 2),
                                              slot(j % slots)[:, k], start=(k == 0), stop=(k == KD - 1))
                    mm.then_inc(rows_summed, 1)
                    if later or j >= 2:
                        turn(g - 2, (j - 2) % body)
            loop(pe, body_of)
            for g in range(layers * per_layer - 2, layers * per_layer):
                pe.wait_ge(rows_copied, g + 1)
                pe.wait_ge(bias_added, g - 1)
                turn(g, g % body)

        @block.scalar
        def _(act):
            def body_of(layer, i, later):
                for j in range(body):
                    g = (layer * R + i) * body + j
                    act.wait_ge(rows_summed, g + 1)
                    if later or j >= 2:
                        act.wait_ge(rows_turned, g - 1)
                    nc.scalar.activation(row(j % 2), core.ps[0:2, j % 2, 0:cols], ACT.Copy).then_inc(rows_copied, 1)
            loop(act, body_of)

        @block.vector
        def _(dve):
            def body_of(layer, i, later):
                for j in range(body):
                    g = (layer * R + i) * body + j
                    dve.wait_ge(rows_turned, g + 1)
                    bias = core.sb(PV0 + P + g * 4, 4).rearrange("p (q n) -> p q n", n=1).broadcast_to([P, 4, 2])
                    nc.vector.tensor_tensor(core.sb(M0 + g * 8, 8).rearrange("p (q n) -> p q n", n=2),
                                            turned(j).rearrange("p (q n) -> p q n", n=2), bias,
                                            ALU.add).then_inc(bias_added, 1)
            loop(dve, body_of)


def norm_stage(core, nc, segs, gain, shift=None, scale=None, src=None, residual=False, then=None):
    src = src or core.x
    lo, w = min(s[0] for s in segs), sum(s[1] for s in segs)
    sq = [core.sb(U0 + b * T, T) for b in range(4)]
    std = core.sb(U0 + 4 * T, T)
    squared, square_used, summed, std_done, rstd_done, scaled, gains, high, low, shifted, pool_low, first_high = core.sems(12)
    gaincol = (lambda n, k: core.col(A0 + n * 8 + k)) if scale is not None else (lambda n, k: core.col(gain + k))
    shiftcol = (lambda n, k: core.col(shift + k * 2 + n)) if shift is not None else (lambda n, k: core.col(ZERO))
    def add(engine, k):
        s, sw = segs[0]
        engine.tensor_tensor(core.x(k)[:, s:s + sw], core.x(k)[:, s:s + sw], src(k)[:, s:s + sw], ALU.add)

    pool_tiles = [1, 4]

    def lower(dve, k):
        dve.wait_ge(high, k + 1)
        for n, (s, sw) in enumerate(segs):
            ins = nc.vector.scalar_tensor_tensor(out=core.h(k, 1)[:, s:s + sw], in0=sq[k % 4][:, s:s + sw],
                                                 scalar=shiftcol(n, k), in1=core.h(k)[:, s:s + sw].bitcast(F32),
                                                 op0=ALU.add, op1=ALU.subtract)
        ins.then_inc(low, 1)

    with nc.Block() as block:
        if then is not None and then.base is None:
            block.sync(then.preload)

        @block.scalar
        def _(act):
            for k in range(KD):
                if k >= 4:
                    act.wait_ge(square_used, max(1, k - 4))
                nc.scalar.activation(sq[k % 4][:, lo:lo + w], src(k)[:, lo:lo + w], ACT.Square).then_inc(squared, 1)
            if then is not None:
                then.first_high(act).then_inc(first_high, 1)
            act.wait_ge(summed, 1)
            for n, (s, sw) in enumerate(segs):
                nc.scalar.activation(std[:, s:s + sw], core.ps[:, n, 0:sw], ACT.Sqrt, bias=core.col(EPS6),
                                     scale=1.0 / D).then_inc(std_done, 1)
            if not residual:
                for k in range(KD):
                    act.wait_ge(scaled, k + 1)
                    for n, (s, sw) in enumerate(segs):
                        ins = nc.scalar.activation(core.h(k)[:, s:s + sw], sq[k % 4][:, s:s + sw], ACT.Identity,
                                                   bias=shiftcol(n, k), scale=1.0)
                    ins.then_inc(high, 1)
                    if k in pool_tiles:
                        for n, (s, sw) in enumerate(segs):
                            t = sq[k % 4][:, s:s + sw]
                            ins = nc.scalar.activation(t, t, ACT.Identity, bias=shiftcol(n, k), scale=1.0)
                        ins.then_inc(shifted, 1)

        @block.tensor
        def _(pe):
            pe.wait_ge(square_used, KD - 1)
            for n, (s, sw) in enumerate(segs):
                mm = nc.tensor.matmul(core.ps[:, n, 0:sw], core.sb(ONES0, P), std[:, s:s + sw], start=True, stop=True)
            mm.then_inc(summed, 1)
            if then is not None:
                pe.wait_ge(high, 5)
                for _ in range(3):
                    nc.tensor.matmul(core.ps[:, 7, :], core.sb(ONES0, P), core.x(0)[:, LAT], start=True, stop=True)

        @block.vector
        def _(dve):
            if scale is not None:
                for n in range(len(segs)):
                    m = core.sb(scale, 16).rearrange("p (k n) -> p k n", n=2)[:, :, n]
                    nc.vector.scalar_tensor_tensor(out=core.sb(A0 + n * 8, 8), in0=m, scalar=1.0,
                                                   in1=core.sb(gain, 8), op0=ALU.add, op1=ALU.mult).then_inc(gains, 1)
                dve.wait_ge(gains, len(segs))
            for k in range(1, KD):
                dve.wait_ge(squared, k + 1)
                if k > 1:
                    dve.wait_ge(square_used, k - 1)
                nc.vector.tensor_tensor(std[:, lo:lo + w], (std if k > 1 else sq[0])[:, lo:lo + w],
                                        sq[k % 4][:, lo:lo + w], ALU.add).then_inc(square_used, 1)
            if then is not None:
                dve.wait_ge(first_high, 1)
                then.first_low(dve)
            for n, (s, sw) in enumerate(segs):
                dve.wait_ge(std_done, n + 1)
                nc.vector.reciprocal(std[:, s:s + sw], std[:, s:s + sw]).then_inc(rstd_done, 1)
            dve.wait_ge(rstd_done, len(segs))

            for k in range(KD):
                if residual and k:
                    dve.wait_ge(scaled, k)
                if not residual and k >= 4:
                    if k - 4 in pool_tiles:
                        dve.wait_ge(pool_low, pool_tiles.index(k - 4) + 1)
                    else:
                        dve.wait_ge(low, len([t for t in range(k - 3) if t not in pool_tiles]))
                for n, (s, sw) in enumerate(segs):
                    o = src(k)[:, s:s + sw] if residual else sq[k % 4][:, s:s + sw]
                    ins = nc.vector.scalar_tensor_tensor(out=o, in0=src(k)[:, s:s + sw], scalar=gaincol(n, k),
                                                         in1=std[:, s:s + sw], op0=ALU.mult, op1=ALU.mult)
                ins.then_inc(scaled, 1)
                if not residual and k and k - 1 not in pool_tiles:
                    lower(dve, k - 1)
                if residual and k and (k - 1) % 3:
                    add(nc.vector, k - 1)
            if residual:
                dve.wait_ge(scaled, KD)
                add(nc.vector, KD - 1)
            else:
                lower(dve, KD - 1)

        @block.gpsimd
        def _(pool):
            if residual:
                for k in range(0, KD, 3):
                    pool.wait_ge(scaled, k + 1)
                    add(nc.gpsimd, k)
            else:
                for n, k in enumerate(pool_tiles):
                    pool.wait_ge(shifted, n + 1)
                    nc.gpsimd.tensor_tensor(core.h(k, 1)[:, lo:lo + w], sq[k % 4][:, lo:lo + w],
                                            core.h(k)[:, lo:lo + w].bitcast(F32), ALU.subtract).then_inc(pool_low, 1)


def store_stage(core, nc, y):
    turned, copied, stored = core.sems(3)
    tok = core.sb(U0, 4 * D).rearrange("p (t d) -> p t d", t=4)
    with nc.Block() as block:
        @block.tensor
        def _(pe):
            for b in range(8):
                t, half = divmod(b, 2)
                for q in range(4):
                    mm = nc.tensor.transpose(core.ps[:, b, q * P:(q + 1) * P],
                                             core.x(half * 4 + q)[:, CTX + t * P:CTX + (t + 1) * P], core.ident())
                mm.then_inc(turned, 1)

        @block.vector
        def _(dve):
            for b in range(8):
                t, half = divmod(b, 2)
                dve.wait_ge(turned, b + 1)
                nc.vector.tensor_copy(tok[:, t, half * 512:half * 512 + 512], core.ps[:, b, :]).then_inc(copied, 1)

        @block.sync
        def _(sp):
            for t in range(4):
                sp.wait_ge(copied, 2 * t + 2)
                sp.dma_start(y[t * P:(t + 1) * P, :], tok[:, t]).then_inc(stored, 16)
            sp.wait_ge(stored, 64)


def group_norm(core, nc, name, groups, ones, count, segs, eps, then=None, scratch=T0):
    lo, w = min(s[0] for s in segs), sum(s[1] for s in segs)
    sq = [core.sb(scratch + b * T, T) for b in range(4)]
    std = [core.sb(scratch + (4 + b) * T, T) for b in range(2)]
    squared, square_used, summed, std_done, rstd_done, scaled, first_high = core.sems(7)
    items = [(g, q, it) for g, grp in enumerate(groups) for q, it in enumerate(grp)]
    first = [sum(len(x) for x in groups[:g]) for g in range(len(groups) + 1)]
    ns = len(segs)
    with nc.Block() as block:
        if then is not None:
            block.sync(then.preload)

        @block.scalar
        def _(act):
            def root(g):
                for n, (s, sw) in enumerate(segs):
                    act.wait_ge(summed, g + 1)
                    if g >= 2:
                        act.wait_ge(scaled, first[g - 1])
                    nc.scalar.activation(std[g % 2][:, s:s + sw], core.ps[:, (g % 2) * 2 + n, 0:sw], ACT.Sqrt,
                                         bias=core.col(eps), scale=1.0 / count).then_inc(std_done, 1)
            for g, grp in enumerate(groups):
                for q, it in enumerate(grp):
                    m = first[g] + q
                    if m >= 4:
                        act.wait_ge(square_used, m - 3)
                    nc.scalar.activation(sq[m % 4][:, lo:lo + w], it[0][:, lo:lo + w], ACT.Square).then_inc(squared, 1)
                if g >= 1:
                    root(g - 1)
            root(len(groups) - 1)
            if then is not None:
                then.first_high(act).then_inc(first_high, 1)

        @block.tensor
        def _(pe):
            for g, grp in enumerate(groups):
                if g >= 2:
                    pe.wait_ge(std_done, (g - 1) * ns)
                for q in range(len(grp)):
                    m = first[g] + q
                    pe.wait_ge(squared, m + 1)
                    for n, (s, sw) in enumerate(segs):
                        mm = nc.tensor.matmul(core.ps[:, (g % 2) * 2 + n, 0:sw], ones, sq[m % 4][:, s:s + sw],
                                              start=(q == 0), stop=(q == len(grp) - 1))
                    mm.then_inc(square_used, 1)
                pe.wait_ge(square_used, first[g + 1])
                pe.sem_inc(summed, 1)
            if then is not None:
                pe.wait_ge(rstd_done, len(groups) * ns)
                for _ in range(3):
                    nc.tensor.matmul(core.ps[:, 7, :], core.sb(ONES0, P), core.x(0)[:, LAT], start=True, stop=True)

        @block.vector
        def _(dve):
            for g, grp in enumerate(groups):
                for n, (s, sw) in enumerate(segs):
                    dve.wait_ge(std_done, g * ns + n + 1)
                    r = std[g % 2][:, s:s + sw]
                    nc.vector.reciprocal(r, r).then_inc(rstd_done, 1)
                dve.wait_ge(rstd_done, (g + 1) * ns)
                for src, out, gain, mul in grp:
                    nc.vector.scalar_tensor_tensor(out=out[:, lo:lo + w], in0=src[:, lo:lo + w],
                                                   scalar=core.col(gain), in1=std[g % 2][:, lo:lo + w],
                                                   op0=ALU.mult, op1=ALU.mult).then_inc(scaled, 1)
            if then is not None:
                dve.wait_ge(first_high, 1)
                then.first_low(dve)

        @block.gpsimd
        def _(pool):
            for m, (g, q, (src, out, gain, mul)) in enumerate(items):
                if mul is not None:
                    pool.wait_ge(scaled, m + 1)
                    nc.gpsimd.tensor_tensor(out[:, lo:lo + w], out[:, lo:lo + w], mul[:, lo:lo + w], ALU.mult)



def rope_stage(core, nc, tiles, wanted, v_tile, kdup, vtok, cos, sin, rot, dups):
    n = len(tiles)
    tmp = [core.sb(T0 + b * SEQ, SEQ) for b in range(4)]
    tables_in, rotated, sined, cosined, roped, duplicated = core.sems(6)
    with nc.Block() as block:
        @block.sync
        def _(sp):
            for dst, name in wanted:
                sp.dma_start(dst, core.const(name)).then_inc(tables_in, 16)

        @block.tensor
        def _(pe):
            pe.wait_ge(tables_in, 16 * len(wanted))
            for t in range(n):
                if t >= 2:
                    pe.wait_ge(sined, t - 1)
                nc.tensor.matmul(core.ps[:, t % 2, :], rot, tiles[t][:, LAT], start=True, stop=True).then_inc(rotated, 1)
            for t in range(6):
                mm = nc.tensor.transpose(core.ps[:, 6 + t // 4, (t % 4) * P:(t % 4 + 1) * P],
                                         v_tile[:, t * P:(t + 1) * P], core.ident())
            mm.then_inc(duplicated, 1)
            pe.wait_ge(roped, n)
            for v in range(2):
                nc.tensor.matmul(core.ps[:, 2 + v, :], dups[v], tiles[n - 1][:, LAT], start=True, stop=True)
                mm = nc.tensor.matmul(core.ps[:, 4 + v, 0:CTX], dups[v], tiles[n - 1][:, 0:CTX], start=True, stop=True)
            mm.then_inc(duplicated, 1)

        @block.gpsimd
        def _(pool):
            pool.wait_ge(tables_in, 16 * len(wanted))
            for t in range(n):
                if t >= 2:
                    pool.wait_ge(roped, t - 1)
                nc.gpsimd.tensor_tensor(tmp[2 + t % 2], tiles[t][:, LAT], cos, ALU.mult).then_inc(cosined, 1)

        @block.vector
        def _(dve):
            dve.wait_ge(tables_in, 16 * len(wanted))
            for t in range(n):
                dve.wait_ge(rotated, t + 1)
                nc.vector.tensor_tensor(tmp[t % 2], core.ps[:, t % 2, :], sin, ALU.mult).then_inc(sined, 1)
                dve.wait_ge(sined, t + 1)
                dve.wait_ge(cosined, t + 1)
                nc.vector.tensor_tensor(tiles[t][:, LAT], tmp[t % 2], tmp[2 + t % 2], ALU.add).then_inc(roped, 1)

        @block.scalar
        def _(act):
            act.wait_ge(duplicated, 1)
            for b, w in ((0, 512), (1, 256)):
                nc.scalar.activation(vtok[:, b * 512:b * 512 + w], core.ps[:, 6 + b, 0:w], ACT.Copy)
            act.wait_ge(duplicated, 2)
            for v in range(2):
                nc.scalar.activation(kdup[v][:, LAT], core.ps[:, 2 + v, :], ACT.Copy)
                nc.scalar.activation(kdup[v][:, 0:CTX], core.ps[:, 4 + v, 0:CTX], ACT.Copy)


def window_stage(core, nc, tiles, kdup, vtok, wmask):
    steps = [(h, i) for h in range(8) for i in range(6)]
    N = len(steps)
    pr = [core.sb(T0 + b * 640, 640) for b in range(2)]
    pt = [core.sb(T0 + 1280 + b * 640, 640) for b in range(2)]
    ident16 = core.sb(T0 + 2560, P // 2).bitcast(BF16)
    mask16 = core.sb(T0 + 2560 + P // 2, 3 * P // 2).bitcast(BF16)
    small = lambda s, c: core.col(GX0 + (s % 2) * 8 + c)
    masks_ready, scored, maxed, exped, normalised, turned, turned_copied, weighted, out_done, chain_s = core.sems(10)
    flat = core.ps[:, :, :].rearrange("p b n -> p (b n)")

    def keys(i):
        if i < 2:
            return [], 0
        b = i - 2
        ks = [t for t in (b - 1, b, b + 1) if 0 <= t < 4]
        return ks, (ks[0] - b + 1) * P

    def span(s):
        n = len(keys(steps[s][1])[0])
        o = (s % 2) * 1024
        return flat[:, o + 512 - n * P:o + 768], n

    with nc.Block() as block:
        @block.tensor
        def _(pe):
            def scores(s):
                h, i = steps[s]
                ks, m0 = keys(i)
                hh = slice((h % 2) * HD, (h % 2 + 1) * HD)
                q = tiles[h // 2][hh, i * P:(i + 1) * P]
                k = kdup[h // 4]
                if s >= 2:
                    pe.wait_ge(exped, s - 1)
                n = len(ks)
                if n:
                    lat = core.ps[:, (s % 2) * 2, 512 - n * P:512]
                    nc.tensor.matmul(lat, ident16, mask16[:, m0:m0 + n * P], start=True, stop=False)
                    nc.tensor.matmul(lat, q, k[hh, CTX + ks[0] * P:CTX + (ks[0] + n) * P], start=False, stop=True)
                nc.tensor.matmul(core.ps[:, (s % 2) * 2 + 1, 0:CTX], q, k[hh, 0:CTX], start=True,
                                 stop=True).then_inc(scored, 1)

            def turn(s):
                pe.wait_ge(normalised, s + 1)
                if s:
                    pe.wait_ge(turned_copied, s)
                _, n = span(s)
                for j in range(n + 2):
                    mm = nc.tensor.transpose(flat[:, 2048 + j * P:2048 + (j + 1) * P],
                                             pr[s % 2][:, j * P:(j + 1) * P], core.ident())
                mm.then_inc(turned, 1)

            def weigh(s):
                h, i = steps[s]
                ks, _ = keys(i)
                vt = [2 + k for k in ks] + [0, 1]
                kv = h // 4
                pe.wait_ge(turned_copied, s + 1)
                if s >= 2:
                    pe.wait_ge(out_done, s - 1)
                o = core.ps[(h % 2) * HD:(h % 2 + 1) * HD, 6 + s % 2, 0:P]
                for j, t in enumerate(vt):
                    mm = nc.tensor.matmul(o, vtok[:, t * P + kv * HD:t * P + (kv + 1) * HD],
                                          pt[s % 2][:, j * P:(j + 1) * P], start=(j == 0), stop=(j == len(vt) - 1))
                mm.then_inc(weighted, 1)

            pe.wait_ge(masks_ready, 2)
            scores(0)
            for s in range(N):
                if s + 1 < N:
                    scores(s + 1)
                if s:
                    weigh(s - 1)
                turn(s)
            weigh(N - 1)

        @block.gpsimd
        def _(pool):
            nc.gpsimd.tensor_copy(ident16, core.ident()).then_inc(masks_ready, 1)
            nc.gpsimd.tensor_copy(mask16, wmask).then_inc(masks_ready, 1)

        @block.scalar
        def _(act):
            def exps(s):
                h, i = steps[s]
                src, n = span(s)
                act.wait_ge(maxed, s + 1)
                if s >= 2:
                    act.wait_ge(turned, s - 1)
                nc.scalar.activation(small(s, 3), core.col(SINK0 + h), ACT.Exp, bias=small(s, 1), scale=1.0)
                nc.scalar.activation(pr[s % 2][:, 0:(n + 2) * P], src, ACT.Exp, bias=small(s, 1), scale=HD ** -0.5,
                                     accum_out=small(s, 2)).then_inc(exped, 1)

            def copy(s):
                _, n = span(s)
                act.wait_ge(turned, s + 1)
                if s >= 2:
                    act.wait_ge(weighted, s - 1)
                nc.scalar.activation(pt[s % 2][:, 0:(n + 2) * P], flat[:, 2048:2048 + (n + 2) * P],
                                     ACT.Copy).then_inc(turned_copied, 1)
            exps(0)
            for s in range(N):
                if s + 1 < N:
                    exps(s + 1)
                copy(s)

        @block.vector
        def _(dve):
            chain = Chain(dve, chain_s)

            def top(s):
                h, i = steps[s]
                src, n = span(s)
                dve.wait_ge(scored, s + 1)
                if s >= 2:
                    dve.wait_ge(normalised, s - 1)
                chain(nc.vector.reduce_max(small(s, 0), src, AXX))
                chain.wait()
                nc.vector.tensor_scalar(small(s, 1), small(s, 0), -HD ** -0.5, core.col(SINK0 + 8 + h), ALU.mult,
                                        ALU.min).then_inc(maxed, 1)

            def normalise(s):
                _, n = span(s)
                dve.wait_ge(exped, s + 1)
                chain(nc.vector.tensor_tensor(small(s, 4), small(s, 2), small(s, 3), ALU.add))
                chain.wait()
                chain(nc.vector.reciprocal(small(s, 5), small(s, 4)))
                chain.wait()
                p = pr[s % 2][:, 0:(n + 2) * P]
                nc.vector.tensor_scalar(p, p, small(s, 5), None, ALU.mult).then_inc(normalised, 1)

            def out(s):
                h, i = steps[s]
                hh = slice((h % 2) * HD, (h % 2 + 1) * HD)
                dve.wait_ge(weighted, s + 1)
                nc.vector.tensor_copy(tiles[h // 2][hh, i * P:(i + 1) * P],
                                      core.ps[hh, 6 + s % 2, 0:P]).then_inc(out_done, 1)
            top(0)
            for s in range(N):
                normalise(s)
                if s + 1 < N:
                    top(s + 1)
                if s:
                    out(s - 1)
            out(N - 1)


def gla_stage(core, nc, name):
    NCH = T // CH
    orders = [list(range(NCH)), list(range(CTX // CH - 1, -1, -1)) + list(range(NCH - 1, CTX // CH - 1, -1))]
    b = lambda n: core.sb(T0 + n * T, T)
    F, KK, CU = b(0), b(1), b(2)
    QE, KE, QS, KDC = [b(3), b(4)], [b(5), b(6)], [b(7), b(8)], [b(9), b(10)]
    SCAN = b(11)
    o = TW0
    S = core.sb(o, NCH * P); o += NCH * P
    V = [core.sb(o, T), core.sb(o + T, T)]; o += 2 * T
    KDT = core.sb(o, T); o += T
    SM = [core.sb(o + d * T, T) for d in range(2)]; o += 2 * T
    TRI = [core.sb(o + d * P, P) for d in range(2)]; o += 2 * P
    DEC = [core.sb(o + d * 16, NCH) for d in range(2)]; o += 32
    VB = core.sb(T0 + 12 * T, 2 * T)
    assert o <= C0 and T0 + 14 * T <= TW0
    (tables_in, gates_done, v_turned, v_done, f_done, k_done, lf_done, cum_done, e_done, prod_done, scored, masked,
     kd_turned, kd_copied, states_in, states_done, outs_done, out_copied, vb_done, chain_s) = core.sems(20)
    runs = [(h, d) for h in range(4) for d in range(2)]
    flat = core.ps[:, :, :].rearrange("p b n -> p (b n)")
    ch3 = lambda ap: ap.rearrange("p (c t) -> p c t", t=CH)
    at_ref = [CH // 2, CH - 1 - CH // 2]
    at_end = [CH - 1, 0]

    with nc.Block() as block:
        @block.sync
        def _(sp):
            sp.dma_start(SCAN, core.const("scan")).then_inc(tables_in, 16)
            sp.dma_start(TRI[0], core.const("tri_fw")).then_inc(tables_in, 16)
            sp.dma_start(TRI[1], core.const("tri_bw")).then_inc(tables_in, 16)

        @block.scalar
        def _(act):
            nc.scalar.activation(core.sb(U0 + 10 * T, 8 * T), core.sb(U0 + 10 * T, 8 * T), ACT.Sigmoid).then_inc(gates_done, 1)
            nc.scalar.activation(core.sb(U0 + 6 * T, 4 * T), core.sb(U0 + 6 * T, 4 * T), ACT.Silu)
            nc.scalar.activation(core.sb(U0 + 22 * T, 4 * T), core.sb(U0 + 22 * T, 4 * T), ACT.Silu).then_inc(gates_done, 1)
            for r, (h, d) in enumerate(runs):
                act.wait_ge(f_done, r + 1)
                if r:
                    act.wait_ge(prod_done, 4 * r)
                nc.scalar.activation(KK, F, ACT.Identity, bias=core.col(ONE), scale=-1.0)
                nc.scalar.activation(F, F, ACT.Ln).then_inc(lf_done, 1)
                act.wait_ge(cum_done, r + 1)
                if r >= 2:
                    act.wait_ge(outs_done, 2 * (r - 1))
                nc.scalar.activation(DEC[d], ch3(CU)[:, :, at_end[d]], ACT.Exp)
                nc.scalar.activation(QS[r % 2], CU, ACT.Exp).then_inc(e_done, 1)
                act.wait_ge(cum_done, r + 1)
                act.wait_ge(k_done, 2 * r + 2)
                nc.scalar.activation(KE[r % 2], QE[r % 2], ACT.Exp, scale=-1.0).then_inc(e_done, 1)
                act.wait_ge(e_done, 4 * r + 2)
                nc.scalar.activation(QE[r % 2], QE[r % 2], ACT.Exp).then_inc(e_done, 1)
                nc.scalar.activation(KDC[r % 2], KDC[r % 2], ACT.Exp).then_inc(e_done, 1)

        @block.gpsimd
        def _(pool):
            for r, (h, d) in enumerate(runs):
                pool.wait_ge(cum_done, r + 1)
                if r >= 2:
                    pool.wait_ge(outs_done, 2 * (r - 1))
                cu = ch3(CU)
                ref = cu[:, :, at_ref[d]:at_ref[d] + 1].broadcast_to([P, NCH, CH])
                end = cu[:, :, at_end[d]:at_end[d] + 1].broadcast_to([P, NCH, CH])
                nc.gpsimd.tensor_tensor(ch3(QE[r % 2]), cu, ref, ALU.subtract).then_inc(k_done, 1)
                nc.gpsimd.tensor_tensor(ch3(KDC[r % 2]), end, cu, ALU.subtract).then_inc(k_done, 1)
                if d == 0:
                    pool.wait_ge(v_done, h + 1)
                    if h:
                        pool.wait_ge(states_in, 2 * h)
                    for e in range(2):
                        ins = nc.gpsimd.tensor_scalar(VB.rearrange("p (c e d) -> p c e d", e=2, d=P)[:, :, e],
                                                      V[h % 2].rearrange("p (c d) -> p c d", d=P),
                                                      core.col(BD0 + e * (P - 1)), None, ALU.mult)
                    ins.then_inc(vb_done, 1)

        @block.vector
        def _(dve):
            chain = Chain(dve, chain_s)
            chain(nc.vector.memset(SM[0], 0.0))
            chain(nc.vector.memset(SM[1], 0.0))
            dve.wait_ge(tables_in, 48)
            dve.wait_ge(gates_done, 1)
            rev = lambda ap: bass.AP(tensor=ap.tensor, offset=ap.offset + T - 1, ap=[ap.ap[0], [-1, T]])

            def gates(r):
                h, d = runs[r]
                if r:
                    dve.wait_ge(cum_done, r)
                nc.vector.tensor_scalar(F, core.u(10 + 4 * d + h), core.col(LBV0 + 4 + h), core.col(LBV0 + h),
                                        ALU.mult, ALU.add).then_inc(f_done, 1)

            def sums(r):
                h, d = runs[r]
                dve.wait_ge(lf_done, r + 1)
                if r:
                    dve.wait_ge(e_done, 4 * r)
                    dve.wait_ge(k_done, 2 * r)
                if d == 0:
                    nc.vector.tensor_tensor_scan(CU, SCAN, F, 0.0, ALU.mult, ALU.add).then_inc(cum_done, 1)
                else:
                    nc.vector.tensor_tensor_scan(rev(CU), SCAN, rev(F), 0.0, ALU.mult, ALU.add).then_inc(cum_done, 1)

            def products(r):
                h, d = runs[r]
                dve.wait_ge(gates_done, 2)
                q = core.u(6 + h)
                for n, (e, x, buf) in enumerate(((1, q, QS), (2, KK, KE), (3, q, QE), (4, KK, KDC))):
                    dve.wait_ge(e_done, 4 * r + e)
                    nc.vector.tensor_tensor(buf[r % 2], buf[r % 2], x, ALU.mult).then_inc(prod_done, 1)

            def values(h):
                dve.wait_ge(v_turned, h + 1)
                nc.vector.tensor_copy(V[h % 2], flat[:, 0:T]).then_inc(v_done, 1)

            def mask_scores(r):
                h, d = runs[r]
                dve.wait_ge(scored, r + 1)
                if r >= 2:
                    dve.wait_ge(outs_done, 2 * (r - 1))
                for e in range(2):
                    part = slice(e * CH, (e + 1) * CH)
                    mask = TRI[d][part, e * CH:(e + 1) * CH].bitcast(U32).rearrange("p (o t) -> p o t", o=1)
                    ins = nc.vector.copy_predicated(
                        SM[d][part].rearrange("p (c e t) -> p c e t", e=2, t=CH)[:, :, e], mask.broadcast_to([CH, 6, CH]),
                        core.ps[part, 0, 0:384].rearrange("p (c t) -> p c t", t=CH))
                ins.then_inc(masked, 1)

            def turned_keys(r):
                dve.wait_ge(kd_turned, r + 1)
                if r:
                    dve.wait_ge(states_in, r)
                nc.vector.tensor_copy(KDT, flat[:, 0:T]).then_inc(kd_copied, 1)

            def states(r):
                h, d = runs[r]
                dve.wait_ge(states_in, r + 1)
                if r:
                    dve.wait_ge(outs_done, 2 * r)
                order = orders[d]
                for n in range(1, NCH):
                    c = order[n - 1]
                    ds = flat[:, 1536 + c * P:1536 + (c + 1) * P]
                    if n == 1:
                        ins = nc.vector.tensor_copy(S[:, P:2 * P], ds)
                    else:
                        dve.wait_ge(states_done, r * (NCH - 1) + n - 1)
                        ins = nc.vector.scalar_tensor_tensor(out=S[:, n * P:(n + 1) * P], in0=S[:, (n - 1) * P:n * P],
                                                             scalar=DEC[d][:, c:c + 1], in1=ds, op0=ALU.mult,
                                                             op1=ALU.add)
                    ins.then_inc(states_done, 1)
                if d == 1:
                    dve.wait_ge(outs_done, 2 * r + 2)
                    nc.vector.tensor_copy(core.u(18 + h), flat[:, 3072:3072 + T]).then_inc(out_copied, 1)

            chain.wait()
            values(0)
            gates(0)
            sums(0)
            products(0)
            gates(1)
            for r in range(8):
                mask_scores(r)
                if r + 1 < 8:
                    sums(r + 1)
                turned_keys(r)
                if r + 1 < 8:
                    products(r + 1)
                if r + 2 < 8:
                    gates(r + 2)
                states(r)
                if r % 2 == 0 and r // 2 + 1 < 4:
                    values(r // 2 + 1)

        @block.tensor
        def _(pe):
            def values(h):
                if h:
                    pe.wait_ge(kd_copied, 2 * h - 1)
                for t in range(6):
                    mm = nc.tensor.transpose(flat[:, t * P:(t + 1) * P],
                                             core.u(18 + h)[:, t * P:(t + 1) * P], core.ident())
                mm.then_inc(v_turned, 1)

            values(0)
            for r, (h, d) in enumerate(runs):
                v = V[h % 2]
                pe.wait_ge(prod_done, 4 * r + 4)
                if r:
                    pe.wait_ge(kd_copied, r)
                pe.wait_ge(v_done, min(h + 1 + r % 2, 4))
                for c in range(NCH):
                    for e in range(2):
                        s0 = c * CH + e * CH // 2
                        a, w = ((CH // 2, CH // 2) if (d, e) == (0, 1) else (0, CH // 2) if (d, e) == (1, 0) else (0, CH))
                        t0 = c * CH + a
                        p0 = (c % 2) * CH + e * CH // 2
                        o0 = (c // 2) * CH + a
                        mm = nc.tensor.matmul(core.ps[p0:p0 + CH // 2, 0, o0:o0 + w], KE[r % 2][:, s0:s0 + CH // 2],
                                              QE[r % 2][:, t0:t0 + w], start=True, stop=True)
                mm.then_inc(scored, 1)
                pe.wait_ge(masked, r + 1)
                for t in range(6):
                    mm = nc.tensor.transpose(flat[:, t * P:(t + 1) * P], KDC[r % 2][:, t * P:(t + 1) * P],
                                             core.ident())
                mm.then_inc(kd_turned, 1)
                pe.wait_ge(kd_copied, r + 1)
                if r:
                    pe.wait_ge(states_done, r * (NCH - 1))
                pe.wait_ge(vb_done, h + 1)
                for c in range(6):
                    mm = nc.tensor.matmul(flat[:, 1536 + 2 * c * P:1536 + 2 * (c + 1) * P], KDT[:, c * P:(c + 1) * P],
                                          VB[:, 2 * c * P:2 * (c + 1) * P], start=True, stop=True)
                mm.then_inc(states_in, 1)
                if d == 0 and h:
                    pe.wait_ge(out_copied, h)
                for c in range(6):
                    cc = slice(c * P, (c + 1) * P)
                    mm = nc.tensor.matmul(flat[:, 3072 + c * P:3072 + (c + 1) * P], v[:, cc], SM[d][:, cc],
                                          start=(d == 0 and c in (0, 4)), stop=False, skip_group_check=True)
                mm.then_inc(outs_done, 1)
                for n in range(1, NCH):
                    c = orders[d][n]
                    pe.wait_ge(states_done, r * (NCH - 1) + n)
                    mm = nc.tensor.matmul(flat[:, 3072 + c * CH:3072 + (c + 1) * CH], S[:, n * P:(n + 1) * P],
                                          QS[r % 2][:, c * CH:(c + 1) * CH], start=False, stop=(d == 1),
                                          skip_group_check=True)
                mm.then_inc(outs_done, 1)
                if r % 2 == 0 and h + 1 < 4:
                    values(h + 1)


def even_mixer(core, nc, a, following):
    ctx_seg, lat_seg = (0, CTX), (CTX, SEQ)
    both = [lat_seg, ctx_seg]
    qk = [core.u(t) for t in range(5)]
    group_norm(core, nc, "qk", [[(qk[t], qk[t], PV0 + ROW_QKG + (t == 4), None)] for t in range(5)],
               core.sb(BD0, P), HD, both, EPS6)
    o = TW0
    cos, sin = core.sb(o, SEQ), core.sb(o + SEQ, SEQ); o += 2 * SEQ
    rot, dup0, dup1 = core.sb(o, P), core.sb(o + P, P), core.sb(o + 2 * P, P); o += 3 * P
    wmask = core.sb(o, 3 * P); o += 3 * P
    kdup = [core.sb(o, T), core.sb(o + T, T)]; o += 2 * T
    vtok = core.sb(o, T); o += T
    rope_stage(core, nc, qk, [(cos, "cosA"), (sin, "sinA"), (rot, "rot"), (dup0, "dup0"), (dup1, "dup1"),
                              (wmask, "wmask")], core.u(5), kdup, vtok, cos, sin, rot, [dup0, dup1])
    window_stage(core, nc, qk[:4], kdup, vtok, wmask)
    gla_stage(core, nc, "gla")
    group_norm(core, nc, "gla_norm", [[(core.u(18 + h), core.u(18 + h), PV0 + ROW_OG, core.u(22 + h))] for h in range(4)],
               core.sb(ONES0, P), P, both, EPS6, then=following)


def retention_stage(core, nc, h, out0):
    o = TW0
    V = core.sb(o, 6 * ODD_DV); o += 6 * ODD_DV
    ST = core.sb(o, 6 * SEQ); o += 6 * SEQ
    W = core.sb(o, 12 * P); o += 12 * P
    tmp = [core.sb(o + n * SEQ, SEQ) for n in range(4)]; o += 4 * SEQ
    cos, sin = core.sb(o, SEQ), core.sb(o + SEQ, SEQ); o += 2 * SEQ
    assert o <= C0
    tables_in, mults, mults_p, roped, v_turned, v_copied, scored, weighted, summed = core.sems(9)
    n_tables = 3
    with nc.Block() as block:
        @block.sync
        def _(sp):
            sp.dma_start(cos, core.const("cosR")).then_inc(tables_in, 16)
            sp.dma_start(sin, core.const("sinR")).then_inc(tables_in, 16)
            sp.dma_start(W, core.const(f"ret{h}")).then_inc(tables_in, 16)

        def rope(eng, x0, x1, t0, t1, done_sem):
            eng.wait_ge(tables_in, 16 * n_tables)
            eng.tensor_tensor(t0, x1, sin, ALU.mult).then_inc(done_sem, 1)
            eng.tensor_tensor(t1, x0, sin, ALU.mult).then_inc(done_sem, 1)
            eng.wait_ge(done_sem, 2)
            eng.tensor_tensor(x0, x0, cos, ALU.mult).then_inc(done_sem, 1)
            eng.tensor_tensor(x1, x1, cos, ALU.mult).then_inc(done_sem, 1)
            eng.wait_ge(done_sem, 4)
            eng.tensor_tensor(x0, x0, t0, ALU.subtract).then_inc(roped, 1)
            eng.tensor_tensor(x1, x1, t1, ALU.add).then_inc(roped, 1)

        @block.gpsimd
        def _(pool):
            rope(nc.gpsimd, core.u(0)[:, LAT], core.u(1)[:, LAT], tmp[0], tmp[1], mults_p)

        @block.vector
        def _(dve):
            rope(nc.vector, core.u(2)[:, LAT], core.u(3)[:, LAT], tmp[2], tmp[3], mults)
            for j in range(6):
                dve.wait_ge(scored, j + 1)
                w0 = 3 * P - (j - 2) * P if j >= 2 else 7 * P + P - j * P
                nc.vector.tensor_tensor(ST[:, j * SEQ:(j + 1) * SEQ], core.ps[:, 6 + j % 2, :], W[:, w0:w0 + SEQ],
                                        ALU.mult).then_inc(weighted, 1)
            for e in range(4):
                dve.wait_ge(summed, e + 1)
                nc.vector.tensor_copy(core.sb(out0 + e * SEQ, SEQ), core.ps[:, e, :])

        @block.tensor
        def _(pe):
            for t in range(6):
                for e in range(4):
                    mm = nc.tensor.transpose(core.ps[:, t, e * P:(e + 1) * P], core.u(4 + e)[:, t * P:(t + 1) * P],
                                             core.ident())
                mm.then_inc(v_turned, 1)
            pe.wait_ge(roped, 4)
            for j in range(6):
                if j >= 2:
                    pe.wait_ge(weighted, j - 1)
                for k in range(2):
                    mm = nc.tensor.matmul(core.ps[:, 6 + j % 2, :], core.u(2 + k)[:, j * P:(j + 1) * P],
                                          core.u(k)[:, LAT], start=(k == 0), stop=(k == 1))
                mm.then_inc(scored, 1)
            pe.wait_ge(v_copied, 6)
            for e in range(4):
                for j in range(6):
                    if e == 0:
                        pe.wait_ge(weighted, j + 1)
                    mm = nc.tensor.matmul(core.ps[:, e, :], V[:, j * ODD_DV + e * P:j * ODD_DV + (e + 1) * P],
                                          ST[:, j * SEQ:(j + 1) * SEQ], start=(j == 0), stop=(j == 5))
                mm.then_inc(summed, 1)

        @block.scalar
        def _(act):
            for t in range(6):
                act.wait_ge(v_turned, t + 1)
                nc.scalar.activation(V[:, t * ODD_DV:(t + 1) * ODD_DV], core.ps[:, t, :], ACT.Copy).then_inc(v_copied, 1)
            for e in range(4):
                nc.scalar.activation(core.u(8 + e)[:, LAT], core.u(8 + e)[:, LAT], ACT.Silu)


def odd_projections(core, nc, a, both, lat):
    K0, V0, G0 = ODD_H * ODD_DK, 2 * ODD_H * ODD_DK, 2 * ODD_H * ODD_DK + ODD_H * ODD_DV
    projections = []
    for h in range(ODD_H):
        kv = [K0 + h * ODD_DK, V0 + h * ODD_DV, V0 + h * ODD_DV + GW]
        qg = [h * ODD_DK, G0 + h * ODD_DV, G0 + h * ODD_DV + GW]
        tiles_kv, tiles_qg = [2, 4, 6], [0, 8, 10]
        place = lambda tiles: lambda g, f: U0 + (tiles[g] + f) * T
        projections.append((
            Dense(core, a["odd_w_in"][0], core.h, KD, 3, (lambda c: lambda ib, j: c[ib + j])(kv), both,
                  Copy(core, nc, U0, both, place(tiles_kv))),
            Dense(core, a["odd_w_in"][0], core.h, KD, 3, (lambda c: lambda ib, j: c[ib + j])(qg), lat,
                  Copy(core, nc, U0, lat, place(tiles_qg)))))
    return projections


def odd_mixer(core, nc, a, both, lat, projections, following):
    OUT0 = U0 + 12 * T
    view = lambda n: core.sb(OUT0 + n * SEQ - CTX, T)
    m = M0 + 96
    out = Dense(core, a["odd_w_out"][0], view, ODD_H * ODD_DV // P, 4, lambda ib, j: ib * GW + j * GW, lat,
                Residual(core, nc, m + 2 * 16, lat), split=True)
    for h in range(ODD_H):
        kv, qg = projections[h]
        kv.run(f"kv{h}", after=qg)
        qg.run(f"qg{h}")
        retention_stage(core, nc, h, OUT0 + 4 * h * SEQ)
        ov = [view(4 * h + e) for e in range(4)]
        group_norm(core, nc, f"ret_norm{h}", [[(ov[e], ov[e], ONE, core.u(8 + e)) for e in range(4)]],
                   core.sb(ONES0, P), ODD_DV, lat, EPS6, scratch=U0,
                   then=projections[h + 1][0] if h + 1 < ODD_H else out)
    out.run("odd_out", after=following)


def u2(core, t):
    return core.sb(U0 + t * SEQ, SEQ)


def lat_view(core, t):
    return core.sb(U0 + t * SEQ - CTX, T)


def taps(n):
    return [n // 2] + [t for t in range(n) if t != n // 2]


def conv_stage(core, nc, l):
    NB, n_sc = 6, 9
    PAD = CONV_K // 2
    pe_taps = 6
    o = S0
    diag = [core.sb(o + b * P, P) for b in range(NB)]; o += NB * P
    hb = [core.sb(o + q * 2 * SEQ, SEQ + 2 * PAD) for q in range(2)]; o += 4 * SEQ
    cv = [core.sb(o + q * SEQ, SEQ) for q in range(2)]; o += 2 * SEQ
    sq = [core.sb(o + q * SEQ, SEQ) for q in range(2)]; o += 2 * SEQ
    rstd = core.sb(o, SEQ)
    work = [("dw", q, t) for q in range(2) for t in range(pe_taps)] + [("sc", q, t) for q in range(n_sc) for t in taps(3)]
    (gated, glu, diag_made, tap_done, conv_done, silu_done, module_done, mean_done, centred, sq_done, var_done,
     std_done, normed, chain_s) = core.sems(14)
    with nc.Block() as block:
        @block.scalar
        def _(act):
            for q in range(2):
                nc.scalar.activation(u2(core, 2 + q), u2(core, 2 + q), ACT.Sigmoid).then_inc(gated, 1)
            for q in range(3):
                nc.scalar.activation(u2(core, 22 + q), u2(core, 22 + q), ACT.Silu)
            for q in range(n_sc):
                act.wait_ge(conv_done, 3 + q)
                nc.scalar.activation(u2(core, 13 + q), core.ps[:, 4 + q % 4, :], ACT.Silu).then_inc(silu_done, 1)
            for q in range(2):
                act.wait_ge(centred, q + 1)
                nc.scalar.activation(sq[q], cv[q], ACT.Square).then_inc(sq_done, 1)
            act.wait_ge(var_done, 1)
            nc.scalar.activation(rstd, core.ps[:, 3, :], ACT.Sqrt, bias=core.col(EPS5),
                                 scale=1.0 / CONV_CH).then_inc(std_done, 1)
            for q in range(2):
                act.wait_ge(normed, q + 1)
                nc.scalar.activation(u2(core, q), u2(core, q), ACT.Silu, bias=core.col(PV0 + ROW_LNB + 2 * l + q),
                                     scale=1.0)

        @block.gpsimd
        def _(pool):
            for n, (kind, q, t) in enumerate(work):
                if n >= NB:
                    pool.wait_ge(tap_done, n - NB + 1)
                c = PV0 + (ROW_DW + (l * CONV_K + t) * 2 + q if kind == "dw" else ROW_SC + (l * 3 + t) * 9 + q)
                nc.gpsimd.tensor_scalar(diag[n % NB], core.ident(), core.col(c), None, ALU.mult).then_inc(diag_made, 1)

        @block.tensor
        def _(pe):
            for n, (kind, q, t) in enumerate(work):
                if kind == "dw":
                    if t == 0:
                        pe.wait_ge(glu, q + 1)
                    out, src = core.ps[:, q, :], hb[q][:, t:t + SEQ]
                    first, last = t == 0, t == pe_taps - 1
                else:
                    if t == 1 and q >= 4:
                        pe.wait_ge(silu_done, q - 3)
                    off = t - 1
                    a, b = max(0, -off), SEQ - max(0, off)
                    out, src = core.ps[:, 4 + q % 4, a:b], u2(core, 13 + q)[:, a + off:b + off]
                    first, last = t == 1, t == 2
                pe.wait_ge(diag_made, n + 1)
                nc.tensor.matmul(out, diag[n % NB], src, start=first, stop=last,
                                 skip_group_check=True).then_inc(tap_done, 1)
                if last:
                    pe.wait_ge(tap_done, n + 1)
                    pe.sem_inc(conv_done, 1)
            for q in range(2):
                pe.wait_ge(module_done, q + 1)
                mm = nc.tensor.matmul(core.ps[:, 2, :], core.sb(ONES0, P), cv[q], start=(q == 0), stop=(q == 1))
            mm.then_inc(mean_done, 1)
            for q in range(2):
                pe.wait_ge(sq_done, q + 1)
                mm = nc.tensor.matmul(core.ps[:, 3, :], core.sb(ONES0, P), sq[q], start=(q == 0), stop=(q == 1))
            mm.then_inc(var_done, 1)

        @block.vector
        def _(dve):
            chain = Chain(dve, chain_s)
            for q in range(2):
                nc.vector.memset(hb[q][:, 0:PAD], 0.0)
                nc.vector.memset(hb[q][:, PAD + SEQ:], 0.0)
            for q in range(2):
                dve.wait_ge(gated, q + 1)
                nc.vector.tensor_tensor(hb[q][:, PAD:PAD + SEQ], u2(core, q), u2(core, 2 + q), ALU.mult).then_inc(glu, 1)
            dve.wait_ge(glu, 2)
            for t in range(pe_taps, CONV_K):
                for q in range(2):
                    w, src = core.col(PV0 + ROW_DW + (l * CONV_K + t) * 2 + q), hb[q][:, t:t + SEQ]
                    if t == pe_taps:
                        chain(nc.vector.tensor_scalar(cv[q], src, w, core.col(PV0 + ROW_DWB + 2 * l + q), ALU.mult,
                                                      ALU.add))
                    else:
                        chain.wait(chain.n - 1)
                        chain(nc.vector.scalar_tensor_tensor(out=cv[q], in0=src, scalar=w, in1=cv[q], op0=ALU.mult,
                                                             op1=ALU.add))
            for q in range(2):
                chain.wait()
                dve.wait_ge(conv_done, q + 1)
                nc.vector.tensor_tensor(cv[q], cv[q], core.ps[:, q, :], ALU.add).then_inc(module_done, 1)
            dve.wait_ge(mean_done, 1)
            for q in range(2):
                nc.vector.scalar_tensor_tensor(out=cv[q], in0=core.ps[:, 2, :], scalar=-1.0 / CONV_CH, in1=cv[q],
                                               op0=ALU.mult, op1=ALU.add).then_inc(centred, 1)
            dve.wait_ge(std_done, 1)
            chain(nc.vector.reciprocal(rstd, rstd))
            chain.wait()
            for q in range(2):
                nc.vector.scalar_tensor_tensor(out=u2(core, q), in0=cv[q], scalar=core.col(PV0 + ROW_LNW + 2 * l + q),
                                               in1=rstd, op0=ALU.mult, op1=ALU.mult).then_inc(normed, 1)


def diff_stage(core, nc, a, l):
    DD = 32
    scale = DD ** -0.5
    lam0 = 0.8 - 0.6 * math.exp(-0.3 * l)
    slopes = [2.0 ** -2, 2.0 ** -4, 2.0 ** -6, 2.0 ** -8, 2.0 ** -1, 2.0 ** -3]
    o = S0
    dist = core.sb(o, 7 * P); o += 7 * P
    dist16 = core.sb(o, 7 * P // 2).bitcast(F16); o += 7 * P // 2
    si = [core.sb(o + n * P // 2, P // 2).bitcast(F16) for n in range(2)]; o += P
    pr = [core.sb(o + n * 2 * SEQ, 2 * SEQ) for n in range(2)]; o += 4 * SEQ
    at = [core.sb(o + n * SEQ, SEQ) for n in range(2)]; o += 2 * SEQ
    both = [core.sb(o + n * SEQ, SEQ) for n in range(2)]; o += 2 * SEQ
    vt = core.sb(o, 4 * DIFF_W); o += 4 * DIFF_W
    lamv = core.sb(o, 4 * DD); o += 4 * DD
    lamp = core.sb(o, 2 * DD); o += 2 * DD
    sc = lambda s, c, w=2: core.sb(GX0 + (s % 2) * 8 + c, w)
    steps = [(h, i) for h in range(6) for i in range(4)]
    N = len(steps)
    (loads_in, lam_s, v_turned, v_copied, slope_made, q_scaled, scored, maxed, exped, subtracted, turned,
     turned_copied, weighted, out_done, chain_s) = core.sems(15)
    with nc.Block() as block:
        @block.sync
        def _(sp):
            sp.dma_start(dist, core.const("dist")).then_inc(loads_in, 16)
            for n, name in enumerate(("diff_lambda_q1_2", "diff_lambda_k1_2", "diff_lambda_q2_2", "diff_lambda_k2_2")):
                sp.dma_start(lamv[:, n * DD:(n + 1) * DD], a[name][l].partition_broadcast(P)).then_inc(loads_in, 16)

        @block.gpsimd
        def _(pool):
            for t in range(3):
                nc.gpsimd.tensor_scalar(u2(core, 4 + t), u2(core, 4 + t), scale, None, ALU.mult).then_inc(q_scaled, 1)
            pool.wait_ge(loads_in, 80)
            nc.gpsimd.tensor_copy(dist16, dist).then_inc(q_scaled, 1)
            for h in range(6):
                if h >= 2:
                    pool.wait_ge(scored, 4 * (h - 1))
                nc.gpsimd.tensor_scalar(si[h % 2], core.ident(), -slopes[h], None, ALU.mult).then_inc(slope_made, 1)

        @block.tensor
        def _(pe):
            for b in range(3):
                for q in range(4):
                    mm = nc.tensor.transpose(core.ps[:, 4 + b, q * P:(q + 1) * P],
                                             u2(core, 10 + b)[:, q * P:(q + 1) * P], core.ident())
            mm.then_inc(v_turned, 1)
            pe.wait_ge(q_scaled, 4)

            def scores(s):
                h, i = steps[s]
                if s >= 2:
                    pe.wait_ge(exped, 2 * (s - 1))
                pe.wait_ge(slope_made, h + 1)
                for m in range(2):
                    mp = 2 * h + m
                    pp = slice((mp % 4) * DD, (mp % 4 + 1) * DD)
                    bank = core.ps[:, (s % 2) * 2 + m, :]
                    nc.tensor.matmul(bank, si[h % 2], dist16[:, 3 * P - i * P:3 * P - i * P + SEQ], start=True, stop=False)
                    mm = nc.tensor.matmul(bank, u2(core, 4 + mp // 4)[pp, i * P:(i + 1) * P],
                                          u2(core, 7 + mp // 4)[pp, :], start=False, stop=True)
                mm.then_inc(scored, 1)

            def turn(s):
                pe.wait_ge(subtracted, s + 1)
                if s >= 2:
                    pe.wait_ge(turned_copied, s - 1)
                if s == 0:
                    pe.wait_ge(v_copied, 1)
                for j in range(4):
                    mm = nc.tensor.transpose(core.ps[:, 4 + s % 2, j * P:(j + 1) * P],
                                             both[s % 2][:, j * P:(j + 1) * P], core.ident())
                mm.then_inc(turned, 1)

            def weigh(s):
                h, i = steps[s]
                pe.wait_ge(turned_copied, s + 1)
                if s >= 2:
                    pe.wait_ge(out_done, s - 1)
                oo = core.ps[(h % 2) * HD:(h % 2 + 1) * HD, 6 + s % 2, 0:P]
                for j in range(4):
                    mm = nc.tensor.matmul(oo, vt[:, j * DIFF_W + h * HD:j * DIFF_W + (h + 1) * HD],
                                          at[s % 2][:, j * P:(j + 1) * P], start=(j == 0), stop=(j == 3))
                mm.then_inc(weighted, 1)
            scores(0)
            for s in range(N):
                if s + 1 < N:
                    scores(s + 1)
                if s:
                    weigh(s - 1)
                turn(s)
            weigh(N - 1)

        @block.scalar
        def _(act):
            act.wait_ge(lam_s, 1)
            nc.scalar.activation(core.sb(GX0 + 32, 2), core.sb(GX0 + 32, 2), ACT.Exp).then_inc(lam_s, 1)

            def exps(s):
                act.wait_ge(maxed, s + 1)
                if s >= 2:
                    act.wait_ge(subtracted, s - 1)
                for m in range(2):
                    nc.scalar.activation(pr[s % 2][:, m * SEQ:(m + 1) * SEQ], core.ps[:, (s % 2) * 2 + m, :], ACT.Exp,
                                         bias=sc(s, 2 + m, 1), scale=1.0, accum_out=sc(s, 4 + m, 1)).then_inc(exped, 1)

            def copy(s):
                act.wait_ge(turned, s + 1)
                if s >= 2:
                    act.wait_ge(weighted, s - 1)
                nc.scalar.activation(at[s % 2], core.ps[:, 4 + s % 2, :], ACT.Copy).then_inc(turned_copied, 1)
            exps(0)
            for s in range(N):
                if s + 1 < N:
                    exps(s + 1)
                copy(s)

        @block.vector
        def _(dve):
            chain = Chain(dve, chain_s)
            dve.wait_ge(v_turned, 1)
            for b in range(3):
                ins = nc.vector.tensor_copy(vt.rearrange("p (q c) -> p q c", c=DIFF_W)[:, :, b * P:(b + 1) * P],
                                            core.ps[:, 4 + b, :].rearrange("p (q c) -> p q c", c=P))
            ins.then_inc(v_copied, 1)
            dve.wait_ge(loads_in, 80)
            l4 = lamv.rearrange("p (n d) -> p n d", d=DD)
            for n in range(2):
                chain(nc.vector.tensor_tensor(lamp[:, n * DD:(n + 1) * DD], l4[:, 2 * n], l4[:, 2 * n + 1], ALU.mult))
            chain.wait()
            nc.vector.reduce_sum(core.sb(GX0 + 32, 2), lamp.rearrange("p (n d) -> p n d", d=DD), AXX).then_inc(lam_s, 1)
            dve.wait_ge(lam_s, 2)
            chain(nc.vector.tensor_tensor(core.col(NLAM), core.col(GX0 + 33), core.col(GX0 + 32), ALU.subtract))
            chain.wait()
            chain(nc.vector.tensor_scalar(core.col(NLAM), core.col(NLAM), -lam0, None, ALU.add))
            chain(nc.vector.tensor_scalar(core.col(SUBG), core.col(PV0 + ROW_SUB + l), 1.0 - lam0, None, ALU.mult))

            def top(s):
                dve.wait_ge(scored, s + 1)
                if s >= 2:
                    dve.wait_ge(subtracted, s - 1)
                chain(nc.vector.reduce_max(sc(s, 0), core.ps[:, (s % 2) * 2:(s % 2) * 2 + 2, :], AXX))
                chain.wait()
                nc.vector.tensor_scalar(sc(s, 2), sc(s, 0), -1.0, None, ALU.mult).then_inc(maxed, 1)

            def subtract(s):
                dve.wait_ge(exped, 2 * s + 2)
                chain(nc.vector.reciprocal(sc(s, 6), sc(s, 4)))
                chain.wait()
                chain(nc.vector.tensor_scalar(pr[s % 2][:, SEQ:], pr[s % 2][:, SEQ:], sc(s, 7, 1), core.col(NLAM),
                                              ALU.mult, ALU.mult))
                chain.wait()
                if s >= 2:
                    dve.wait_ge(turned, s - 1)
                nc.vector.scalar_tensor_tensor(out=both[s % 2], in0=pr[s % 2][:, 0:SEQ], scalar=sc(s, 6, 1),
                                               in1=pr[s % 2][:, SEQ:], op0=ALU.mult, op1=ALU.add
                                               ).then_inc(subtracted, 1)

            def out(s):
                h, i = steps[s]
                hh = slice((h % 2) * HD, (h % 2 + 1) * HD)
                dve.wait_ge(weighted, s + 1)
                nc.vector.tensor_copy(u2(core, 4 + h // 2)[hh, i * P:(i + 1) * P],
                                      core.ps[hh, 6 + s % 2, 0:P]).then_inc(out_done, 1)
            top(0)
            for s in range(N):
                subtract(s)
                if s + 1 < N:
                    top(s + 1)
                if s:
                    out(s - 1)
            out(N - 1)


class DeltaPlan:

    def __init__(self, core):
        o = S0

        def take(w):
            nonlocal o
            o += w
            return core.sb(o - w, w)
        self.kt, self.vt = take(4 * DELTA_W), take(4 * DELTA_W)
        self.cum = [take(P), take(P)]
        self.lev = [[take(P) for _ in range(7)] for _ in range(2)]
        self.beta, self.g, self.gsum, self.eg, self.ekd, self.gl, self.bge, self.z, self.r = [take(48) for _ in range(9)]
        self.dtb, self.al = take(12), take(12)
        self.run = []
        for _ in range(2):
            self.run.append({n: take(w) for n, w in (
                ("x", 512), ("u", 512), ("pt", 512), ("bm", 512), ("nw", 512), ("vn", 256), ("s", 256))})
            self.run[-1].update({n: [take(w), take(w)] for n, w in (
                ("a", 512), ("at", 512), ("qg", 512), ("rv", 256), ("rw", 256), ("kd", 256))})
        self.d = [take(512) for _ in range(2)]
        assert o <= C0


def delta_gates_stage(core, nc, a, l, pl):
    loads_in, turned, betas, zs, lns, gs, sums, chain_s, chain_a = core.sems(9)
    v4 = lambda ap: ap.rearrange("p (c n) -> p c n", n=12)
    with nc.Block() as block:
        @block.sync
        def _(sp):
            for d, n in enumerate(("fw", "bw")):
                sp.dma_start(pl.cum[d], core.const("cum_" + n)).then_inc(loads_in, 16)
                for lv in range(7):
                    sp.dma_start(pl.lev[d][lv], core.const(f"lev_{n}{lv}")).then_inc(loads_in, 16)
            sp.dma_start(pl.dtb, a["delta_dt_bias_2"][l].rearrange("a b -> (a b)").partition_broadcast(P)).then_inc(loads_in, 16)
            sp.dma_start(pl.al, a["delta_A_log_2"][l].rearrange("a b -> (a b)").partition_broadcast(P)).then_inc(loads_in, 16)

        @block.tensor
        def _(pe):
            for c in range(4):
                mm = nc.tensor.transpose(core.ps[:, 6, c * 24:(c + 1) * 24], u2(core, DT)[0:24, c * P:(c + 1) * P],
                                         core.sb(IDENT0, 24, 24))
            mm.then_inc(turned, 1)
            for b in range(6):
                for c in range(4):
                    mm = nc.tensor.transpose(core.ps[:, b, c * P:(c + 1) * P], u2(core, 16 + b)[:, c * P:(c + 1) * P],
                                             core.ident())
                mm.then_inc(turned, 1)
            pe.wait_ge(gs, 1)
            pe.wait_ge(loads_in, 16 * 18)
            for d in range(2):
                nc.tensor.matmul(core.ps[:, 7, d * 24:(d + 1) * 24].rearrange("p (c n) -> p c n", n=6), pl.cum[d],
                                 v4(pl.g)[:, :, d * 6:(d + 1) * 6], start=(d == 0), stop=False, skip_group_check=True)
            nc.tensor.matmul(core.ps[:, 7, 48:96], core.sb(ONES0, P), pl.g, start=False, stop=True,
                             skip_group_check=True).then_inc(sums, 1)

        @block.vector
        def _(dve):
            chain = Chain(dve, chain_s)
            dve.wait_ge(loads_in, 16 * 18)
            dve.wait_ge(chain_a, 1)
            gate = core.ps[:, 6, 0:96].rearrange("p (c n) -> p c n", n=24)
            dtb = pl.dtb.rearrange("p (o n) -> p o n", o=1).broadcast_to([P, 4, 12])
            al = pl.al.rearrange("p (o n) -> p o n", o=1).broadcast_to([P, 4, 12])
            chain(nc.vector.tensor_tensor(v4(pl.z), gate[:, :, 12:24], dtb, ALU.add))
            chain.wait()
            chain(nc.vector.tensor_scalar(pl.r, pl.z, 0.0, None, ALU.max))
            chain.wait()
            nc.vector.scalar_tensor_tensor(out=pl.z, in0=pl.r, scalar=-2.0, in1=pl.z, op0=ALU.mult,
                                           op1=ALU.add).then_inc(zs, 1)
            dve.wait_ge(lns, 1)
            chain(nc.vector.tensor_tensor(pl.r, pl.r, pl.z, ALU.add))
            chain.wait()
            nc.vector.scalar_tensor_tensor(out=v4(pl.g), in0=v4(pl.r), scalar=-1.0, in1=al, op0=ALU.mult,
                                           op1=ALU.mult).then_inc(gs, 1)
            for b in range(6):
                dst = (pl.kt if b < 3 else pl.vt).rearrange("p (c n) -> p c n", n=DELTA_W)
                dve.wait_ge(turned, b + 2)
                nc.vector.tensor_copy(dst[:, :, (b % 3) * P:(b % 3 + 1) * P],
                                      core.ps[:, b, :].rearrange("p (c n) -> p c n", n=P))
            dve.wait_ge(sums, 1)
            for d in range(2):
                chain(nc.vector.tensor_copy(v4(pl.gsum)[:, :, d * 6:(d + 1) * 6],
                                            core.ps[:, 7, d * 24:(d + 1) * 24].rearrange("p (c n) -> p c n", n=6)))
            chain.wait()
            nc.vector.tensor_tensor(pl.ekd, core.ps[:, 7, 48:96], pl.gsum, ALU.subtract).then_inc(sums, 1)
            dve.wait_ge(chain_a, 2)
            nc.vector.tensor_tensor(pl.bge, pl.beta, pl.eg, ALU.mult)

        @block.scalar
        def _(act):
            act.wait_ge(turned, 1)
            nc.scalar.activation(v4(pl.beta), core.ps[:, 6, 0:96].rearrange("p (c n) -> p c n", n=24)[:, :, 0:12],
                                 ACT.Sigmoid).then_inc(chain_a, 1)
            act.wait_ge(loads_in, 16 * 18)
            act.wait_ge(zs, 1)
            nc.scalar.activation(pl.al, pl.al, ACT.Exp).then_inc(betas, 1)
            nc.scalar.activation(pl.z, pl.z, ACT.Exp).then_inc(betas, 1)
            act.wait_ge(betas, 2)
            nc.scalar.activation(pl.z, pl.z, ACT.Ln, bias=core.col(ONE), scale=1.0).then_inc(lns, 1)
            act.wait_ge(sums, 2)
            nc.scalar.activation(pl.eg, pl.gsum, ACT.Exp).then_inc(chain_a, 1)
            nc.scalar.activation(pl.ekd, pl.ekd, ACT.Exp)
            nc.scalar.activation(pl.gl, core.ps[:, 7, 48:96], ACT.Exp)


def delta_stage(core, nc, pl):
    LV = 7
    (prep_in, row_read, diff_done, d_done, qg_done, exps_in, xinit, a_done, at_done, ops_done, bm_done, x_ready,
     pt_done, pt_copied, xu_done, u_done, u_turned, x_done, w_turned, nw_done, vn_sum, vn_copied, ds_done, s_done,
     o_done, o_copied) = core.sems(26)
    c4 = lambda ap: ap.rearrange("p (c n) -> p c n", c=4)
    bc = lambda ap, w: ap.rearrange("p (c o) -> p c o", o=1).broadcast_to([P, 4, w])
    mat = lambda ap: ap.rearrange("p (o n) -> p o n", o=1).broadcast_to([P, 4, P])
    cols = lambda t, h, d: t.rearrange("p (c n) -> p c n", n=12)[:, :, d * 6 + h]
    bank = lambda d, n: core.ps[:, 3 * d + n, :]
    cc = lambda c: slice(c * P, (c + 1) * P)

    def half(h):
        return slice((h % 2) * HD, (h % 2 + 1) * HD)

    def order(d):
        return range(4) if d == 0 else range(3, -1, -1)

    with nc.Block() as block:
        @block.tensor
        def _(pe):
            def prepare(h, step):
                hh = half(h)
                q, k = u2(core, 13 + h // 2), u2(core, 16 + h // 2)
                b = core.ps[:, 6 + h % 2, :]
                if step == 0:
                    if h >= 2:
                        pe.wait_ge(o_copied, h - 1)
                elif step < 3:
                    pe.wait_ge(diff_done, 2 * h + step)
                else:
                    pe.wait_ge(a_done, 2 * h + 2)
                for c in range(4):
                    if step < 2:
                        g = cols(pl.g, h, step)[:, c:c + 1].broadcast_to([P, P])
                        mm = nc.tensor.matmul(b[:, cc(c)], g, pl.cum[step], start=True, stop=True)
                    else:
                        mm = nc.tensor.matmul(b[:, cc(c)], k[hh, cc(c)], (k if step == 2 else q)[hh, cc(c)], start=True,
                                              stop=True)
                mm.then_inc(prep_in, 1)

            for step in range(4):
                prepare(0, step)
            for h in range(6):
                hh = half(h)
                if h:
                    pe.wait_ge(s_done, 8 * h)
                for lv in range(LV):
                    for d in range(2):
                        R = pl.run[d]
                        nn = 2 * (h * LV + lv) + d
                        pe.wait_ge(bm_done, nn + 1)
                        if lv > 0:
                            pe.wait_ge(u_done, nn - 1)
                        if lv > 1:
                            for c in range(4):
                                mm = nc.tensor.transpose(bank(d, 1)[:, cc(c)], R["u"][:, cc(c)], core.ident())
                            mm.then_inc(u_turned, 1)
                        for c in range(4):
                            rhs = core.ident() if lv == 0 else R["u"][:, cc(c)]
                            mm = nc.tensor.matmul(bank(d, 0)[:, cc(c)], R["bm"][:, cc(c)], rhs, start=True, stop=True)
                        mm.then_inc(pt_done, 1)
                    if lv == 0:
                        continue
                    for d in range(2):
                        r, R = 2 * h + d, pl.run[d]
                        nn = 2 * (h * (LV - 1) + lv - 1) + d
                        pe.wait_ge(pt_copied, nn + 1)
                        if lv == 1:
                            pe.wait_ge(x_ready, r + 1)
                        else:
                            pe.wait_ge(x_done, 2 * (h * (LV - 2) + lv - 2) + d + 1)
                        for c in range(4):
                            mm = nc.tensor.matmul(bank(d, 2)[:, cc(c)], R["x"][:, cc(c)], R["pt"][:, cc(c)],
                                                  start=True, stop=True)
                        mm.then_inc(xu_done, 1)
                    if h < 5 and lv in (1, 2, 3, 5):
                        prepare(h + 1, (1, 2, 3, 5).index(lv))
                for d in range(2):
                    r, R = 2 * h + d, pl.run[d]
                    pe.wait_ge(u_done, 2 * (h * LV + LV - 1) + d + 1)
                    pe.wait_ge(ops_done, r + 1)
                    for c in range(4):
                        mm = nc.tensor.matmul(bank(d, 0)[hh, cc(c)], R["rw"][h % 2][:, c * HD:(c + 1) * HD], R["u"][:, cc(c)],
                                              start=True, stop=True)
                    mm.then_inc(w_turned, 1)
                pe.wait_ge(at_done, 2 * h + 2)
                pe.wait_ge(qg_done, 2 * h + 2)
                ob = core.ps[:, 6 + h % 2, :]
                for n in range(4):
                    for d in range(2):
                        r, R = 2 * h + d, pl.run[d]
                        c = order(d)[n]
                        m = 8 * h + 2 * n + d
                        v = bank(d, 1)[:, (n % 2) * HD:(n % 2 + 1) * HD]
                        if n:
                            pe.wait_ge(nw_done, r + 1)
                            pe.wait_ge(s_done, m - 1)
                        mm = nc.tensor.matmul(v, R["u"][:, cc(c)], R["rv"][h % 2][:, c * HD:(c + 1) * HD], start=True,
                                              stop=(n == 0))
                        if n:
                            mm = nc.tensor.matmul(v, R["nw"][hh, cc(c)], R["s"][hh, (n - 1) * HD:n * HD], start=False,
                                                  stop=True)
                        mm.then_inc(vn_sum, 1)
                    for d in range(2):
                        r, R = 2 * h + d, pl.run[d]
                        c = order(d)[n]
                        m = 8 * h + 2 * n + d
                        pe.wait_ge(vn_copied, m + 1)
                        vn = R["vn"][:, n * HD:(n + 1) * HD]
                        nc.tensor.matmul(bank(d, 2)[hh, (n % 2) * HD:(n % 2 + 1) * HD], R["kd"][h % 2][:, c * HD:(c + 1) * HD], vn,
                                         start=True, stop=True).then_inc(ds_done, 1)
                        mm = nc.tensor.matmul(ob[hh, cc(c)], vn, R["at"][h % 2][:, cc(c)], start=(n == 0 and d == 0),
                                              stop=False, skip_group_check=True)
                        if n:
                            mm = nc.tensor.matmul(ob[hh, cc(c)], R["s"][hh, (n - 1) * HD:n * HD], R["qg"][h % 2][hh, cc(c)],
                                                  start=False, stop=(n == 3), skip_group_check=True)
                mm.then_inc(o_done, 1)

        @block.scalar
        def _(act):
            def row_exp(h, d):
                act.wait_ge(prep_in, 4 * h + d + 1)
                nc.scalar.activation(pl.run[d]["qg"][h % 2][half(h)], core.ps[half(h), 6 + h % 2, :],
                                     ACT.Exp).then_inc(row_read, 1)

            def decays(h, d):
                a, at = pl.run[d]["a"][h % 2], pl.run[d]["at"][h % 2]
                act.wait_ge(d_done, 2 * h + d + 1)
                nc.scalar.activation(a, a, ACT.Exp, scale=-1.0).then_inc(exps_in, 1)
                nc.scalar.activation(at, at, ACT.Exp).then_inc(exps_in, 1)

            def prepare(h, step):
                if step < 2:
                    row_exp(h, step)
                if step > 0:
                    decays(h, step - 1)

            for step in range(3):
                prepare(0, step)
            for h in range(6):
                hh = half(h)
                for lv in range(1, LV):
                    for d in range(2):
                        R = pl.run[d]
                        if lv > 1:
                            act.wait_ge(u_turned, 2 * (h * (LV - 2) + lv - 2) + d + 1)
                            nc.scalar.activation(R["x"], bank(d, 1), ACT.Copy).then_inc(x_done, 1)
                        act.wait_ge(pt_done, 2 * (h * LV + lv) + d + 1)
                        nc.scalar.activation(R["pt"], bank(d, 0), ACT.Copy).then_inc(pt_copied, 1)
                    if h < 5 and lv in (1, 2, 3):
                        prepare(h + 1, lv - 1)
                for d in range(2):
                    r, R = 2 * h + d, pl.run[d]
                    act.wait_ge(w_turned, r + 1)
                    nc.scalar.activation(R["nw"][hh], bank(d, 0)[hh], ACT.Copy, scale=-1.0).then_inc(nw_done, 1)
                act.wait_ge(o_done, h + 1)
                nc.scalar.activation(u2(core, 19 + h // 2)[hh], core.ps[hh, 6 + h % 2, :], ACT.Copy).then_inc(o_copied, 1)

        @block.gpsimd
        def _(pool):
            def prepare(h, step):
                d = step % 2
                r, R = 2 * h + d, pl.run[d]
                if step < 2:
                    a, at = R["a"][h % 2], R["at"][h % 2]
                    pool.wait_ge(exps_in, 2 * r + 1)
                    nc.gpsimd.tensor_tensor(c4(a), c4(a), bc(cols(pl.beta, h, d), P), ALU.mult).then_inc(xinit, 1)
                    pool.wait_ge(exps_in, 2 * r + 2)
                    nc.gpsimd.tensor_tensor(c4(at), c4(at), mat(pl.cum[d]), ALU.mult).then_inc(xinit, 1)
                else:
                    kt = c4(pl.kt)[:, :, h * HD:(h + 1) * HD]
                    vt = c4(pl.vt)[:, :, h * HD:(h + 1) * HD]
                    nc.gpsimd.tensor_tensor(c4(R["rv"][h % 2]), vt, bc(cols(pl.beta, h, d), HD), ALU.mult)
                    nc.gpsimd.tensor_tensor(c4(R["rw"][h % 2]), kt, bc(cols(pl.bge, h, d), HD), ALU.mult)
                    nc.gpsimd.tensor_tensor(c4(R["kd"][h % 2]), kt, bc(cols(pl.ekd, h, d), HD),
                                            ALU.mult).then_inc(ops_done, 1)

            for step in range(4):
                prepare(0, step)
            for h in range(6):
                for lv in range(LV):
                    for d in range(2):
                        r, R = 2 * h + d, pl.run[d]
                        nn = 2 * (h * LV + lv) + d
                        if lv == 0:
                            pool.wait_ge(a_done, r + 1)
                        if h or lv:
                            pool.wait_ge(pt_done, nn - 1)
                        if lv == 1:
                            pool.wait_ge(x_ready, r + 1)
                        nc.gpsimd.tensor_tensor(c4(R["bm"]), c4(R["a"][h % 2]), mat(pl.lev[d][lv]),
                                                ALU.mult).then_inc(bm_done, 1)
                        if lv == 0:
                            pool.wait_ge(bm_done, nn + 1)
                            if h:
                                pool.wait_ge(xu_done, 2 * h * (LV - 1) - 1 + d)
                            nc.gpsimd.tensor_tensor(c4(R["x"]), mat(core.ident()), c4(R["bm"]),
                                                    ALU.subtract).then_inc(x_ready, 1)
                    if h < 5 and lv >= 3:
                        prepare(h + 1, lv - 3)

        @block.vector
        def _(dve):
            def differences(h, d):
                hh, r, R = half(h), 2 * h + d, pl.run[d]
                dve.wait_ge(row_read, r + 1)
                nc.vector.tensor_tensor(c4(pl.d[d]), c4(core.ps[:, 6 + h % 2, :]), bc(cols(pl.gsum, h, d), P),
                                        ALU.subtract).then_inc(diff_done, 1)
                dve.wait_ge(diff_done, r + 1)
                nc.vector.tensor_scalar(R["a"][h % 2], pl.d[d], 0.0, None, ALU.max)
                nc.vector.tensor_scalar(R["at"][h % 2], pl.d[d], 0.0, None, ALU.min).then_inc(d_done, 1)
                nc.vector.tensor_tensor(R["qg"][h % 2][hh], R["qg"][h % 2][hh], u2(core, 13 + h // 2)[hh],
                                        ALU.mult).then_inc(qg_done, 1)

            def times_gram(h, name, gram, done):
                for d in range(2):
                    o = pl.run[d][name][h % 2]
                    dve.wait_ge(xinit, 2 * (2 * h + d) + gram + 1)
                    dve.wait_ge(prep_in, 4 * h + 3 + gram)
                    nc.vector.tensor_tensor(o, o, core.ps[:, 6 + h % 2, :], ALU.mult).then_inc(done, 1)

            def prepare(h, step):
                if step < 2:
                    differences(h, step)
                elif step == 2:
                    times_gram(h, "a", 0, a_done)
                else:
                    times_gram(h, "at", 1, at_done)

            for step in range(4):
                prepare(0, step)
            for h in range(6):
                hh = half(h)
                for lv in range(LV):
                    for d in range(2):
                        r, R = 2 * h + d, pl.run[d]
                        nn = 2 * (h * LV + lv) + d
                        if lv == 0:
                            dve.wait_ge(pt_done, nn + 1)
                            nc.vector.tensor_tensor(c4(R["u"]), mat(core.ident()), c4(bank(d, 0)),
                                                    ALU.subtract).then_inc(u_done, 1)
                            continue
                        dve.wait_ge(xu_done, 2 * (h * (LV - 1) + lv - 1) + d + 1)
                        nc.vector.tensor_tensor(R["u"], R["u"], bank(d, 2), ALU.subtract).then_inc(u_done, 1)
                    if h < 5 and lv in (1, 2, 4, 5):
                        prepare(h + 1, (1, 2, 4, 5).index(lv))
                for n in range(4):
                    for d in range(2):
                        r, R = 2 * h + d, pl.run[d]
                        m = 8 * h + 2 * n + d
                        dve.wait_ge(vn_sum, m + 1)
                        nc.vector.tensor_copy(R["vn"][:, n * HD:(n + 1) * HD],
                                              bank(d, 1)[:, (n % 2) * HD:(n % 2 + 1) * HD]).then_inc(vn_copied, 1)
                    for d in range(2):
                        r, R = 2 * h + d, pl.run[d]
                        c = order(d)[n]
                        m = 8 * h + 2 * n + d
                        dve.wait_ge(ds_done, m + 1)
                        ds = bank(d, 2)[hh, (n % 2) * HD:(n % 2 + 1) * HD]
                        if n == 0:
                            nc.vector.tensor_copy(R["s"][hh, 0:HD], ds).then_inc(s_done, 1)
                        else:
                            dve.wait_ge(s_done, m - 1)
                            gl = cols(pl.gl, h, d)[hh, c:c + 1]
                            nc.vector.scalar_tensor_tensor(out=R["s"][hh, n * HD:(n + 1) * HD],
                                                           in0=R["s"][hh, (n - 1) * HD:n * HD], scalar=gl, in1=ds,
                                                           op0=ALU.mult, op1=ALU.add).then_inc(s_done, 1)


def second_in(core, nc, a, l, lat, plain):
    return Dense(core, a["w_in_2"][l], core.h, KD, 13, plain(0), lat,
                 Copy(core, nc, U0, lat, lambda g, f: U0 - CTX + g * 2 * SEQ + f * SEQ), widths={12: IN2 - 12 * GW})


def second_layer(core, nc, a, l, lat, plain, into, following):
    view = lambda t: lat_view(core, t)
    y_view = lambda k: core.sb(Y0 - CTX + k * SEQ, T)
    y_at = lambda g, f: Y0 - CTX + g * 2 * SEQ + f * SEQ
    cat = (0, 1, 4, 5, 6, 19, 20, 21)
    norm_stage(core, nc, lat, PV0 + ROW_PREMIX + 8 * l, then=into)
    into.run(f"in2_{l}")
    conv_stage(core, nc, l)
    group_norm(core, nc, "l2", [[(view(13 + t), view(13 + t), EIGHTH if t < 3 else ONE, None)] for t in range(6)],
               core.sb(BD0, P), 1.0, lat, EPS6)
    pl = DeltaPlan(core)
    delta_gates_stage(core, nc, a, l, pl)
    delta_stage(core, nc, pl)
    diff_stage(core, nc, a, l)
    group_norm(core, nc, "sub", [[(view(4 + t), view(4 + t), SUBG, None)] for t in range(3)],
               core.sb(BD0, P), HD, lat, EPS5)
    out = Dense(core, a["w_out_2"][l], lambda k: view(cat[k]), KD, 4, plain(0), lat,
                Copy(core, nc, 0, lat, y_at), split=True)
    group_norm(core, nc, "dn", [[(view(19 + t), view(19 + t), PV0 + ROW_DN + l, view(22 + t))] for t in range(3)],
               core.sb(BD0, P), HD, lat, EPS6, then=out)
    up = Dense(core, a["w_ff1_2"][l], core.h, KD, D_FF // GW, plain(0), lat, SquaredRelu(core, nc, U0, lat))
    out.run(f"out2_{l}", after=up)
    down = Dense(core, a["w_ff2_2"][l], view, D_FF // P, 4, plain(0), lat,
                 Copy(core, nc, 0, lat, y_at), split=True)
    norm_stage(core, nc, lat, PV0 + ROW_POSTMIX + 8 * l, src=y_view, residual=True)
    norm_stage(core, nc, lat, PV0 + ROW_PREMLP + 8 * l, then=up)
    up.run(f"ff1_{l}", after=down)
    down.run(f"ff2_{l}", after=following)
    norm_stage(core, nc, lat, PV0 + ROW_POSTMLP + 8 * l, src=y_view, residual=True)


def build(nc, a, y):
    table, at = constants()
    core = Core(nc, table, at)

    ctx_seg, lat_seg = (0, CTX), (CTX, SEQ)
    both, lat = [lat_seg, ctx_seg], [lat_seg]

    def plain(start):
        return lambda ib, j: start + ib * GW + j * GW

    def gate_up(ib, j):
        return HID * (j % 2) + ib * (GW // 2) + (j // 2) * GW

    def ffn_in(l, segs):
        return Dense(core, a["ffn_w_in"][l], core.h, KD, 2 * HID // GW, gate_up, segs, Swiglu(core, nc, U0, segs))

    def ffn1(l, segs, up, following):
        m = M0 + 96 * l
        down = Dense(core, a["ffn_w_out"][l], core.u, HID // P, 4, plain(0), segs,
                     Residual(core, nc, m + 5 * 16, segs), split=True)
        norm_stage(core, nc, segs, PV0 + ROW_NG + l * 16 + 8, shift=m + 3 * 16, scale=m + 4 * 16, then=up)
        up.run(f"up{l}", after=down)
        down.run(f"down{l}", after=following)

    def mixer_norm(l, projection):
        m = M0 + 96 * l
        norm_stage(core, nc, both, PV0 + ROW_NG + l * 16, shift=m, scale=m + 16, then=projection)

    params_stage(core, nc, a, a["x"][0], a["ctx"][0])
    modulation_stage(core, nc, a["mod_w"])
    even_in = Dense(core, a["even_w_in"][0], core.h, KD, EVEN_IN // GW, plain(0), both, Copy(core, nc, U0, both))
    mixer_norm(0, even_in)
    even_in.run("even_in")
    cat = (0, 1, 2, 3, 18, 19, 20, 21)
    even_out = Dense(core, a["even_w_out"][0], lambda k: core.u(cat[k]), KD, 4, plain(0), both,
                     Residual(core, nc, M0 + 2 * 16, both), split=True)
    even_mixer(core, nc, a, even_out)
    up = ffn_in(0, both)
    even_out.run("even_out", after=up)
    projections = odd_projections(core, nc, a, both, lat)
    ffn1(0, both, up, projections[0][0])
    mixer_norm(1, projections[0][0])
    up = ffn_in(1, lat)
    odd_mixer(core, nc, a, both, lat, projections, up)
    into = [second_in(core, nc, a, l, lat, plain) for l in range(2)]
    ffn1(1, lat, up, into[0])
    for l in range(2):
        second_layer(core, nc, a, l, lat, plain, into[l], into[1] if l == 0 else None)
    store_stage(core, nc, y)


_INS = ["x", "c", "ctx", "c_ctx", "mod_w", "mod_b", "norm_g", "ffn_w_in", "ffn_w_out", "even_w_in",
        "even_w_out", "attn_qk_norm_g", "attn_sink", "hgrn_out_norm_g", "hgrn_lb", "odd_w_in", "odd_w_out",
        "w_in_2", "w_out_2", "pre_mix_w_2", "post_mix_w_2", "pre_mlp_w_2", "post_mlp_w_2", "w_ff1_2", "w_ff2_2",
        "conv_dw_w_2", "conv_dw_b_2", "conv_ln_w_2", "conv_ln_b_2", "diff_lambda_q1_2", "diff_lambda_k1_2",
        "diff_lambda_q2_2", "diff_lambda_k2_2", "diff_subln_w_2", "delta_conv_w_2", "delta_A_log_2",
        "delta_dt_bias_2", "delta_norm_w_2"]
_OUT = (1, SEQ, D)


def kernel(**inputs):
    import numpy as _np
    import concourse.bacc as _bacc
    from concourse import mybir as _mybir
    from concourse.bass_utils import run_bass_kernel_spmd as _run

    nc = _bacc.Bacc("TRN2", target_bir_lowering=False, num_devices=1)
    arrays, args = {}, {}
    for name in _INS:
        a = _np.ascontiguousarray(inputs[name])
        arrays[f"in_{name}"] = a
        args[name] = nc.dram_tensor(f"in_{name}", a.shape, _mybir.dt.from_np(a.dtype), kind="ExternalInput").ap()
    out = nc.dram_tensor("out_0", _OUT, _mybir.dt.float32, kind="ExternalOutput").ap()
    build(nc, args, out[0])
    r = _run(nc, [arrays], core_ids=[0])
    return r.results[0]["out_0"]
```
